# Optimizing a Trainium2 kernel written in Bass

```python
import jax
import jax.numpy as jnp
from jax import lax
import numpy as np
import math
import jax, jax.numpy as jnp

D_MODEL = 1024
BATCH = 1
SEQ = 512
DEPTH = 2

MEM_LEN = 256
MIX_WIDTH = D_MODEL
A_WIDTH = MIX_WIDTH // 2
HGRN_HEAD_DIM = 128
HGRN_HEADS = A_WIDTH // HGRN_HEAD_DIM
HGRN_CHUNK = 64
B_WIDTH = MIX_WIDTH - A_WIDTH
CONV_WIDTH = 31
C_WIDTH = MIX_WIDTH // 2
MOBA_HEAD_DIM = 64
MOBA_HEADS = C_WIDTH // MOBA_HEAD_DIM
MOBA_BLOCK = 256
MOBA_TOPK = 3
MOBA_QCHUNK = 64
D_WIDTH = MIX_WIDTH - C_WIDTH
SGU_CHUNK = 128
SGU_GROUPS = 4
SGU_GROUP_DIM = D_WIDTH // SGU_GROUPS
XA_HEADS = 4
XA_HEAD_DIM = D_MODEL // XA_HEADS
FFN_HIDDEN = ((-(-8 * D_MODEL // 3) + 255) // 256) * 256
EVEN_IN = 4 * A_WIDTH + 2 * B_WIDTH
ODD_IN = 3 * C_WIDTH + 2 * D_WIDTH
N_EVEN = (DEPTH + 1) // 2
N_ODD = DEPTH // 2
EPS = 1e-6


def _rmsnorm(x, g):
    xf = x.astype(jnp.float32)
    y = xf * lax.rsqrt(jnp.mean(xf * xf, axis=-1, keepdims=True) + EPS)
    return (y * g.astype(jnp.float32)).astype(x.dtype)

def _layernorm(x, g, b):
    xf = x.astype(jnp.float32)
    mu = jnp.mean(xf, axis=-1, keepdims=True)
    var = jnp.mean(jnp.square(xf - mu), axis=-1, keepdims=True)
    y = (xf - mu) * lax.rsqrt(var + EPS) * g.astype(jnp.float32) + b.astype(jnp.float32)
    return y.astype(x.dtype)

def _hgrn2_chunkwise(q, f, v):
    bsz, seq, _ = q.shape
    n_chunks = seq // HGRN_CHUNK

    def heads(t):
        t = t.astype(jnp.float32).reshape(bsz, n_chunks, HGRN_CHUNK, HGRN_HEADS, HGRN_HEAD_DIM)
        return t.transpose(1, 0, 3, 2, 4)

    qf, ff, vf = heads(q), heads(f), heads(v)
    cum = jnp.cumsum(jnp.log(ff), axis=3)
    kf = 1.0 - ff
    q_in = qf * jnp.exp(cum)
    k_in = kf * jnp.exp(-cum)
    causal = jnp.tril(jnp.ones((HGRN_CHUNK, HGRN_CHUNK), dtype=bool))
    att = jnp.where(causal, jnp.einsum('nbhcd,nbhsd->nbhcs', q_in, k_in), 0.0)
    o_intra = jnp.einsum('nbhcs,nbhse->nbhce', att, vf)
    cum_last = cum[..., -1:, :]
    chunk_kv = jnp.einsum('nbhsd,nbhse->nbhde', kf * jnp.exp(cum_last - cum), vf)
    decay = jnp.exp(cum_last[..., 0, :])

    def step(state, xs):
        q_n, kv_n, d_n = xs
        o_n = jnp.einsum('bhcd,bhde->bhce', q_n, state)
        return d_n[..., None] * state + kv_n, o_n

    state0 = jnp.zeros((bsz, HGRN_HEADS, HGRN_HEAD_DIM, HGRN_HEAD_DIM), jnp.float32)
    _, o_inter = lax.scan(step, state0, (q_in, chunk_kv, decay))
    o = (o_intra + o_inter).transpose(1, 0, 3, 2, 4)
    return o.reshape(bsz, seq, HGRN_HEADS, HGRN_HEAD_DIM)

def _causal_depthwise_conv(x, w, b):
    y = lax.conv_general_dilated(
        x, w[:, None, :], window_strides=(1,), padding=[(CONV_WIDTH - 1, 0)],
        dimension_numbers=('NWC', 'WIO', 'NWC'), feature_group_count=x.shape[-1])
    return y + b

def _mixer_hgrn2_conv(h, w_in, w_out, lb, out_norm, dw_w, dw_b, ln_g, ln_b):
    bsz, seq, _ = h.shape
    proj = h @ w_in
    qz, fz, iz, gz, glu_a, glu_b = jnp.split(
        proj, [A_WIDTH, 2 * A_WIDTH, 3 * A_WIDTH, 4 * A_WIDTH, 4 * A_WIDTH + B_WIDTH], axis=-1)
    f = lb + (1.0 - lb) * jax.nn.sigmoid(fz.astype(jnp.float32))
    o = _hgrn2_chunkwise(jax.nn.silu(qz), f, iz)
    o = o * lax.rsqrt(jnp.mean(o * o, axis=-1, keepdims=True) + EPS)
    o_a = (o.reshape(bsz, seq, A_WIDTH) * out_norm.astype(jnp.float32)
           * jax.nn.silu(gz.astype(jnp.float32))).astype(h.dtype)
    c = glu_a * jax.nn.sigmoid(glu_b)
    c = _causal_depthwise_conv(c, dw_w, dw_b)
    o_b = jax.nn.silu(_layernorm(c, ln_g, ln_b))
    return jnp.concatenate([o_a, o_b], axis=-1) @ w_out

def _moba_attention(q, k, v):
    bsz, seq, n_h, hd = q.shape
    n_blk = -(-seq // MOBA_BLOCK)
    s_pad = n_blk * MOBA_BLOCK
    pad = s_pad - seq
    if pad:
        cfg = ((0, 0), (0, pad), (0, 0), (0, 0))
        q, k, v = jnp.pad(q, cfg), jnp.pad(k, cfg), jnp.pad(v, cfg)
    qh = q.transpose(0, 2, 1, 3)
    kb = k.transpose(0, 2, 1, 3).reshape(bsz, n_h, n_blk, MOBA_BLOCK, hd)
    vb = v.transpose(0, 2, 1, 3).reshape(bsz, n_h, n_blk, MOBA_BLOCK, hd)
    topk = min(MOBA_TOPK, n_blk - 1)
    scale = MOBA_HEAD_DIM ** -0.5
    if topk > 0:
        k_mean = jnp.mean(kb.astype(jnp.float32), axis=3)
        blk_score = jnp.einsum('bhqd,bhnd->bhqn', qh.astype(jnp.float32), k_mean)
        q_blk = jnp.arange(s_pad) // MOBA_BLOCK
        fully_past = jnp.arange(n_blk)[None, :] < q_blk[:, None]
        blk_score = jnp.where(fully_past, blk_score, -jnp.inf)
        _, idx = lax.top_k(blk_score, topk)
        idx = idx.astype(jnp.int32)
    else:
        idx = jnp.zeros((bsz, n_h, s_pad, 0), jnp.int32)
    n_qc = s_pad // MOBA_QCHUNK
    h_ar = jnp.arange(n_h)[:, None, None]

    def per_batch(args):
        q_b, kb_b, vb_b, idx_b = args

        def per_chunk(c):
            start = c * MOBA_QCHUNK
            q_c = lax.dynamic_slice_in_dim(q_b, start, MOBA_QCHUNK, axis=1)
            jq = start // MOBA_BLOCK
            k_own = lax.dynamic_index_in_dim(kb_b, jq, axis=1, keepdims=False)
            v_own = lax.dynamic_index_in_dim(vb_b, jq, axis=1, keepdims=False)
            qpos = start + jnp.arange(MOBA_QCHUNK)
            kpos = jq * MOBA_BLOCK + jnp.arange(MOBA_BLOCK)
            s_own = jnp.einsum('hqd,hpd->hqp', q_c, k_own).astype(jnp.float32) * scale
            s_own = jnp.where(kpos[None, :] <= qpos[:, None], s_own, -jnp.inf)
            if topk > 0:
                idx_c = lax.dynamic_slice_in_dim(idx_b, start, MOBA_QCHUNK, axis=1)
                kg = kb_b[h_ar, idx_c]
                vg = vb_b[h_ar, idx_c]
                s_sel = jnp.einsum('hqd,hqkpd->hqkp', q_c, kg).astype(jnp.float32) * scale
                s_sel = jnp.where((idx_c < jq)[..., None], s_sel, -jnp.inf)
                s_sel = s_sel.reshape(n_h, MOBA_QCHUNK, topk * MOBA_BLOCK)
                p = jax.nn.softmax(jnp.concatenate([s_sel, s_own], axis=-1), axis=-1).astype(v_own.dtype)
                p_sel = p[..., :topk * MOBA_BLOCK].reshape(n_h, MOBA_QCHUNK, topk, MOBA_BLOCK)
                o = (jnp.einsum('hqkp,hqkpe->hqe', p_sel, vg)
                     + jnp.einsum('hqp,hpe->hqe', p[..., topk * MOBA_BLOCK:], v_own))
            else:
                p = jax.nn.softmax(s_own, axis=-1).astype(v_own.dtype)
                o = jnp.einsum('hqp,hpe->hqe', p, v_own)
            return o

        out = lax.map(per_chunk, jnp.arange(n_qc))
        return out.transpose(1, 0, 2, 3).reshape(n_h, s_pad, hd)

    out = lax.map(per_batch, (qh, kb, vb, idx))
    return out.transpose(0, 2, 1, 3)[:, :seq]

def _mixer_moba_sgu(h, w_in, w_out, sgu_ln_g, sgu_ln_b, sgu_w, sgu_b):
    bsz, seq, _ = h.shape
    proj = h @ w_in
    qz, kz, vz, uz, zz = jnp.split(
        proj, [C_WIDTH, 2 * C_WIDTH, 3 * C_WIDTH, 3 * C_WIDTH + D_WIDTH], axis=-1)
    hs = (bsz, seq, MOBA_HEADS, MOBA_HEAD_DIM)
    o_c = _moba_attention(qz.reshape(hs), kz.reshape(hs), vz.reshape(hs)).reshape(bsz, seq, C_WIDTH)
    u = jax.nn.gelu(uz, approximate=False)
    z = jax.nn.gelu(zz, approximate=False).reshape(bsz, seq, SGU_GROUPS, SGU_GROUP_DIM)
    z = _layernorm(z, sgu_ln_g.reshape(SGU_GROUPS, SGU_GROUP_DIM), sgu_ln_b.reshape(SGU_GROUPS, SGU_GROUP_DIM))
    zc = z.reshape(bsz, seq // SGU_CHUNK, SGU_CHUNK, SGU_GROUPS, SGU_GROUP_DIM)
    w_s = jnp.where(jnp.tril(jnp.ones((SGU_CHUNK, SGU_CHUNK), dtype=bool)), sgu_w, 0.0)
    mixed = jnp.einsum('gts,bnsgc->bntgc', w_s.astype(zc.dtype), zc) + sgu_b.T[None, None, :, :, None]
    o_d = u * mixed.reshape(bsz, seq, D_WIDTH)
    return jnp.concatenate([o_c, o_d], axis=-1) @ w_out

def _cross_attention(h, mem_n, wq, wkv, wo):
    bsz, seq, _ = h.shape
    q = (h @ wq).reshape(bsz, seq, XA_HEADS, XA_HEAD_DIM)
    k, v = jnp.split(mem_n @ wkv, 2, axis=-1)
    k = k.reshape(bsz, -1, XA_HEADS, XA_HEAD_DIM)
    v = v.reshape(bsz, -1, XA_HEADS, XA_HEAD_DIM)
    s = jnp.einsum('bshd,bmhd->bhsm', q, k).astype(jnp.float32) * (XA_HEAD_DIM ** -0.5)
    p = jax.nn.softmax(s, axis=-1).astype(v.dtype)
    o = jnp.einsum('bhsm,bmhd->bshd', p, v).reshape(bsz, seq, D_MODEL)
    return o @ wo

def _swiglu(h, w_in, w_out):
    a, g = jnp.split(h @ w_in, 2, axis=-1)
    return (jax.nn.silu(a) * g) @ w_out

def first_inputs(seed: int = 0) -> dict:
    key = jax.random.key(seed)
    ks = jax.random.split(key, 32)

    def nrm(k, shape, scale):
        return jax.random.normal(k, shape, jnp.float32) * scale

    def gain(k, shape):
        return 1.0 + 0.02 * jax.random.normal(k, shape, jnp.float32)

    return {
        'x': nrm(ks[0], (BATCH, SEQ, D_MODEL), 1.0),
        'mem': nrm(ks[1], (BATCH, MEM_LEN, D_MODEL), 1.0),
        'norm_mix': gain(ks[2], (DEPTH, D_MODEL)),
        'norm_xattn': gain(ks[3], (DEPTH, D_MODEL)),
        'norm_ffn': gain(ks[4], (DEPTH, D_MODEL)),
        'mem_norm': gain(ks[5], (D_MODEL,)),
        'final_norm': gain(ks[6], (D_MODEL,)),
        'w_in_ab': nrm(ks[7], (N_EVEN, D_MODEL, EVEN_IN), D_MODEL ** -0.5),
        'w_out_ab': nrm(ks[8], (N_EVEN, MIX_WIDTH, D_MODEL), MIX_WIDTH ** -0.5),
        'hgrn_lower_bounds': nrm(ks[9], (DEPTH + 1, A_WIDTH), 0.1),
        'hgrn_out_norm': gain(ks[10], (N_EVEN, A_WIDTH)),
        'conv_dw_w': nrm(ks[11], (N_EVEN, CONV_WIDTH, B_WIDTH), CONV_WIDTH ** -0.5),
        'conv_dw_b': nrm(ks[12], (N_EVEN, B_WIDTH), 0.02),
        'conv_ln_g': gain(ks[13], (N_EVEN, B_WIDTH)),
        'conv_ln_b': nrm(ks[14], (N_EVEN, B_WIDTH), 0.02),
        'w_in_cd': nrm(ks[15], (N_ODD, D_MODEL, ODD_IN), D_MODEL ** -0.5),
        'w_out_cd': nrm(ks[16], (N_ODD, MIX_WIDTH, D_MODEL), MIX_WIDTH ** -0.5),
        'sgu_ln_g': gain(ks[17], (N_ODD, D_WIDTH)),
        'sgu_ln_b': nrm(ks[18], (N_ODD, D_WIDTH), 0.02),
        'sgu_w': nrm(ks[19], (N_ODD, SGU_GROUPS, SGU_CHUNK, SGU_CHUNK), SGU_CHUNK ** -0.5),
        'sgu_b': gain(ks[20], (N_ODD, SGU_GROUPS, SGU_CHUNK)),
        'xa_wq': nrm(ks[21], (DEPTH, D_MODEL, D_MODEL), D_MODEL ** -0.5),
        'xa_wkv': nrm(ks[22], (DEPTH, D_MODEL, 2 * D_MODEL), D_MODEL ** -0.5),
        'xa_wo': nrm(ks[23], (DEPTH, D_MODEL, D_MODEL), D_MODEL ** -0.5),
        'ffn_w_in': nrm(ks[24], (DEPTH, D_MODEL, 2 * FFN_HIDDEN), D_MODEL ** -0.5),
        'ffn_w_out': nrm(ks[25], (DEPTH, FFN_HIDDEN, D_MODEL), FFN_HIDDEN ** -0.5),
    }

def first_block(x, mem, norm_mix, norm_xattn, norm_ffn, mem_norm, final_norm,
              w_in_ab, w_out_ab, hgrn_lower_bounds, hgrn_out_norm,
              conv_dw_w, conv_dw_b, conv_ln_g, conv_ln_b,
              w_in_cd, w_out_cd, sgu_ln_g, sgu_ln_b, sgu_w, sgu_b,
              xa_wq, xa_wkv, xa_wo, ffn_w_in, ffn_w_out):
    lb_all = jnp.cumsum(jax.nn.softmax(hgrn_lower_bounds.astype(jnp.float32), axis=0), axis=0)
    mem_n = _rmsnorm(mem, mem_norm)
    for l in range(DEPTH):
        h = _rmsnorm(x, norm_mix[l])
        if l % 2 == 0:
            e = l // 2
            x = x + _mixer_hgrn2_conv(h, w_in_ab[e], w_out_ab[e], lb_all[l], hgrn_out_norm[e],
                                      conv_dw_w[e], conv_dw_b[e], conv_ln_g[e], conv_ln_b[e])
        else:
            o = l // 2
            x = x + _mixer_moba_sgu(h, w_in_cd[o], w_out_cd[o], sgu_ln_g[o], sgu_ln_b[o],
                                    sgu_w[o], sgu_b[o])
        x = x + _cross_attention(_rmsnorm(x, norm_xattn[l]), mem_n, xa_wq[l], xa_wkv[l], xa_wo[l])
        x = x + _swiglu(_rmsnorm(x, norm_ffn[l]), ffn_w_in[l], ffn_w_out[l])
    return _rmsnorm(x, final_norm)


_first_inputs = first_inputs


def first_inputs(seed=0):
    import zlib

    import numpy as np

    out = dict(_first_inputs(seed))
    spreads = {}
    factors = {}
    for name, (base, spread) in spreads.items():
        noise = np.random.default_rng([zlib.crc32(name.encode()), seed]).standard_normal(out[name].shape)
        drawn = base * np.exp(spread * noise) if base else spread * noise
        out[name] = jnp.asarray(drawn.astype(out[name].dtype))
    for name, factor in factors.items():
        out[name] = (out[name] * factor).astype(out[name].dtype)
    return out


_narrow_inputs = first_inputs


def first_inputs(seed=0):

    out = dict(_narrow_inputs(seed))
    wider = {'norm_mix': 3.16,
     'norm_xattn': 12.0,
     'norm_ffn': 3.49,
     'mem_norm': 12.0,
     'final_norm': 3.08,
     'hgrn_lower_bounds': 12.0,
     'hgrn_out_norm': 6.78,
     'conv_dw_b': 3.33,
     'conv_ln_g': 5.87,
     'conv_ln_b': 6.9,
     'sgu_ln_g': 12.0,
     'sgu_ln_b': 12.0,
     'sgu_b': 9.71}
    for name, times in wider.items():
        mean = out[name].mean()
        out[name] = (mean + times * (out[name] - mean)).astype(out[name].dtype)
    return out


DEPTH_2 = 1

DIFF_HEADS = 4
DIFF_HEAD_DIM = 64
DIFF_QK = DIFF_HEADS * 2 * DIFF_HEAD_DIM
DIFF_V = DIFF_HEADS * 2 * DIFF_HEAD_DIM
RWKV_HEAD_DIM = 64
RWKV_WIDTH = D_MODEL // 2
RWKV_HEADS = RWKV_WIDTH // RWKV_HEAD_DIM
DECAY_RANK = 64
ICLR_RANK = 64
GATE_RANK = 128
FFN_HIDDEN_2 = -(-8 * D_MODEL // (3 * 256)) * 256
NUM_BUCKETS = 32
MAX_DISTANCE = 128
Q_BLOCK = 128
LN_EPS = 1e-5
LNX_EPS = 64e-5
NEG_BIG = -1e30
DEEPNORM_ALPHA = (2.0 * DEPTH_2) ** 0.25
DEEPNORM_BETA = (8.0 * DEPTH_2) ** -0.25

RWKV_SHIFT_WIDTH = 3 * RWKV_WIDTH + DECAY_RANK + ICLR_RANK + GATE_RANK
IN_SIZES = (DIFF_QK, DIFF_QK, DIFF_V, RWKV_SHIFT_WIDTH, D_MODEL, D_MODEL)
IN_SPLIT = tuple(int(s) for s in np.cumsum(IN_SIZES)[:-1])
W_IN_COLS = int(sum(IN_SIZES))
RWKV_SIZES = (RWKV_WIDTH, RWKV_WIDTH, RWKV_WIDTH, DECAY_RANK, ICLR_RANK, GATE_RANK)
RWKV_SPLIT = tuple(int(s) for s in np.cumsum(RWKV_SIZES)[:-1])


def _layer_norm(x, g, b, eps=LN_EPS):
    xf = x.astype(jnp.float32)
    mu = jnp.mean(xf, -1, keepdims=True)
    var = jnp.mean(jnp.square(xf - mu), -1, keepdims=True)
    return ((xf - mu) * lax.rsqrt(var + eps) * g + b).astype(x.dtype)

def _rms_norm(x, g, eps=LN_EPS):
    xf = x.astype(jnp.float32)
    return (xf * lax.rsqrt(jnp.mean(xf * xf, -1, keepdims=True) + eps) * g).astype(x.dtype)

def _t5_bucket(dist):
    max_exact = NUM_BUCKETS // 2
    d = jnp.maximum(dist, 1).astype(jnp.float32)
    large = max_exact + (jnp.log(d / max_exact) / math.log(MAX_DISTANCE / max_exact)
                         * (NUM_BUCKETS - max_exact)).astype(jnp.int32)
    large = jnp.minimum(large, NUM_BUCKETS - 1)
    return jnp.where(dist < max_exact, dist, large)

def _diff_attention(q, k, v, lam, rel_bias):
    B, S = q.shape[0], q.shape[1]
    nblk = S // Q_BLOCK
    scale = DIFF_HEAD_DIM ** -0.5
    qb = q.reshape(B, nblk, Q_BLOCK, DIFF_HEADS, 2, DIFF_HEAD_DIM).transpose(1, 0, 2, 3, 4, 5)
    k_pos = jnp.arange(S, dtype=jnp.int32)

    def block(args):
        i, q_blk = args
        q_pos = i * Q_BLOCK + jnp.arange(Q_BLOCK, dtype=jnp.int32)
        dist = q_pos[:, None] - k_pos[None, :]
        bias = rel_bias[_t5_bucket(jnp.maximum(dist, 0))].astype(jnp.float32)
        logits = jnp.einsum('bqhcd,bkhcd->bhcqk', q_blk, k).astype(jnp.float32) * scale
        logits = logits + bias.transpose(2, 0, 1)[None, :, None]
        logits = jnp.where((dist >= 0)[None, None, None], logits, NEG_BIG)
        p = jax.nn.softmax(logits, axis=-1)
        p = p[:, :, 0] - lam * p[:, :, 1]
        return jnp.einsum('bhqk,bkhe->bqhe', p.astype(v.dtype), v)

    out = lax.map(block, (jnp.arange(nblk, dtype=jnp.int32), qb))
    return out.transpose(1, 0, 2, 3, 4).reshape(B, S, DIFF_HEADS, 2 * DIFF_HEAD_DIM)

def _diff_branch(p_q, p_k, p_v, lq1, lk1, lq2, lk2, subln_g, rel_bias, lambda_init):
    B, S = p_q.shape[0], p_q.shape[1]
    q = p_q.reshape(B, S, DIFF_HEADS, 2, DIFF_HEAD_DIM)
    k = p_k.reshape(B, S, DIFF_HEADS, 2, DIFF_HEAD_DIM)
    v = p_v.reshape(B, S, DIFF_HEADS, 2 * DIFF_HEAD_DIM)
    f32 = jnp.float32
    lam = (jnp.exp(jnp.sum(lq1.astype(f32) * lk1.astype(f32)))
           - jnp.exp(jnp.sum(lq2.astype(f32) * lk2.astype(f32))) + lambda_init)
    o = _diff_attention(q, k, v, lam, rel_bias)
    o = _rms_norm(o, subln_g) * (1.0 - lambda_init)
    return o.reshape(B, S, DIFF_HEADS * 2 * DIFF_HEAD_DIM)

def _rwkv7_scan(r, w, k, v, kk, a):
    B, S, H, N = r.shape

    def step(state, inp):
        r_t, w_t, k_t, v_t, kk_t, a_t = inp
        sa = jnp.einsum('bhij,bhj->bhi', state, -kk_t)
        state = (state * w_t[:, :, None, :]
                 + sa[..., None] * (kk_t * a_t)[:, :, None, :]
                 + v_t[..., None] * k_t[:, :, None, :])
        y = jnp.einsum('bhij,bhj->bhi', state, r_t)
        return state, y

    xs = tuple(t.transpose(1, 0, 2, 3) for t in (r, w, k, v, kk, a))
    state0 = jnp.zeros((B, H, N, N), jnp.float32)
    _, ys = lax.scan(step, state0, xs)
    return ys.transpose(1, 0, 2, 3)

def _rwkv_branch(p, mu, w0, w2, a0, a2, g2, k_k, k_a, r_k, lnx_g, lnx_b):
    B, S = p.shape[0], p.shape[1]
    f32 = jnp.float32
    p_prev = jnp.pad(p[:, :-1], ((0, 0), (1, 0), (0, 0)))
    p = p + (p_prev - p) * mu
    r, k, v, wl, al, gl = jnp.split(p, RWKV_SPLIT, axis=-1)
    w = -jax.nn.softplus(-(w0 + jnp.tanh(wl) @ w2)) - 0.5
    decay = jnp.exp(-jnp.exp(w.astype(f32)))
    a = jax.nn.sigmoid(a0 + al @ a2)
    g = jax.nn.sigmoid(gl) @ g2
    heads = lambda t: t.reshape(B, S, RWKV_HEADS, RWKV_HEAD_DIM)
    kk = heads(k * k_k).astype(f32)
    kk = kk * lax.rsqrt(jnp.maximum(jnp.sum(kk * kk, -1, keepdims=True), 1e-24))
    k = k * (1.0 + (a - 1.0) * k_a)
    r_h, k_h, v_h, a_h = heads(r), heads(k), heads(v), heads(a)
    y = _rwkv7_scan(r_h.astype(f32), heads(decay), k_h.astype(f32), v_h.astype(f32),
                    kk, a_h.astype(f32))
    mean = jnp.mean(y, -1, keepdims=True)
    var = jnp.mean(jnp.square(y - mean), -1, keepdims=True)
    y = ((y - mean) * lax.rsqrt(var + LNX_EPS)).reshape(B, S, RWKV_WIDTH) * lnx_g + lnx_b
    bonus = jnp.sum(r_h.astype(f32) * k_h.astype(f32) * r_k, -1, keepdims=True) * v_h.astype(f32)
    y = y + bonus.reshape(B, S, RWKV_WIDTH)
    return (y * g).astype(p.dtype)

def second_inputs(seed: int = 0) -> dict:
    key = jax.random.key(seed)
    ks = iter(jax.random.split(key, 48))
    L, D, beta = DEPTH_2, D_MODEL, DEEPNORM_BETA

    def nrm(shape, scale):
        return scale * jax.random.normal(next(ks), shape, jnp.float32)

    x = nrm((BATCH, SEQ, D), 1.0)
    ln_in_g = 1.0 + nrm((D,), 0.02)
    ln_in_b = nrm((D,), 0.02)
    rel_bias = nrm((NUM_BUCKETS, DIFF_HEADS), 0.3)
    w_in = jnp.concatenate([
        nrm((L, D, DIFF_QK), D ** -0.5),
        nrm((L, D, DIFF_QK), D ** -0.5),
        nrm((L, D, DIFF_V), beta * D ** -0.5),
        nrm((L, D, 2 * RWKV_WIDTH), D ** -0.5),
        nrm((L, D, RWKV_WIDTH), beta * D ** -0.5),
        nrm((L, D, DECAY_RANK + ICLR_RANK + GATE_RANK), D ** -0.5),
        nrm((L, D, 2 * D), D ** -0.5),
    ], axis=-1)
    diff_lam_q1 = nrm((L, DIFF_HEAD_DIM), 0.1)
    diff_lam_k1 = nrm((L, DIFF_HEAD_DIM), 0.1)
    diff_lam_q2 = nrm((L, DIFF_HEAD_DIM), 0.1)
    diff_lam_k2 = nrm((L, DIFF_HEAD_DIM), 0.1)
    diff_subln_g = 1.0 + nrm((L, 2 * DIFF_HEAD_DIM), 0.02)
    rwkv_mu = jax.random.uniform(next(ks), (L, RWKV_SHIFT_WIDTH), jnp.float32)
    rwkv_w0 = jnp.broadcast_to(jnp.linspace(-6.0, -1.0, RWKV_WIDTH, dtype=jnp.float32),
                               (L, RWKV_WIDTH)) + nrm((L, RWKV_WIDTH), 0.1)
    rwkv_w2 = nrm((L, DECAY_RANK, RWKV_WIDTH), 0.5 * DECAY_RANK ** -0.5)
    rwkv_a0 = nrm((L, RWKV_WIDTH), 0.1)
    rwkv_a2 = nrm((L, ICLR_RANK, RWKV_WIDTH), 0.5 * ICLR_RANK ** -0.5)
    rwkv_g2 = nrm((L, GATE_RANK, RWKV_WIDTH), GATE_RANK ** -0.5)
    rwkv_k_k = 0.85 + nrm((L, RWKV_WIDTH), 0.02)
    rwkv_k_a = 1.0 + nrm((L, RWKV_WIDTH), 0.02)
    rwkv_r_k = nrm((L, RWKV_HEADS, RWKV_HEAD_DIM), 0.1)
    rwkv_lnx_g = 1.0 + nrm((L, RWKV_WIDTH), 0.02)
    rwkv_lnx_b = nrm((L, RWKV_WIDTH), 0.02)
    w_up_a = nrm((L, DIFF_V, D), beta * DIFF_V ** -0.5)
    w_up_b = nrm((L, RWKV_WIDTH, D), beta * RWKV_WIDTH ** -0.5)
    w_out = nrm((L, D, D), beta * D ** -0.5)
    ln1_g = 1.0 + nrm((L, D), 0.02)
    ln1_b = nrm((L, D), 0.02)
    ffn_w_gate = nrm((L, D, FFN_HIDDEN_2), beta * D ** -0.5)
    ffn_w_up = nrm((L, D, FFN_HIDDEN_2), beta * D ** -0.5)
    ffn_w_down = nrm((L, FFN_HIDDEN_2, D), beta * FFN_HIDDEN_2 ** -0.5)
    ln2_g = 1.0 + nrm((L, D), 0.02)
    ln2_b = nrm((L, D), 0.02)
    return {'x': x, 'ln_in_g': ln_in_g, 'ln_in_b': ln_in_b, 'rel_bias': rel_bias,
            'w_in': w_in, 'diff_lam_q1': diff_lam_q1, 'diff_lam_k1': diff_lam_k1,
            'diff_lam_q2': diff_lam_q2, 'diff_lam_k2': diff_lam_k2,
            'diff_subln_g': diff_subln_g, 'rwkv_mu': rwkv_mu, 'rwkv_w0': rwkv_w0,
            'rwkv_w2': rwkv_w2, 'rwkv_a0': rwkv_a0, 'rwkv_a2': rwkv_a2, 'rwkv_g2': rwkv_g2,
            'rwkv_k_k': rwkv_k_k, 'rwkv_k_a': rwkv_k_a, 'rwkv_r_k': rwkv_r_k,
            'rwkv_lnx_g': rwkv_lnx_g, 'rwkv_lnx_b': rwkv_lnx_b, 'w_up_a': w_up_a,
            'w_up_b': w_up_b, 'w_out': w_out, 'ln1_g': ln1_g, 'ln1_b': ln1_b,
            'ffn_w_gate': ffn_w_gate, 'ffn_w_up': ffn_w_up, 'ffn_w_down': ffn_w_down,
            'ln2_g': ln2_g, 'ln2_b': ln2_b}

def second_block(x, ln_in_g, ln_in_b, rel_bias, w_in, diff_lam_q1, diff_lam_k1, diff_lam_q2,
              diff_lam_k2, diff_subln_g, rwkv_mu, rwkv_w0, rwkv_w2, rwkv_a0, rwkv_a2, rwkv_g2,
              rwkv_k_k, rwkv_k_a, rwkv_r_k, rwkv_lnx_g, rwkv_lnx_b, w_up_a, w_up_b, w_out,
              ln1_g, ln1_b, ffn_w_gate, ffn_w_up, ffn_w_down, ln2_g, ln2_b):
    h = _layer_norm(x, ln_in_g, ln_in_b)
    for l in range(DEPTH_2):
        lambda_init = 0.8 - 0.6 * math.exp(-0.3 * l)
        proj = h @ w_in[l]
        p_q, p_k, p_v, p_rwkv, p_ga, p_gb = jnp.split(proj, IN_SPLIT, axis=-1)
        y_a = _diff_branch(p_q, p_k, p_v, diff_lam_q1[l], diff_lam_k1[l], diff_lam_q2[l],
                           diff_lam_k2[l], diff_subln_g[l], rel_bias, lambda_init)
        y_b = _rwkv_branch(p_rwkv, rwkv_mu[l], rwkv_w0[l], rwkv_w2[l], rwkv_a0[l],
                           rwkv_a2[l], rwkv_g2[l], rwkv_k_k[l], rwkv_k_a[l], rwkv_r_k[l],
                           rwkv_lnx_g[l], rwkv_lnx_b[l])
        merged = (jax.nn.sigmoid(p_ga) * (y_a @ w_up_a[l])
                  + jax.nn.sigmoid(p_gb) * (y_b @ w_up_b[l]))
        mix = merged @ w_out[l]
        h = _layer_norm(DEEPNORM_ALPHA * h + mix, ln1_g[l], ln1_b[l])
        ffn = (jax.nn.silu(h @ ffn_w_gate[l]) * (h @ ffn_w_up[l])) @ ffn_w_down[l]
        h = _layer_norm(DEEPNORM_ALPHA * h + ffn, ln2_g[l], ln2_b[l])
    return h


_first_inputs_2 = second_inputs


def second_inputs(seed=0):
    import zlib

    import numpy as np

    out = dict(_first_inputs_2(seed))
    spreads = {}
    factors = {'diff_lam_q1': 2.867,
     'diff_lam_k1': 7.791,
     'diff_lam_q2': 7.796,
     'diff_lam_k2': 8.0,
     'diff_subln_g': 8.0,
     'rwkv_w2': 8.0,
     'rwkv_a0': 8.0,
     'rwkv_a2': 3.439,
     'rwkv_k_k': 8.0,
     'rwkv_k_a': 8.0,
     'rwkv_r_k': 5.382,
     'rwkv_lnx_g': 8.0,
     'rwkv_lnx_b': 8.0,
     'ln1_g': 2.769,
     'ln1_b': 2.882,
     'ln2_g': 2.948,
     'ln2_b': 2.687}
    for name, (base, spread) in spreads.items():
        noise = np.random.default_rng([zlib.crc32(name.encode()), seed]).standard_normal(out[name].shape)
        drawn = base * np.exp(spread * noise) if base else spread * noise
        out[name] = __import__('jax').numpy.asarray(drawn.astype(out[name].dtype))
    for name, factor in factors.items():
        out[name] = (out[name] * factor).astype(out[name].dtype)
    return out


_narrow_inputs_2 = second_inputs


def second_inputs(seed=0):

    out = dict(_narrow_inputs_2(seed))
    wider = {'diff_subln_g': 4.82,
     'rwkv_k_k': 12.0,
     'rwkv_k_a': 5.02,
     'rwkv_lnx_g': 7.0,
     'rwkv_lnx_b': 7.64,
     'ln2_g': 3.32,
     'ln2_b': 3.32}
    for name, times in wider.items():
        mean = out[name].mean()
        out[name] = (mean + times * (out[name] - mean)).astype(out[name].dtype)
    return out


DEPTH_3 = 1

ML_HEADS = 4
ML_WIDTH = D_MODEL
ML_HEAD_DIM = ML_WIDTH // ML_HEADS
ML_CHUNK = 64
CONV_WIDTH_3 = 4
FOX_HEADS = 8
FOX_WIDTH = D_MODEL
FOX_HEAD_DIM = FOX_WIDTH // FOX_HEADS
POOL_GROUPS = 4
POOL_WIDTH = D_MODEL
POOL_GROUP_DIM = POOL_WIDTH // POOL_GROUPS
POOL_WINDOWS = (2, 4, 8, 16)
N_BRANCH = 3

SPLIT_SIZES = ((ML_WIDTH,) * 5 + (ML_HEADS,) * 2 + (FOX_WIDTH,) * 4 + (FOX_HEADS,)
               + (POOL_WIDTH,) * 2 + (N_BRANCH * D_MODEL,))
N_IN = sum(SPLIT_SIZES)
SPLIT_POINTS = tuple(np.cumsum(SPLIT_SIZES)[:-1].tolist())


def rmsnorm(x, g):
    xf = x.astype(jnp.float32)
    r = lax.rsqrt(jnp.mean(xf * xf, axis=-1, keepdims=True) + EPS)
    return (xf * r).astype(x.dtype) * g

def causal_depthwise_conv(x, w):
    K = w.shape[0]
    S = x.shape[1]
    xp = jnp.pad(x, ((0, 0), (K - 1, 0), (0, 0)))
    out = xp[:, 0:S] * w[0]
    for kk in range(1, K):
        out = out + xp[:, kk:kk + S] * w[kk]
    return out

def mlstm_chunkwise(q, k, v, i_pre, f_pre):
    B, S, H, dh = q.shape
    L = ML_CHUNK
    nc = S // L
    q = q.astype(jnp.float32) * (dh ** -0.5)
    k = k.astype(jnp.float32)
    v = v.astype(jnp.float32)
    log_f = jax.nn.log_sigmoid(f_pre.astype(jnp.float32))
    i_g = i_pre.astype(jnp.float32)

    def to_chunks(a):
        a = a.reshape((B, nc, L, H) + a.shape[3:])
        return jnp.moveaxis(a, (1, 3), (0, 2))

    tri = jnp.tril(jnp.ones((L, L), dtype=bool))

    def step(carry, inp):
        C, n, m = carry
        qc, kc, vc, ic, fc = inp
        b = jnp.cumsum(fc, axis=-1)
        D = b[..., :, None] - b[..., None, :] + ic[..., None, :]
        D = jnp.where(tri, D, -jnp.inf)
        inter = b + m[..., None]
        m_t = jnp.maximum(inter, jnp.max(D, axis=-1))
        w_inter = jnp.exp(inter - m_t)
        P = jnp.exp(D - m_t[..., None]) * jnp.einsum('bhtd,bhsd->bhts', qc, kc)
        num = (w_inter[..., None] * jnp.einsum('bhvk,bhtk->bhtv', C, qc)
               + jnp.einsum('bhts,bhsv->bhtv', P, vc))
        den = w_inter * jnp.einsum('bhk,bhtk->bht', n, qc) + jnp.sum(P, axis=-1)
        h = num / jnp.maximum(jnp.abs(den), jnp.exp(-m_t))[..., None]
        bL = b[..., -1]
        dec = bL[..., None] - b + ic
        m_new = jnp.maximum(bL + m, jnp.max(dec, axis=-1))
        w_s = jnp.exp(dec - m_new[..., None])
        w_old = jnp.exp(bL + m - m_new)
        C_new = w_old[..., None, None] * C + jnp.einsum('bhsv,bhsk->bhvk', vc * w_s[..., None], kc)
        n_new = w_old[..., None] * n + jnp.einsum('bhs,bhsk->bhk', w_s, kc)
        return (C_new, n_new, m_new), h

    init = (jnp.zeros((B, H, dh, dh), jnp.float32),
            jnp.zeros((B, H, dh), jnp.float32),
            jnp.zeros((B, H), jnp.float32))
    _, hs = lax.scan(step, init, (to_chunks(q), to_chunks(k), to_chunks(v),
                                  to_chunks(i_g), to_chunks(log_f)))
    hs = jnp.moveaxis(hs, (0, 2), (1, 3))
    return hs.reshape(B, S, H, dh)

def forgetting_attention(q, k, v, f_pre):
    B, S, H, dh = q.shape
    scale = dh ** -0.5
    q = jnp.moveaxis(q, 2, 1)
    k = jnp.moveaxis(k, 2, 1)
    v = jnp.moveaxis(v, 2, 1)
    F = jnp.moveaxis(jnp.cumsum(jax.nn.log_sigmoid(f_pre.astype(jnp.float32)), axis=1), 2, 1)
    k_pos = jnp.arange(S)

    def block(i):
        start = i * Q_BLOCK
        qb = lax.dynamic_slice_in_dim(q, start, Q_BLOCK, axis=2)
        Fb = lax.dynamic_slice_in_dim(F, start, Q_BLOCK, axis=2)
        s = (jnp.einsum('bhqd,bhkd->bhqk', qb, k).astype(jnp.float32) * scale
             + Fb[..., :, None] - F[..., None, :])
        q_pos = start + jnp.arange(Q_BLOCK)
        s = jnp.where(k_pos[None, :] <= q_pos[:, None], s, -jnp.inf)
        p = jax.nn.softmax(s, axis=-1).astype(v.dtype)
        return jnp.einsum('bhqk,bhkd->bhqd', p, v)

    out = lax.map(block, jnp.arange(S // Q_BLOCK))
    out = jnp.moveaxis(out, 0, 2).reshape(B, H, S, dh)
    return jnp.moveaxis(out, 1, 2)

def multiscale_pool(u, pool_w, pool_scale):
    B, S, W = u.shape
    uf = u.astype(jnp.float32)
    cs = jnp.concatenate([jnp.zeros((B, 1, W), jnp.float32), jnp.cumsum(uf, axis=1)], axis=1)
    cs = cs.reshape(B, S + 1, POOL_GROUPS, POOL_GROUP_DIM)
    ug = uf.reshape(B, S, POOL_GROUPS, POOL_GROUP_DIM)
    t = jnp.arange(S)[:, None]
    win = jnp.array(POOL_WINDOWS, dtype=jnp.int32)[None, :]
    lo = jnp.maximum(t + 1 - win, 0)
    g_idx = jnp.arange(POOL_GROUPS)[None, :]
    win_sum = cs[:, 1:] - cs[:, lo, g_idx]
    cnt = jnp.minimum(t + 1, win).astype(jnp.float32)
    d = win_sum / cnt[None, :, :, None] - ug
    y = jnp.einsum('bsgc,gcd->bsgd', d, pool_w.astype(jnp.float32)).reshape(B, S, W)
    return (y * pool_scale).astype(u.dtype)

def hybrid_layer(x, norm_g, w_in, conv_w, ml_bi, ml_bf, ml_norm_g, fox_bf,
                 pool_w, pool_scale, w_branch, w_out):
    B, S, _ = x.shape
    h = rmsnorm(x, norm_g)
    proj = jnp.einsum('bsd,dn->bsn', h, w_in)
    (aq, ak, av, ao, az, ai, af, bq, bk, bv, bz, bf, cu, cz, gates) = jnp.split(proj, SPLIT_POINTS, axis=-1)

    qk = jax.nn.silu(causal_depthwise_conv(jnp.concatenate([aq, ak], axis=-1), conv_w))
    aq, ak = jnp.split(qk, 2, axis=-1)
    hA = mlstm_chunkwise(aq.reshape(B, S, ML_HEADS, ML_HEAD_DIM),
                         ak.reshape(B, S, ML_HEADS, ML_HEAD_DIM),
                         av.reshape(B, S, ML_HEADS, ML_HEAD_DIM),
                         ai + ml_bi, af + ml_bf)
    hA = hA * lax.rsqrt(jnp.mean(hA * hA, axis=-1, keepdims=True) + EPS)
    yA = (hA.reshape(B, S, ML_WIDTH).astype(x.dtype) * ml_norm_g
          * jax.nn.sigmoid(ao) * jax.nn.silu(az))

    hB = forgetting_attention(bq.reshape(B, S, FOX_HEADS, FOX_HEAD_DIM),
                              bk.reshape(B, S, FOX_HEADS, FOX_HEAD_DIM),
                              bv.reshape(B, S, FOX_HEADS, FOX_HEAD_DIM),
                              bf + fox_bf)
    yB = hB.reshape(B, S, FOX_WIDTH) * jax.nn.silu(bz)

    yC = multiscale_pool(cu, pool_w, pool_scale) * jax.nn.silu(cz)

    ys = jnp.stack([yA, yB, yC], axis=2)
    yb = jnp.einsum('bsnw,nwd->bsnd', ys, w_branch)
    g = jax.nn.sigmoid(gates.reshape(B, S, N_BRANCH, D_MODEL))
    merged = jnp.sum(g * yb, axis=2)
    return x + jnp.einsum('bsd,de->bse', merged, w_out)

def third_inputs(seed: int = 0) -> dict:
    key = jax.random.key(seed)
    ks = jax.random.split(key, 16)
    f32 = jnp.float32
    nrm = lambda k, shape: jax.random.normal(k, shape, f32)
    x = nrm(ks[0], (BATCH, SEQ, D_MODEL))
    norm_g = 1.0 + 0.02 * nrm(ks[1], (DEPTH_3, D_MODEL))
    w_in = nrm(ks[2], (DEPTH_3, D_MODEL, N_IN)) * D_MODEL ** -0.5
    conv_w = nrm(ks[3], (DEPTH_3, CONV_WIDTH_3, 2 * ML_WIDTH)) * CONV_WIDTH_3 ** -0.5
    ml_bi = 0.1 * nrm(ks[4], (DEPTH_3, ML_HEADS))
    ml_bf = jnp.linspace(3.0, 6.0, ML_HEADS, dtype=f32)[None, :] + 0.1 * nrm(ks[5], (DEPTH_3, ML_HEADS))
    ml_norm_g = 1.0 + 0.02 * nrm(ks[6], (DEPTH_3, ML_WIDTH))
    fox_bf = jnp.linspace(0.0, 4.0, FOX_HEADS, dtype=f32)[None, :] + 0.1 * nrm(ks[7], (DEPTH_3, FOX_HEADS))
    pool_w = nrm(ks[8], (DEPTH_3, POOL_GROUPS, POOL_GROUP_DIM, POOL_GROUP_DIM)) * POOL_GROUP_DIM ** -0.5
    pool_scale = 1.0 + 0.02 * nrm(ks[9], (DEPTH_3, POOL_WIDTH))
    w_branch = nrm(ks[10], (DEPTH_3, N_BRANCH, ML_WIDTH, D_MODEL)) * ML_WIDTH ** -0.5
    w_out = nrm(ks[11], (DEPTH_3, D_MODEL, D_MODEL)) * D_MODEL ** -0.5
    final_g = 1.0 + 0.02 * nrm(ks[12], (D_MODEL,))
    return {"x": x, "norm_g": norm_g, "w_in": w_in, "conv_w": conv_w, "ml_bi": ml_bi,
            "ml_bf": ml_bf, "ml_norm_g": ml_norm_g, "fox_bf": fox_bf, "pool_w": pool_w,
            "pool_scale": pool_scale, "w_branch": w_branch, "w_out": w_out, "final_g": final_g}

def third_block(x, norm_g, w_in, conv_w, ml_bi, ml_bf, ml_norm_g, fox_bf,
              pool_w, pool_scale, w_branch, w_out, final_g):
    for l in range(DEPTH_3):
        x = hybrid_layer(x, norm_g[l], w_in[l], conv_w[l], ml_bi[l], ml_bf[l], ml_norm_g[l],
                         fox_bf[l], pool_w[l], pool_scale[l], w_branch[l], w_out[l])
    return rmsnorm(x, final_g)


_first_inputs_3 = third_inputs


def third_inputs(seed=0):
    import zlib

    import numpy as np

    out = dict(_first_inputs_3(seed))
    spreads = {}
    factors = {'norm_g': 4.674,
     'ml_bi': 200.0,
     'ml_norm_g': 200.0,
     'pool_scale': 75.386,
     'final_g': 24.166,
     'conv_w': 4.087,
     'fox_bf': 2.915}
    for name, (base, spread) in spreads.items():
        noise = np.random.default_rng([zlib.crc32(name.encode()), seed]).standard_normal(out[name].shape)
        drawn = base * np.exp(spread * noise) if base else spread * noise
        out[name] = __import__('jax').numpy.asarray(drawn.astype(out[name].dtype))
    for name, factor in factors.items():
        out[name] = (out[name] * factor).astype(out[name].dtype)
    return out


_narrow_inputs_3 = third_inputs


def third_inputs(seed=0):

    out = dict(_narrow_inputs_3(seed))
    wider = {'ml_norm_g': 9.49, 'fox_bf': 6.11, 'pool_scale': 3.46, 'final_g': 3.26}
    for name, times in wider.items():
        mean = out[name].mean()
        out[name] = (mean + times * (out[name] - mean)).astype(out[name].dtype)
    return out


def setup_inputs(seed=0):
    out = dict(first_inputs(seed))
    for name, value in second_inputs(seed + 1).items():
        if name != "x":
            out[name + "_2"] = value
    for name, value in third_inputs(seed + 2).items():
        if name != "x":
            out[name + "_3"] = value
    return out


def reference(
    x, mem, norm_mix, norm_xattn, norm_ffn, mem_norm, final_norm, w_in_ab, w_out_ab,
    hgrn_lower_bounds, hgrn_out_norm, conv_dw_w, conv_dw_b, conv_ln_g, conv_ln_b, w_in_cd,
    w_out_cd, sgu_ln_g, sgu_ln_b, sgu_w, sgu_b, xa_wq, xa_wkv, xa_wo, ffn_w_in, ffn_w_out,
    ln_in_g_2, ln_in_b_2, rel_bias_2, w_in_2, diff_lam_q1_2, diff_lam_k1_2, diff_lam_q2_2,
    diff_lam_k2_2, diff_subln_g_2, rwkv_mu_2, rwkv_w0_2, rwkv_w2_2, rwkv_a0_2, rwkv_a2_2,
    rwkv_g2_2, rwkv_k_k_2, rwkv_k_a_2, rwkv_r_k_2, rwkv_lnx_g_2, rwkv_lnx_b_2, w_up_a_2,
    w_up_b_2, w_out_2, ln1_g_2, ln1_b_2, ffn_w_gate_2, ffn_w_up_2, ffn_w_down_2, ln2_g_2,
    ln2_b_2, norm_g_3, w_in_3, conv_w_3, ml_bi_3, ml_bf_3, ml_norm_g_3, fox_bf_3, pool_w_3,
    pool_scale_3, w_branch_3, w_out_3, final_g_3,
):
    x = first_block(
        x, mem, norm_mix, norm_xattn, norm_ffn, mem_norm, final_norm, w_in_ab, w_out_ab,
        hgrn_lower_bounds, hgrn_out_norm, conv_dw_w, conv_dw_b, conv_ln_g, conv_ln_b, w_in_cd,
        w_out_cd, sgu_ln_g, sgu_ln_b, sgu_w, sgu_b, xa_wq, xa_wkv, xa_wo, ffn_w_in, ffn_w_out,
    )
    x = second_block(
        x, ln_in_g_2, ln_in_b_2, rel_bias_2, w_in_2, diff_lam_q1_2, diff_lam_k1_2,
        diff_lam_q2_2, diff_lam_k2_2, diff_subln_g_2, rwkv_mu_2, rwkv_w0_2, rwkv_w2_2,
        rwkv_a0_2, rwkv_a2_2, rwkv_g2_2, rwkv_k_k_2, rwkv_k_a_2, rwkv_r_k_2, rwkv_lnx_g_2,
        rwkv_lnx_b_2, w_up_a_2, w_up_b_2, w_out_2, ln1_g_2, ln1_b_2, ffn_w_gate_2, ffn_w_up_2,
        ffn_w_down_2, ln2_g_2, ln2_b_2,
    )
    return third_block(
        x, norm_g_3, w_in_3, conv_w_3, ml_bi_3, ml_bf_3, ml_norm_g_3, fox_bf_3, pool_w_3,
        pool_scale_3, w_branch_3, w_out_3, final_g_3,
    )


_drawn_inputs = setup_inputs


def setup_inputs(seed=0):
    import zlib

    import numpy as np

    out = dict(_drawn_inputs(seed))
    spreads = {}
    factors = {}
    for name, (base, spread) in spreads.items():
        noise = np.random.default_rng([zlib.crc32(name.encode()), seed]).standard_normal(out[name].shape)
        drawn = base * np.exp(spread * noise) if base else spread * noise
        out[name] = jnp.asarray(drawn.astype(out[name].dtype))
    for name, factor in factors.items():
        out[name] = (out[name] * factor).astype(out[name].dtype)
    return out
```

```python
import math
from contextlib import ExitStack

import numpy as np
import concourse.bass as bass
from concourse import mybir

F32 = mybir.dt.float32
F32R = mybir.dt.float32r
U32 = mybir.dt.uint32
ALU = mybir.AluOpType
ACT = mybir.ActivationFunctionType
AX = mybir.AxisListType

P = 128
S = 512
TT = S // P
D = 1024
KT = D // P
MEM = 256
HID = 2816
NH = HID // P
SPLIT = 2
RAW = 4
NEG = -1e30
EPS6, EPS5, EPSX = 1e-6, 1e-5, 64e-5
ALPHA = 2.0 ** 0.25
LAMBDA0 = 0.8 - 0.6 * math.exp(0.0)

VECS = [
    ("norm_mix0", 8), ("norm_mix1", 8), ("norm_xattn0", 8), ("norm_xattn1", 8), ("norm_ffn0", 8), ("norm_ffn1", 8),
    ("mem_norm", 8), ("final_norm", 8), ("lb", 12), ("hgrn_out_norm", 4), ("conv_dw_w", 124), ("conv_dw_b", 4),
    ("conv_ln_g", 4), ("conv_ln_b", 4), ("sgu_ln_g", 4), ("sgu_ln_b", 4),
    ("ln_in_g", 8), ("ln_in_b", 8), ("subln_g", 1), ("mu", 14), ("w0", 4), ("a0", 4), ("k_k", 4), ("k_a", 4),
    ("r_k", 4), ("lnx_g", 4), ("lnx_b", 4), ("ln1_g", 8), ("ln1_b", 8), ("ln2_g", 8), ("ln2_b", 8),
    ("norm_g3", 8), ("conv_w3", 64), ("ml_norm_g", 8), ("pool_scale", 8), ("final_g", 8),
    ("ml_bi", 1), ("ml_bf", 1), ("fox_bf", 1),
]
VCOL = {}
for _name, _n in VECS:
    VCOL[_name] = sum(n for _, n in VECS[:len(VCOL)])
NVEC = sum(n for _, n in VECS)

CONSTS = [("ident", 128), ("ones", 128), ("ones64", 128), ("cadd", 128), ("caddT", 128), ("chunkT", 128),
          ("causalT", 128), ("sub16", 128), ("off16", 128), ("sub16T", 128), ("strictT", 128),
          ("icnt", 128), ("flip", 128), ("caddR", 128),
          ("eps6", 1), ("eps5", 1), ("epsx", 1), ("one", 1)]
CCOL = {}
for _name, _n in CONSTS:
    CCOL[_name] = sum(n for _, n in CONSTS[:len(CCOL)])
NCONST = sum(n for _, n in CONSTS)


def constants():
    c = np.zeros((P, NCONST), np.float32)

    def put(name, a):
        c[:a.shape[0], CCOL[name]:CCOL[name] + a.shape[1]] = a

    p, f = np.arange(P)[:, None], np.arange(P)[None, :]
    chunk = p // 64 == f // 64
    block = p // 16 == f // 16
    put("ident", np.eye(P))
    put("ones", np.ones((P, P)))
    put("ones64", chunk * 1.0)
    put("cadd", np.where(f <= p, 0.0, NEG))
    put("flip", np.eye(P)[::-1])
    put("caddR", np.where(f <= P - 1 - p, 0.0, NEG))
    put("caddT", np.where(p <= f, 0.0, NEG))
    put("chunkT", (chunk & (p <= f)) * 1.0)
    put("causalT", (p <= f) * 1.0)
    put("sub16", (block & (f < p)) * 1.0)
    put("off16", (chunk & ~block & (f < p)) * 1.0)
    put("sub16T", (block & (p < f)) * 1.0)
    put("strictT", (chunk & (p < f)) * 1.0)
    cnt = np.zeros((8, 16))
    for g, w in enumerate((2, 4, 8, 16)):
        cnt[2 * g:2 * g + 2] = 1.0 / np.minimum(np.arange(16) + 1, w)
    put("icnt", np.repeat(cnt.reshape(1, 128), P, 0))
    for name, v in (("eps6", EPS6), ("eps5", EPS5), ("epsx", EPSX), ("one", 1.0)):
        put(name, np.full((P, 1), v))
    return c


def reset_mask():
    return np.repeat((np.arange(S) % 64 != 0)[None].astype(np.float32), P, 0)


def bucket_table():
    dist = np.maximum(255 - np.arange(383), 0)
    d = np.maximum(dist, 1).astype(np.float32)
    large = 16 + (np.log(d / np.float32(16)) / np.float32(math.log(8.0)) * np.float32(16)).astype(np.int32)
    bucket = np.where(dist < 16, dist, np.minimum(large, 31))
    hot = np.zeros((32, 384), np.float32)
    hot[bucket, np.arange(383)] = 1.0
    return hot


UNITS = [
    ("l0.glu", 8), ("l0.q", 4), ("l0.f", 4), ("l0.i", 4), ("l0.g", 4), ("l0.out", 8),
    ("x0.k", 8), ("x0.v", 8), ("x0.q", 8), ("x0.o", 8), ("f0.up", 2 * NH), ("f0.down", NH),
    ("l1.qk", 8), ("l1.v", 4), ("l1.uz", 8), ("l1.out", 8),
    ("x1.k", 8), ("x1.v", 8), ("x1.q", 8), ("x1.o", 8), ("f1.up", 2 * NH), ("f1.down", NH),
    ("s.q", 4), ("s.k", 4), ("s.v", 4), ("s.rwkv", 14), ("s.up", 24), ("s.out", 8),
    ("fs.up", 2 * NH), ("fs.down", NH),
    ("t.gif", 1), ("t.qk", 16), ("t.v", 8), ("t.oz", 16), ("t.br0", 16),
    ("t.fq", 8), ("t.fk", 8), ("t.fv", 8), ("t.fz", 8), ("t.br1", 16),
    ("t.cu", 8), ("t.pool", 2), ("t.cz", 8), ("t.br2", 16), ("t.out", 8),
]
U0 = {}
for _name, _n in UNITS:
    U0[_name] = sum(n for _, n in UNITS[:len(U0)])
NUNITS = sum(n for _, n in UNITS)
NU = dict(UNITS)


class Steps:

    def __init__(self, eng, sem, names, sems):
        self.eng, self.sem, self.names, self.sems, self.n, self.seen = eng, sem, names, sems, 0, 0

    def do(self, ins, name=None):
        ins.then_inc(self.sem, 1)
        self.n = self.n + 1
        if name is not None:
            self.names[name] = (self.sem, self.n)

    def settle(self):
        if self.seen is not self.n:
            self.eng.wait_ge(self.sem, self.n)
            self.seen = self.n

    def wait(self, *names):
        for name in names:
            sem, n = self.names[name] if name in self.names else self.names["unknown"]
            self.eng.wait_ge(self.sems.get(sem.name, sem), n)


def program(nc, io, names):
    ctx = ExitStack()
    with ctx:
        def sb(name, shape, dt=F32):
            return ctx.enter_context(nc.sbuf_tensor(name, shape, dt))

        sems = {}

        def sem(name):
            sems[name] = ctx.enter_context(nc.semaphore(name))
            return sems[name]

        X = sb("X", [P, KT, S])
        XH, XL = sb("XH", [P, KT, S], F32R), sb("XL", [P, KT, S], F32R)
        YH, YL = sb("YH", [P, KT, S], F32R), sb("YL", [P, KT, S], F32R)
        RW = sb("RW", [P, RAW, D])
        WH, WL = sb("WH", [P, SPLIT, D], F32R), sb("WL", [P, SPLIT, D], F32R)
        A = sb("A", [P, 38, S])
        VEC = sb("VEC", [P, NVEC])
        CST = sb("CST", [P, NCONST])
        SD = sb("SD", [P, S])
        SM = sb("SM", [P, 160])
        PS = ctx.enter_context(nc.psum_tensor("PS", [P, 8, S], F32))
        TAB = nc.dram_tensor("bias_by_distance", [4, 384], F32, kind="Internal").ap()

        raw_full = [sem(f"raw_full{i}") for i in range(RAW)]
        split_hi, split_done = sem("split_hi"), sem("split_done")
        slots_open = sem("slots_open")
        unit_done = sem("unit_done")
        banks_free = sem("banks_free")
        params = sem("params")
        loads = [sem(f"load{i}") for i in range(16)]
        scalar_steps, vector_steps, tensor_steps = sem("scalar_steps"), sem("vector_steps"), sem("tensor_steps")

        MH = YH[:, 0:4, :].rearrange("p a (b c) -> p (a b) c", c=MEM)
        ML = YL[:, 0:4, :].rearrange("p a (b c) -> p (a b) c", c=MEM)

        def vec(name, k=0, n=1):
            return VEC[:, VCOL[name] + k:VCOL[name] + k + n]

        def cst(name, rows=P, k=0, n=None):
            n = dict(CONSTS)[name] if n is None else n
            return CST[0:rows, CCOL[name] + k:CCOL[name] + k + n]

        ident, ones, ones64 = cst("ident"), cst("ones"), cst("ones64")

        def T(i, n=None):
            return A[:, i, :] if n is None else A[:, i:i + n, :]

        def W2(i, n):
            return A[:, i:i + n, :].rearrange("p a b -> p (a b)")

        def bank(b, cols=S, rows=P, base=0):
            return PS[base:base + rows, b, 0:cols]

        mm = nc.tensor.matmul

        evac = [0]

        def unit_passes(out, hi, lo, xh, xl, first, last):
            mm(out, hi, xh, start=first, stop=False)
            mm(out, hi, xl, start=False, stop=False)
            return mm(out, lo, xh, start=False, stop=last)

        def pe_tile(pe, u, e, slot, b, xh, xl, cols):
            pe.wait_ge(split_done, u + 1)
            pe.wait_ge(banks_free, e + 1)
            for k in range(KT):
                last = unit_passes(bank(b, cols), WH[:, slot, k * P:(k + 1) * P], WL[:, slot, k * P:(k + 1) * P],
                                   xh[:, k, 0:cols], xl[:, k, 0:cols], k == 0, k == KT - 1)
            last.then_inc(unit_done, 1)

        def pe_linear(pe, name, e0, xh=None, xl=None, cols=S, n=None):
            xh, xl = (XH, XL) if xh is None else (xh, xl)
            u0, n = U0[name], NU[name] if n is None else n
            if n >= 4:
                with pe.Fori(0, n // 4) as i:
                    for j in range(4):
                        pe_tile(pe, u0 + i * 4 + j, e0 + i * 4 + j, (u0 + j) % SPLIT, (e0 + j) % 4, xh, xl, cols)
            for j in range(n // 4 * 4, n):
                pe_tile(pe, u0 + j, e0 + j, (u0 + j) % SPLIT, (e0 + j) % 4, xh, xl, cols)

        def each_tile(eng, st, n, e0, u0, take, steps=0):
            def one(j, jj):
                eng.wait_ge(unit_done, u0 + j + 1)
                take(j, (e0 + jj) % 4).then_inc(banks_free, 1)
            eng.wait_ge(banks_free, 4 + e0)
            if n >= 4:
                base = st.n
                with eng.Fori(0, n // 4) as i:
                    for j in range(4):
                        st.n = base + (i * 4 + j) * steps
                        one(i * 4 + j, j)
                st.n = base + n // 4 * 4 * steps
            for j in range(n // 4 * 4, n):
                one(j, j)

        PLAN = []

        def stage(f, *args, **kw):
            PLAN.append((f, args, kw))

        class Linear:

            def __init__(self, name, dst=None, func=ACT.Copy, xh=None, xl=None, cols=S, n=None, ready=(), add=None,
                         scale=1.0, alpha=None, dstf=None, pre=()):
                self.name, self.dst, self.func, self.cols = name, dst, func, cols
                self.xh, self.xl, self.ready, self.add, self.scale, self.alpha = xh, xl, ready, add, scale, alpha
                self.n = NU[name] if n is None else n
                self.dstf, self.pre = dstf, pre
                self.e0 = evac[0]
                evac[0] += self.n
                PLAN.append(self)

            def tensor(self, pe, st):
                st.wait(*self.ready)
                pe_linear(pe, self.name, self.e0, self.xh, self.xl, self.cols, self.n)

            def scalar(self, act, st):
                if self.add is not None:
                    return
                st.wait(*self.pre)
                st.settle()

                def take(j, b):
                    return nc.scalar.activation(self.dst(j), PS[:, b:b + 1, 0:self.cols], self.func, scale=self.scale)
                each_tile(act, st, self.n, self.e0, U0[self.name], take)

            def vector(self, dve, st):
                if self.add is None:
                    return
                st.settle()

                def take(j, b):
                    x = X[:, bass.ds(j, 1), :]
                    if self.alpha is None:
                        return nc.vector.tensor_tensor(x, x, PS[:, b:b + 1, :], ALU.add)
                    return nc.vector.scalar_tensor_tensor(out=x, in0=x, scalar=self.alpha, in1=PS[:, b:b + 1, :],
                                                          op0=ALU.mult, op1=ALU.add)
                each_tile(dve, st, self.n, self.e0, U0[self.name], take)

        class Pairs:

            def __init__(self, name, n, dst, func, of=0, yh=None, acc=None, ready=(), u_off=0, func2=None):
                self.name, self.n, self.dst, self.func, self.of, self.acc, self.ready = name, n, dst, func, of, acc, ready
                self.yh, self.u0, self.func2 = yh, U0[name] + u_off, func2
                self.e0 = evac[0]
                evac[0] += 2 * n
                PLAN.append(self)

            def tensor(self, pe, st):
                st.wait(*self.ready)
                with pe.Fori(0, self.n // 2) as i:
                    for j in range(4):
                        xh, xl = self.yh if (self.yh is not None and j % 2 == 0) else (XH, XL)
                        pe_tile(pe, self.u0 + i * 4 + j, self.e0 + i * 4 + j, (self.u0 + j) % SPLIT, (self.e0 + j) % 4, xh, xl, S)

            def scalar(self, act, st):
                st.settle()
                base = st.n
                k = 1 if self.func2 is None else 2
                with act.Fori(0, self.n // 2) as i:
                    for j in range(2):
                        act.wait_ge(unit_done, self.u0 + i * 4 + 2 * j + 1 + self.of)
                        act.wait_ge(banks_free, self.e0 + 2 + i * 4 + 2 * j)
                        st.n = base + (i * 2 + j) * k
                        st.do(nc.scalar.activation(SG[:, j, :], bank((self.e0 + 2 * j + self.of) % 4), self.func))
                        if self.func2 is not None:
                            act.wait_ge(unit_done, self.u0 + i * 4 + 2 * j + 2 - self.of)
                            st.do(nc.scalar.activation(SG[:, 2 + j, :], bank((self.e0 + 2 * j + 1 - self.of) % 4), self.func2))
                st.n = base + self.n * k
                self.names_base = base
                st.names[self.name + ".pairs"] = (scalar_steps, base)

            def vector(self, dve, st):
                st.settle()
                dve.wait_ge(banks_free, 4 + self.e0)
                k = 1 if self.func2 is None else 2
                base = st.names[self.name + ".pairs"][1]
                with dve.Fori(0, self.n // 2) as i:
                    for j in range(2):
                        dve.wait_ge(scalar_steps, base + (i * 2 + j + 1) * k)
                        dve.wait_ge(unit_done, self.u0 + i * 4 + 2 * j + 2)
                        other = PS[:, (self.e0 + 2 * j + 1 - self.of) % 4, :] if self.func2 is None else SG[:, 2 + j, :]
                        if self.acc is None:
                            nc.vector.tensor_tensor(self.dst(i * 2 + j), SG[:, j:j + 1, :] , other.rearrange("p (a b) -> p a b", a=1),
                                                    ALU.mult).then_inc(banks_free, 2)
                        else:
                            nc.vector.tensor_tensor(SG[:, j, :], SG[:, j, :], other, ALU.mult).then_inc(pair_products, 1)
                            dve.wait_ge(pair_products, self.acc + i * 2 + j + 1)
                            nc.vector.tensor_tensor(self.dst(i * 2 + j), self.dst(i * 2 + j), SG[:, j:j + 1, :],
                                                    ALU.add).then_inc(banks_free, 2)

        SG = sb("SG", [P, 4, S])
        pair_products = sem("pair_products")

        class TokenMajor:

            def __init__(self, name, halves, dst, xh=None, xl=None, tiles=TT, ready=(), pre=()):
                self.name, self.halves, self.dst, self.tiles, self.ready, self.pre = name, halves, dst, tiles, ready, pre
                self.xh, self.xl = (XH, XL) if xh is None else (xh, xl)
                self.e0 = evac[0]
                evac[0] += halves * tiles
                PLAN.append(self)

            def tensor(self, pe, st):
                st.wait(*self.ready)
                for h in range(self.halves):
                    e = self.e0 + h * self.tiles
                    pe.wait_ge(banks_free, e + self.tiles)
                    for m in range(4):
                        u = U0[self.name] + 4 * h + m
                        pe.wait_ge(split_done, u + 1)
                        for kk in range(2):
                            k = 2 * m + kk
                            wh = WH[:, u % SPLIT, kk * S:(kk + 1) * S]
                            wl = WL[:, u % SPLIT, kk * S:(kk + 1) * S]
                            for t in range(self.tiles):
                                o = bank((e + t) % 4)
                                xh, xl = self.xh[:, k, t * P:(t + 1) * P], self.xl[:, k, t * P:(t + 1) * P]
                                mm(o, xh, wh, start=(k == 0), stop=False)
                                mm(o, xh, wl, start=False, stop=False)
                                last = mm(o, xl, wh, start=False, stop=(k == KT - 1))
                        last.then_inc(unit_done, 1)

            def scalar(self, act, st):
                st.wait(*self.pre)
                st.settle()
                act.wait_ge(banks_free, 4 + self.e0)
                for h in range(self.halves):
                    e = self.e0 + h * self.tiles
                    act.wait_ge(unit_done, U0[self.name] + 4 * h + 4)
                    for t in range(self.tiles):
                        nc.scalar.activation(self.dst(h, t), bank((e + t) % 4), ACT.Copy).then_inc(banks_free, 1)

            def vector(self, dve, st):
                pass

        class Down:

            def __init__(self, name, alpha=None):
                self.name, self.alpha, self.e0 = name, alpha, evac[0]
                evac[0] += KT
                PLAN.append(self)

            def hslot(self, k):
                return 4 + k % 4

            def tensor(self, pe, st):
                pe.wait_ge(banks_free, 4 + self.e0)
                u0 = U0[self.name]
                for k in range(NH):
                    pe.wait_ge(split_done, u0 + k + 1)
                    st.wait(f"{self.name}.lo{k}")
                    xh, xl = YH[:, self.hslot(k), :], YL[:, self.hslot(k), :]
                    for j in range(KT):
                        last = unit_passes(bank(j), WH[:, (u0 + k) % SPLIT, j * P:(j + 1) * P],
                                           WL[:, (u0 + k) % SPLIT, j * P:(j + 1) * P], xh, xl, k == 0, k == NH - 1)
                        if k == NH - 1 and j < KT - 1:
                            st.do(last, f"{self.name}.out{j}")
                    last.then_inc(unit_done, 1)

            def scalar(self, act, st):
                act.wait_ge(banks_free, 4 + self.e0)
                for k in range(NH):
                    if k >= 4:
                        act.wait_ge(unit_done, U0[self.name] + k - 3)
                        st.wait(f"{self.name}.lo{k - 4}")
                    st.do(nc.scalar.activation(YH[:, self.hslot(k), :], T(k), ACT.Copy), f"{self.name}.hi{k}")

            def vector(self, dve, st):
                dve.wait_ge(banks_free, 4 + self.e0)
                for k in range(NH):
                    st.wait(f"{self.name}.hi{k}")
                    st.do(nc.vector.tensor_tensor(YL[:, self.hslot(k), :], T(k), YH[:, self.hslot(k), :].bitcast(F32),
                                                  ALU.subtract), f"{self.name}.lo{k}")
                for j in range(KT):
                    if j < KT - 1:
                        st.wait(f"{self.name}.out{j}")
                    else:
                        dve.wait_ge(unit_done, U0[self.name] + NH)
                    if self.alpha is None:
                        nc.vector.tensor_tensor(X[:, j, :], X[:, j, :], bank(j), ALU.add).then_inc(banks_free, 1)
                    else:
                        nc.vector.scalar_tensor_tensor(out=X[:, j, :], in0=X[:, j, :], scalar=self.alpha, in1=bank(j),
                                                       op0=ALU.mult, op1=ALU.add).then_inc(banks_free, 1)

        class Stage:
            def __init__(self, **fns):
                self.fns = fns
                self.e = evac[0]
                PLAN.append(self)

            def run(self, role, eng, st):
                if role in self.fns:
                    st.settle()
                    self.fns[role](eng, st, self.e)

        def colnorm(id, groups, n, eps, center, apply, sq, xc, sums=ones, cols=S, b0=4, rows=None):
            def src(g, k):
                i = sum(len(x) for x in groups[:g]) + k
                return xc(i) if center else groups[g][k]

            def tensor(pe, st, e):
                pe.wait_ge(banks_free, 4 + e)
                st.wait(*[id + ".in"] * (id + ".in" in names))
                for g, tiles in enumerate(groups):
                    if center:
                        if g >= 2:
                            st.wait(f"{id}.xc{sum(len(x) for x in groups[:g - 1]) - 1}")
                        for k, t in enumerate(tiles):
                            last = mm(bank(b0 + g % 2, cols), sums, t, start=(k == 0), stop=(k == len(tiles) - 1))
                        st.do(last, f"{id}.mean{g}")
                    if g >= 1 or not center:
                        squares(pe, st, g - 1 if center else g)
                if center:
                    squares(pe, st, len(groups) - 1)

            def squares(pe, st, g):
                i0 = sum(len(x) for x in groups[:g])
                if g >= 2:
                    st.wait(f"{id}.std{g - 2}")
                for k in range(len(groups[g])):
                    st.wait(f"{id}.sq{i0 + k}")
                    last = mm(bank(b0 + 2 + g % 2, cols), sums, sq(i0 + k), start=(k == 0), stop=(k == len(groups[g]) - 1))
                st.do(last, f"{id}.var{g}")

            def scalar(act, st, e):
                act.wait_ge(banks_free, 4 + e)
                st.wait(*[id + ".in"] * (id + ".in" in names))
                i = 0
                for g, tiles in enumerate(groups):
                    for k in range(len(tiles)):
                        if center:
                            st.wait(f"{id}.xc{i}")
                        st.do(nc.scalar.activation(sq(i), src(g, k), ACT.Square), f"{id}.sq{i}")
                        i += 1
                for g in range(len(groups)):
                    st.wait(f"{id}.var{g}")
                    if g >= 2:
                        st.wait(f"{id}.rstd{g - 2}")
                    st.do(nc.scalar.activation(NR[:, g % 2, 0:cols], bank(b0 + 2 + g % 2, cols), ACT.Sqrt,
                                               bias=cst(eps), scale=1.0 / n), f"{id}.std{g}")

            def vector(dve, st, e):
                dve.wait_ge(banks_free, 4 + e)
                i = 0
                if center:
                    for g, tiles in enumerate(groups):
                        st.wait(f"{id}.mean{g}")
                        for k, t in enumerate(tiles):
                            st.do(nc.vector.scalar_tensor_tensor(out=xc(i), in0=bank(b0 + g % 2, cols), scalar=-1.0 / n,
                                                                 in1=t, op0=ALU.mult, op1=ALU.add), f"{id}.xc{i}")
                            i += 1
                for g, tiles in enumerate(groups):
                    st.wait(f"{id}.std{g}")
                    st.settle()
                    st.do(nc.vector.reciprocal(NR[:, g % 2, 0:cols], NR[:, g % 2, 0:cols]))
                    st.settle()
                    for k in range(len(tiles)):
                        apply(st, g, k, src(g, k), NR[:, g % 2, 0:cols])
                    st.settle()
                    names[f"{id}.rstd{g}"] = (vector_steps, st.n)

            Stage(tensor=tensor, scalar=scalar, vector=vector)

        NR = sb("NR", [P, 2, S])

        def split(id, tiles, hi, lo, ready=None):
            def scalar(act, st, e):
                for k, t in enumerate(tiles):
                    if ready is not None:
                        st.wait(ready(k))
                    st.do(nc.scalar.activation(hi[:, k, :], t, ACT.Copy), f"{id}.hi{k}")

            def vector(dve, st, e):
                st.settle()
                for k, t in enumerate(tiles):
                    st.wait(f"{id}.hi{k}")
                    st.do(nc.vector.tensor_tensor(lo[:, k, :], t, hi[:, k, :].bitcast(F32), ALU.subtract), f"{id}.lo{k}")
                names[f"{id}.ready"] = (vector_steps, st.n)
            Stage(scalar=scalar, vector=vector)

        def rmsnorm(id, gain, eps="eps6", src=None, hi=None, lo=None, cols=S, s0=0, out=None):
            src = [X[:, k, :] for k in range(KT)] if src is None else src
            hi, lo = (XH, XL) if hi is None else (hi, lo)
            if cols == S:
                sq = lambda i: T(s0 + i)
            else:
                v = A[:, s0:s0 + 4, :].rearrange("p a (b c) -> p (a b) c", c=cols)
                sq = lambda i: v[:, i, :]

            def apply(st, g, k, x, rstd):
                st.do(nc.vector.scalar_tensor_tensor(out=sq(k), in0=x, scalar=vec(gain, k), in1=rstd,
                                                     op0=ALU.mult, op1=ALU.mult), f"{id}.y{k}")
            colnorm(id, [src], D, eps, False, apply, sq, None, cols=cols)
            if out is None:
                split(id, [sq(k) for k in range(KT)], hi, lo, ready=lambda k: f"{id}.y{k}")

        def layernorm(id, gain, bias, split_it=True):
            def apply(st, g, k, x, rstd):
                st.do(nc.vector.scalar_tensor_tensor(out=X[:, k, :], in0=x, scalar=vec(gain, k), in1=rstd,
                                                     op0=ALU.mult, op1=ALU.mult))
                st.settle()
                st.do(nc.vector.tensor_scalar(X[:, k, :], X[:, k, :], vec(bias, k), None, ALU.add), f"{id}.y{k}")
            colnorm(id, [[X[:, k, :] for k in range(KT)]], D, "eps5", True, apply, lambda i: T(i), lambda i: T(8 + i))
            if split_it:
                split(id, [X[:, k, :] for k in range(KT)], XH, XL, ready=lambda k: f"{id}.y{k}")

        class Attention:

            def __init__(self, id, heads, keys, score, value, outd, dst, comps=1, scale=1.0, ptile=0, nkeys=4, lam=None, nsub=1, prob=None, pt=None):
                self.id, self.heads, self.keys, self.score, self.value, self.outd, self.dst = id, heads, keys, score, value, outd, dst
                self.comps, self.scale, self.nkeys, self.lam, self.nsub = comps, scale, nkeys, lam, nsub
                self.ptiles = (lambda n: A[:, ptile + n, :]) if prob is None else prob
                self.pt0 = ptile + 8 if pt is None else pt
                self.e = evac[0]
                PLAN.append(self)

            def prob(self, n, i):
                return self.ptiles(4 * (n % (2 * self.comps)) + i)[:, 0:self.keys(i) * P]

            def ptile(self, j, lo, hi):
                return A[:, self.pt0 + j, lo:hi]

            def tensor(self, pe, st):
                pe.wait_ge(banks_free, 4 + self.e)
                st.wait(*[self.id + ".in"] * (self.id + ".in" in names))
                n = self.heads * self.comps
                for m in range(n + 1):
                    if m < n:
                        for i in range(TT):
                            if m >= 1:
                                st.wait(f"{self.id}.exp{m - 1}.{i}")
                            last = self.score(m // self.comps, m % self.comps, i, bank(i, self.keys(i) * P))
                            st.do(last, f"{self.id}.sc{m}.{i}")
                    if m >= 1 and m % self.comps == 0:
                        h = m // self.comps - 1
                        for i in range(TT):
                            st.wait(f"{self.id}.prob{h}.{i}")
                            if i >= 2:
                                st.wait(f"{self.id}.pt{h}.{i - 2}")
                            elif h >= 1:
                                st.wait(f"{self.id}.pt{h - 1}.{i + 2}")
                            for j in range(self.keys(i)):
                                last = nc.tensor.transpose(PS[:, 4 + i % 2, j * P:(j + 1) * P],
                                                           self.ptiles(4 * (self.comps * (h % 2)) + i)[:, j * P:(j + 1) * P], ident)
                            st.do(last, f"{self.id}.tr{h}.{i}")
                        for i in range(TT):
                            st.wait(f"{self.id}.pt{h}.{i}")
                        for s in range(self.nsub):
                            ob = 6 + (h * self.nsub + s) % 2
                            if h * self.nsub + s >= 2:
                                q = h * self.nsub + s - 2
                                st.wait(f"{self.id}.o{q // self.nsub}.{q % self.nsub}")
                            base, rows = self.outd(h)
                            for j in range(self.nkeys):
                                c0 = j * P if self.nkeys == TT and self.keys(0) == 1 else 0
                                last = mm(PS[base:base + rows, ob, c0:S], self.value(h, j, s), self.ptile(j, c0, S),
                                          start=(j == 0), stop=(j == self.nkeys - 1))
                            st.do(last, f"{self.id}.pv{h}.{s}")

            def scalar(self, act, st):
                st.settle()
                n = self.heads * self.comps
                for m in range(n + 1):
                    if m < n:
                        for i in range(TT):
                            st.wait(f"{self.id}.max{m}.{i}")
                            if m >= 2 * self.comps:
                                st.wait(f"{self.id}.tr{m // self.comps - 2}.{i}")
                            st.do(nc.scalar.activation(self.prob(m, i), bank(i, self.keys(i) * P), ACT.Exp,
                                                       bias=SM[:, (m % 2) * 4 + i:(m % 2) * 4 + i + 1], scale=self.scale,
                                                       accum_out=SM[:, 8 + (m % 2) * 4 + i:9 + (m % 2) * 4 + i]), f"{self.id}.exp{m}.{i}")
                    if m >= 1 and m % self.comps == 0:
                        h = m // self.comps - 1
                        for i in range(TT):
                            st.wait(f"{self.id}.tr{h}.{i}")
                            if h >= 1 and i == 0:
                                for s in range(self.nsub):
                                    st.wait(f"{self.id}.pv{h - 1}.{s}")
                            kk = self.keys(i)
                            st.do(nc.scalar.activation(A[:, self.pt0:self.pt0 + kk, i * P:(i + 1) * P],
                                                       PS[:, 4 + i % 2, 0:kk * P].rearrange("p (a b) -> p a b", b=P), ACT.Copy),
                                  f"{self.id}.pt{h}.{i}")

            def vector(self, dve, st):
                st.settle()
                n = self.heads * self.comps
                for m in range(n + 1):
                    if m < n:
                        for i in range(TT):
                            st.wait(f"{self.id}.sc{m}.{i}")
                            mx = SM[:, (m % 2) * 4 + i:(m % 2) * 4 + i + 1]
                            st.settle()
                            st.do(nc.vector.tensor_reduce(mx, bank(i, self.keys(i) * P), AX.X, ALU.max, negate=True))
                            if self.scale != 1.0:
                                st.settle()
                                st.do(nc.vector.tensor_scalar(mx, mx, self.scale, None, ALU.mult))
                            names[f"{self.id}.max{m}.{i}"] = (vector_steps, st.n)
                        for i in range(TT):
                            st.wait(f"{self.id}.exp{m}.{i}")
                            c, h = m % self.comps, m // self.comps
                            s = SM[:, 8 + (m % 2) * 4 + i:9 + (m % 2) * 4 + i]
                            r = SM[:, 16 + (m % 2) * 4 + i:17 + (m % 2) * 4 + i]
                            st.settle()
                            st.do(nc.vector.reciprocal(r, s))
                            st.settle()
                            if self.comps == 1:
                                st.do(nc.vector.tensor_scalar(self.prob(m, i), self.prob(m, i), r, None, ALU.mult), f"{self.id}.prob{h}.{i}")
                            elif c == 0:
                                st.do(nc.vector.tensor_scalar(self.prob(m, i), self.prob(m, i), r, None, ALU.mult))
                            else:
                                st.do(nc.vector.tensor_scalar(self.prob(m, i), self.prob(m, i), r, self.lam, ALU.mult, ALU.mult))
                                st.settle()
                                st.do(nc.vector.tensor_tensor(self.prob(m - 1, i), self.prob(m - 1, i), self.prob(m, i), ALU.subtract),
                                      f"{self.id}.prob{h}.{i}")
                    if m >= 1 and m % self.comps == 0:
                        h = m // self.comps - 1
                        for s in range(self.nsub):
                            st.wait(f"{self.id}.pv{h}.{s}")
                            base, rows = self.outd(h)
                            ob = 6 + (h * self.nsub + s) % 2
                            st.do(nc.vector.tensor_copy(self.dst(h, s), PS[base:base + rows, ob, :]), f"{self.id}.o{h}.{s}")
                names[f"{self.id}.done"] = (vector_steps, st.n)

        def at(i):
            return lambda j: A[:, bass.ds(i + j, 1), :]

        def mark(name, engine="vector"):
            def f(eng, st, e):
                names[name] = (st.sem, st.n)
            Stage(**{engine: f})

        def free_until(*roles):
            def f(eng, st, e):
                eng.wait_ge(banks_free, 4 + e)
            Stage(**{r: f for r in roles})

        nload = [0]

        def dma(id, dst, src, ready=(), settle=True):
            k = nload[0]
            nload[0] += 1

            def f(act, st, e):
                act.wait_ge(banks_free, 4 + e)
                st.wait(*ready)
                act.dma_start(dst, src).then_inc(loads[k], 16)
                names[id] = (loads[k], 16)
            Stage(scalar=f)

        def vs(f):
            Stage(vector=lambda dve, st, e: (dve.wait_ge(banks_free, 4 + e), f(st)))

        def bcast(ap, n):
            return ap.to_broadcast([ap.shape[0], n])

        v, a_ = nc.vector, nc.scalar

        def xattn(l):
            KM = A[:, 20:24, :].rearrange("p a (b c) -> p (a b) c", c=MEM)
            Linear(f"x{l}.k", dst=lambda j: KM[:, bass.ds(j, 1), :], xh=MH, xl=ML, cols=MEM, ready=["mem.ready"], pre=[f"x{l}.clear"])
            TokenMajor(f"x{l}.v", 2, lambda h, t: T(24 + 2 * t + h), MH, ML, tiles=2)
            rmsnorm(f"xn{l}", f"norm_xattn{l}")
            Linear(f"x{l}.q", dst=at(12), ready=[f"xn{l}.ready"])

            def score(h, c, i, out):
                for d in range(2):
                    last = mm(out, T(12 + 2 * h + d)[:, i * P:(i + 1) * P], KM[:, 2 * h + d, :], start=(d == 0), stop=(d == 1))
                return last
            Attention(f"xa{l}", 4, lambda i: 2, score, lambda h, j, s: W2(24 + 2 * j, 2)[:, h * 256 + s * P:h * 256 + (s + 1) * P],
                      lambda h: (0, P), lambda h, s: T(28 + 2 * h + s), scale=1.0 / 16, nkeys=2, nsub=2)
            split(f"xo{l}", [T(28 + k) for k in range(KT)], XH, XL, ready=lambda k: f"xa{l}.o{k // 2}.{k % 2}")
            Linear(f"x{l}.o", add=True, ready=[f"xo{l}.ready"])

        def ffn(l, alpha=None):
            Pairs(f"f{l}.up", NH, at(0), ACT.Silu, ready=[f"fn{l}.ready"])
            Down(f"f{l}.down", alpha)

        dma("reset0", T(36), io["reset"])
        memt = A[:, 8:12, :].rearrange("p a (b c) -> p (a b) c", c=MEM)
        rmsnorm("mem", "mem_norm", src=[memt[:, k, :] for k in range(KT)], hi=MH, lo=ML, cols=MEM, s0=12)
        rmsnorm("n0", "norm_mix0")
        LB = 24

        def lower_bounds(st):
            r = [vec("lb", 4 * i, 4) for i in range(3)]
            m = SM[:, LB + 12:LB + 16]
            st.do(v.tensor_tensor(m, r[0], r[1], ALU.max))
            st.settle()
            st.do(v.tensor_tensor(m, m, r[2], ALU.max))
            st.settle()
            for i in range(3):
                st.do(v.tensor_tensor(SM[:, LB + 4 * i:LB + 4 * i + 4], r[i], m, ALU.subtract), "lb.centred")
        vs(lower_bounds)

        def lb_exp(act, st, e):
            st.wait("lb.centred")
            st.do(a_.activation(SM[:, LB:LB + 12], SM[:, LB:LB + 12], ACT.Exp), "lb.exp")
        Stage(scalar=lb_exp)

        def lb_ratio(st):
            st.wait("lb.exp")
            m = SM[:, LB + 12:LB + 16]
            st.do(v.tensor_tensor(m, SM[:, LB:LB + 4], SM[:, LB + 4:LB + 8], ALU.add))
            st.settle()
            st.do(v.tensor_tensor(m, m, SM[:, LB + 8:LB + 12], ALU.add))
            st.settle()
            st.do(v.reciprocal(m, m))
            st.settle()
            st.do(v.tensor_tensor(SM[:, LB:LB + 4], SM[:, LB:LB + 4], m, ALU.mult))
            st.settle()
            st.do(v.tensor_scalar(SM[:, LB + 4:LB + 8], SM[:, LB:LB + 4], -1.0, 1.0, ALU.mult, ALU.add))
        vs(lb_ratio)

        Pairs("l0.glu", 4, at(0), ACT.Sigmoid, of=1, ready=["n0.ready"])

        def depthwise(st, src, dst, taps, w, b, n):
            for k in range(n):
                x, y = src(k), dst(k)
                wk = lambda t: vec(w, k * taps + t)
                st.do(v.tensor_scalar(y, x, wk(taps - 1), vec(b, k) if b else 0.0, ALU.mult, ALU.add))
            for t in range(taps - 2, -1, -1):
                sh = taps - 1 - t
                st.settle()
                for k in range(n):
                    x, y = src(k), dst(k)
                    st.do(v.scalar_tensor_tensor(out=y[:, sh:], in0=x[:, :S - sh], scalar=vec(w, k * taps + t),
                                                 in1=y[:, sh:], op0=ALU.mult, op1=ALU.add))
        vs(lambda st: depthwise(st, lambda k: T(k), lambda k: T(4 + k), 31, "conv_dw_w", "conv_dw_b", 4))
        Linear("l0.q", dst=at(8), func=ACT.Silu)
        Linear("l0.f", dst=at(12), func=ACT.Sigmoid)
        Linear("l0.i", dst=at(16))
        Linear("l0.g", dst=at(20), func=ACT.Silu)

        def h_gates(st):
            st.settle()
            for h in range(4):
                st.do(v.tensor_scalar(T(12 + h), T(12 + h), SM[:, LB + 4 + h:LB + 5 + h], SM[:, LB + h:LB + h + 1], ALU.mult, ALU.add))
            st.settle()
            st.do(v.tensor_scalar(W2(32, 4), W2(12, 4), -1.0, 1.0, ALU.mult, ALU.add), "h.f")
        vs(h_gates)

        def h_ln(act, st, e):
            st.wait("h.f")
            st.do(a_.activation(W2(12, 4), W2(12, 4), ACT.Ln), "h.ln")
        Stage(scalar=h_ln)
        chunks = lambda i, n: W2(i, n).rearrange("p (c t) -> p c t", t=64)

        def h_cum(st):
            st.wait("h.ln", "reset0")
            for h in range(4):
                st.do(v.tensor_tensor_scan(T(24 + h), T(36), T(12 + h), 0.0, ALU.mult, ALU.add), "h.cum")
            st.settle()
            last = chunks(24, 4)[:, :, 63:64].to_broadcast([P, 32, 64])
            st.do(v.tensor_tensor(chunks(0, 4), last, chunks(24, 4), ALU.subtract), "h.kd")
            st.do(v.memset(W2(12, 4), 0.0))
        vs(h_cum)

        def h_exps(act, st, e):
            st.wait("h.cum")
            st.do(a_.activation(W2(28, 4), W2(24, 4), ACT.Exp), "h.e")
            st.wait("h.kd")
            st.do(a_.activation(W2(0, 4), W2(0, 4), ACT.Exp), "h.ekd")
            st.settle()
            st.do(a_.activation(W2(24, 4), W2(24, 4), ACT.Exp, scale=-1.0), "h.en")
        Stage(scalar=h_exps)
        DEC = 48

        def h_scaled(st):
            st.wait("h.e")
            st.do(v.tensor_copy(SM[:, DEC:DEC + 32].rearrange("p (a b) -> p a b", b=1), chunks(28, 4)[:, :, 63:64]))
            st.do(v.tensor_tensor(W2(8, 4), W2(8, 4), W2(28, 4), ALU.mult))
            st.wait("h.ekd")
            st.do(v.tensor_tensor(W2(0, 4), W2(0, 4), W2(32, 4), ALU.mult))
            st.wait("h.en")
            st.settle()
            st.do(v.tensor_tensor(W2(32, 4), W2(32, 4), W2(24, 4), ALU.mult), "h.scaled")
        vs(h_scaled)

        def h_turn_pe(pe, st, e):
            st.wait("h.scaled")
            for n in range(8):
                h, src = n // 2, (16, 0)[n % 2]
                if n >= 2:
                    st.wait(f"h.turned{n - 2}")
                for t in range(TT):
                    last = nc.tensor.transpose(PS[:, n % 2, t * P:(t + 1) * P], T(src + h)[:, t * P:(t + 1) * P], ident)
                st.do(last, f"h.turn{n}")

        def h_turn_act(act, st, e):
            for n in range(8):
                st.wait(f"h.turn{n}")
                st.do(a_.activation(T((28, 24)[n % 2] + n // 2), bank(n % 2), ACT.Copy), f"h.turned{n}")
        Stage(tensor=h_turn_pe, scalar=h_turn_act)

        def h_pe(pe, st, e):
            def inner(h):
                if h >= 2:
                    st.wait(f"h.att{h - 2}")
                elif h == 0:
                    st.wait("h.turned7")
                for t in range(TT):
                    c = slice(t * P, (t + 1) * P)
                    last = mm(PS[:, h % 2, c], T(32 + h)[:, c], T(8 + h)[:, c], start=True, stop=True)
                st.do(last, f"h.qk{h}")
                if h >= 2:
                    st.wait(f"h.state{h - 2}")
                for c in range(8):
                    b, t = 64 * (c % 2), c // 2
                    last = mm(PS[:, 2 + 2 * (h % 2) + c % 2, (c // 2) * P:(c // 2 + 1) * P], A[b:b + 64, 24 + h, t * P:(t + 1) * P],
                              A[b:b + 64, 28 + h, t * P:(t + 1) * P], start=True, stop=True)
                st.do(last, f"h.kv{h}")

            def outer(h):
                st.wait(f"h.att{h}", f"h.state{h}")
                if h >= 2:
                    st.wait(f"h.out{h - 2}")
                for t in range(TT):
                    c = slice(t * P, (t + 1) * P)
                    last = mm(PS[:, 6 + h % 2, c], T(28 + h)[:, c], T(12 + h)[:, c], start=True, stop=(t == 0 and False))
                    for q in range(2):
                        n = 2 * t + q
                        if n:
                            last = mm(PS[:, 6 + h % 2, n * 64:(n + 1) * 64], W2(2 * (h % 2), 2)[:, n * P:(n + 1) * P],
                                      T(8 + h)[:, n * 64:(n + 1) * 64], start=False, stop=(q == 1))
                st.do(last, f"h.o{h}")
            inner(0)
            for h in range(4):
                if h < 3:
                    inner(h + 1)
                outer(h)

        def h_vec(dve, st, e):
            for h in range(4):
                st.wait(f"h.qk{h}")
                for t in range(TT):
                    c = slice(t * P, (t + 1) * P)
                    st.do(v.copy_predicated(T(12 + h)[:, c], cst("chunkT").bitcast(U32), PS[:, h % 2, c]), f"h.att{h}")
                st.wait(f"h.kv{h}")
                if h >= 2:
                    st.wait(f"h.o{h - 2}")
                S2 = W2(2 * (h % 2), 2)
                kv = lambda c: PS[:, 2 + 2 * (h % 2) + c % 2, (c // 2) * P:(c // 2 + 1) * P]
                st.settle()
                st.do(v.tensor_copy(S2[:, P:2 * P], kv(0)))
                for c in range(1, 7):
                    st.settle()
                    st.do(v.scalar_tensor_tensor(out=S2[:, (c + 1) * P:(c + 2) * P], in0=S2[:, c * P:(c + 1) * P],
                                                 scalar=SM[:, DEC + 8 * h + c:DEC + 8 * h + c + 1], in1=kv(c),
                                                 op0=ALU.mult, op1=ALU.add))
                names[f"h.state{h}"] = (vector_steps, st.n)

        def h_act(act, st, e):
            for h in range(4):
                st.wait(f"h.o{h}")
                st.do(a_.activation(T(16 + h), bank(6 + h % 2), ACT.Copy), f"h.out{h}")
        Stage(tensor=h_pe, vector=h_vec, scalar=h_act)
        mark("ho.in", "scalar")

        def h_apply(st, g, k, x, rstd):
            st.do(v.scalar_tensor_tensor(out=x, in0=x, scalar=vec("hgrn_out_norm", g), in1=rstd, op0=ALU.mult, op1=ALU.mult))
            st.settle()
            st.do(v.tensor_tensor(x, x, T(20 + g), ALU.mult), f"y0.{g}")
        colnorm("ho", [[T(16 + h)] for h in range(4)], P, "eps6", False, h_apply, lambda i: T(24 + i), None)

        def c_apply(st, g, k, x, rstd):
            st.do(v.scalar_tensor_tensor(out=x, in0=x, scalar=vec("conv_ln_g", k), in1=rstd, op0=ALU.mult, op1=ALU.mult), f"cl.y{k}")
        colnorm("cl", [[T(4 + k) for k in range(4)]], 512, "eps6", True, c_apply, lambda i: T(24 + i), lambda i: T(8 + i), b0=0)

        def c_silu(act, st, e):
            for k in range(4):
                st.wait(f"cl.y{k}")
                st.do(a_.activation(T(8 + k), T(8 + k), ACT.Silu, bias=vec("conv_ln_b", k)), f"y0.{4 + k}")
        Stage(scalar=c_silu)
        split("y0", [T(16 + k) for k in range(4)] + [T(8 + k) for k in range(4)], XH, XL, ready=lambda k: f"y0.{k}")
        mark("x0.clear", "vector")
        Linear("l0.out", add=True, ready=["y0.ready"])
        xattn(0)
        rmsnorm("fn0", "norm_ffn0")
        ffn(0)

        rmsnorm("n1", "norm_mix1", s0=24)
        dma("sgu_w", T(36), io["sguw"])
        dma("sgu_b", T(37)[0:1, :], io["sgub"])
        Linear("l1.qk", dst=at(12), ready=["n1.ready"], pre=["n1.ready"])
        TokenMajor("l1.v", 1, lambda h, t: T(20 + t))
        Linear("l1.uz", dst=at(24), func=ACT.Gelu)

        def causal_score(q0, k0):
            def score(h, c, i, out):
                b = 64 * (h % 2)
                mm(out, A[b:b + 64, q0 + h // 2, i * P:(i + 1) * P], A[b:b + 64, k0 + h // 2, 0:(i + 1) * P], start=True, stop=False)
                return mm(out[:, i * P:(i + 1) * P], ident, cst("cadd"), start=False, stop=True)
            return score
        Attention("moba", 8, lambda i: i + 1, causal_score(12, 16), lambda h, j, s: T(20 + j)[:, h * 64:(h + 1) * 64],
                  lambda h: (64 * (h % 2), 64), lambda h, s: A[64 * (h % 2):64 * (h % 2) + 64, 32 + h // 2, :], scale=0.125)

        def z_apply(st, g, k, x, rstd):
            st.do(v.scalar_tensor_tensor(out=x, in0=x, scalar=vec("sgu_ln_g", g), in1=rstd, op0=ALU.mult, op1=ALU.mult))
            st.settle()
            st.do(v.tensor_scalar(x, x, vec("sgu_ln_b", g), None, ALU.add), f"z.{g}")
        colnorm("zn", [[T(28 + g)] for g in range(4)], P, "eps6", True, z_apply, lambda i: T(16 + i), lambda i: T(12 + i), b0=0)

        def sgu_mask(st):
            st.wait("sgu_w")
            for g in range(4):
                st.do(v.tensor_tensor(T(36)[:, g * P:(g + 1) * P], T(36)[:, g * P:(g + 1) * P], cst("causalT"), ALU.mult), "sgu.w")
        vs(sgu_mask)

        def sgu_pe(pe, st, e):
            for g in range(4):
                st.wait(f"z.{g}")
                if g >= 2:
                    st.wait(f"z.copied{g - 2}")
                for t in range(TT):
                    last = nc.tensor.transpose(PS[:, 4 + g % 2, t * P:(t + 1) * P], T(12 + g)[:, t * P:(t + 1) * P], ident)
                st.do(last, f"z.turned{g}")
            st.wait("sgu.w", "sgu_b")
            for g in range(4):
                st.wait(f"z.copied{g}")
                if g >= 2:
                    st.wait(f"z.mixed{g - 2}")
                for t in range(TT):
                    o = PS[:, 6 + g % 2, t * P:(t + 1) * P]
                    mm(o, T(16 + g)[:, t * P:(t + 1) * P], T(36)[:, g * P:(g + 1) * P], start=True, stop=False)
                    last = mm(o, ones[0:1, :], T(37)[0:1, g * P:(g + 1) * P], start=False, stop=True)
                st.do(last, f"z.mix{g}")

        def sgu_act(act, st, e):
            for g in range(4):
                st.wait(f"z.turned{g}")
                st.do(a_.activation(T(16 + g), bank(4 + g % 2), ACT.Copy), f"z.copied{g}")

        def sgu_dve(dve, st, e):
            for g in range(4):
                st.wait(f"z.mix{g}")
                st.do(v.tensor_tensor(T(24 + g), T(24 + g), bank(6 + g % 2), ALU.mult), f"z.mixed{g}")
        Stage(tensor=sgu_pe, scalar=sgu_act, vector=sgu_dve)
        split("y1", [T(32 + k) for k in range(4)] + [T(24 + k) for k in range(4)], XH, XL,
              ready=lambda k: "moba.done" if k < 4 else f"z.mixed{k - 4}")
        mark("x1.clear", "vector")
        Linear("l1.out", add=True, ready=["y1.ready"])
        xattn(1)
        rmsnorm("fn1", "norm_ffn1")
        ffn(1)

        def to_residual(gain):
            def apply(st, g, k, x, rstd):
                st.do(v.scalar_tensor_tensor(out=X[:, k, :], in0=x, scalar=vec(gain, k), in1=rstd, op0=ALU.mult, op1=ALU.mult), "res")
            return apply
        allx = [X[:, k, :] for k in range(KT)]
        colnorm("end1", [allx], D, "eps6", False, to_residual("final_norm"), lambda i: T(24 + i), None)
        mark("li.in", "vector")

        layernorm("li", "ln_in_g", "ln_in_b")
        mark("li.done", "vector")
        dma("spill", io["spill"], X[:], ready=["li.done"])
        dma("onehot", T(30)[0:32, 0:384], io["onehot"], ready=["li.done"])
        dma("rel", T(31)[0:32, 0:4], io["rel"])
        dma("lamv", T(29)[:, 0:256], io["lam"])
        Linear("s.q", dst=at(12), ready=["li.ready"], pre=["li.ready"], scale=0.125)
        Linear("s.k", dst=at(16))
        TokenMajor("s.v", 1, lambda h, t: T(20 + t))

        def t5_pe(pe, st, e):
            st.wait("onehot", "rel")
            pe.wait_ge(banks_free, 4 + e)
            st.do(mm(PS[0:4, 0, 0:384], T(31)[0:32, 0:4], T(30)[0:32, 0:384], start=True, stop=True), "t5.g")

        def t5_act(act, st, e):
            st.wait("t5.g")
            st.do(a_.activation(T(28)[0:4, 0:384], PS[0:4, 0, 0:384], ACT.Copy), "t5.row")
        Stage(tensor=t5_pe, scalar=t5_act)
        dma("t5.out", TAB, T(28)[0:4, 0:384], ready=["t5.row"])
        BT = W2(36, 2).rearrange("p (h c) -> p h c", h=4)
        dma("t5.in", BT, bass.AP(tensor=TAB.tensor, offset=0, ap=[[1, P], [384, 4], [1, 256]]), ready=["t5.out"])

        def t5_mask(st):
            st.wait("t5.in")
            for h in range(4):
                st.do(v.tensor_tensor(BT[:, h, P:2 * P], BT[:, h, P:2 * P], cst("caddR"), ALU.add), "t5.masked")
        LAM = 40

        def lam_dots(st):
            st.wait("lamv")
            st.do(v.tensor_tensor(T(29)[:, 256:384].rearrange("p (a b) -> p a b", b=64), T(29)[:, 0:256].rearrange("p (a c b) -> p a c b", c=2, b=64)[:, :, 0, :],
                                  T(29)[:, 0:256].rearrange("p (a c b) -> p a c b", c=2, b=64)[:, :, 1, :], ALU.mult))
            st.settle()
            st.do(v.tensor_reduce(SM[:, LAM:LAM + 2], T(29)[:, 256:384].rearrange("p (a b) -> p a b", b=64), AX.X, ALU.add), "lam.dots")
        vs(lam_dots)

        def lam_exp(act, st, e):
            st.wait("lam.dots")
            st.do(a_.activation(SM[:, LAM:LAM + 2], SM[:, LAM:LAM + 2], ACT.Exp), "lam.exp")
        Stage(scalar=lam_exp)

        def lam_diff(st):
            st.wait("lam.exp")
            st.do(v.tensor_tensor(SM[:, LAM + 2:LAM + 3], SM[:, LAM:LAM + 1], SM[:, LAM + 1:LAM + 2], ALU.subtract))
            st.settle()
            st.do(v.tensor_scalar(SM[:, LAM + 2:LAM + 3], SM[:, LAM + 2:LAM + 3], LAMBDA0, None, ALU.add))
            st.do(v.tensor_scalar(SM[:, LAM + 3:LAM + 4], vec("subln_g"), 1.0 - LAMBDA0, None, ALU.mult))
            t5_mask(st)
        vs(lam_diff)
        mark("diff.in", "vector")

        def diff_score(h, c, i, out):
            b = 64 * c
            mm(out, A[b:b + 64, 12 + h, i * P:(i + 1) * P], A[b:b + 64, 16 + h, 0:(i + 1) * P], start=True, stop=False)
            if i >= 2:
                mm(out[:, 0:(i - 1) * P], bcast(ident[0:32, 31:32], P), bcast(T(31)[0:32, h:h + 1], (i - 1) * P), start=False, stop=False)
            if i == 0:
                return mm(out, cst("flip"), BT[:, h, P:2 * P], start=False, stop=True)
            return mm(out[:, (i - 1) * P:(i + 1) * P], cst("flip"), BT[:, h, :], start=False, stop=True)
        Stage(scalar=lambda act, st, e: st.wait("spill"))
        Attention("diff", 4, lambda i: i + 1, diff_score, lambda h, j, s: T(20 + j)[:, h * P:(h + 1) * P],
                  lambda h: (0, P), lambda h, s: T(32 + h), comps=2, prob=lambda n: A[:, n, :] if n < 8 else X[:, n - 8, :], pt=8, lam=SM[:, LAM + 2:LAM + 3])
        mark("dn.in", "vector")

        def d_apply(st, g, k, x, rstd):
            st.do(v.scalar_tensor_tensor(out=x, in0=x, scalar=SM[:, LAM + 3:LAM + 4], in1=rstd, op0=ALU.mult, op1=ALU.mult), f"ya.{g}")
        colnorm("dn", [[T(32 + h)] for h in range(4)], P, "eps5", False, d_apply, lambda i: T(24 + i), None)
        split("ya", [T(32 + k) for k in range(4)], YH, YL, ready=lambda k: f"ya.{k}")

        mark("rw.clear", "vector")
        dma("lora", W2(36, 2), io["lora"], ready=["rw.clear"])
        dma("reset1", T(35), io["reset"], ready=["rw.clear"])
        Linear("s.rwkv", dst=at(0), pre=["rw.clear"])
        OM, DCY = 96, 64

        def rw_shift(st):
            st.do(v.tensor_tensor(A[:, 14:28, 1:S], A[:, 0:14, 0:S - 1], A[:, 0:14, 1:S], ALU.subtract))
            st.do(v.tensor_scalar(A[:, 14:28, 0:1], A[:, 0:14, 0:1], -1.0, None, ALU.mult))
            st.settle()
            for k in (12, 13, *range(12)):
                st.do(v.scalar_tensor_tensor(out=T(k), in0=T(14 + k), scalar=vec("mu", k), in1=T(k), op0=ALU.mult, op1=ALU.add), f"rw.p{k}")
            st.do(v.tensor_scalar(SM[:, OM:OM + 4], vec("k_a", 0, 4), -1.0, 1.0, ALU.mult, ALU.add))
            st.settle()
            for j in range(4):
                st.do(v.tensor_scalar(T(30 + j), T(4 + j), vec("k_k", j), None, ALU.mult), f"rw.kk{j}")
        vs(rw_shift)

        def rw_lora_act(act, st, e):
            st.wait("rw.p12")
            st.do(a_.activation(A[0:64, 12, :], A[0:64, 12, :], ACT.Tanh), "rw.tanh")
            st.wait("rw.p13")
            st.do(a_.activation(T(13), T(13), ACT.Sigmoid))
            st.wait("rw.kk3")
            for j in range(4):
                st.wait(f"rw.zmm{j}")
                st.do(a_.activation(T(14 + j), bank(j), ACT.Sigmoid, bias=vec("w0", j)), f"rw.w{j}")
            for j in range(4):
                st.wait(f"rw.amm{j}")
                st.do(a_.activation(T(18 + j), bank(4 + j), ACT.Sigmoid, bias=vec("a0", j)), f"rw.a{j}")
            for j in range(4):
                st.do(a_.activation(T(22 + j), T(30 + j), ACT.Square), f"rw.sq{j}")
            st.wait("rw.kmax")
            st.do(a_.activation(W2(22, 4), W2(22, 4), ACT.Sqrt), "rw.knorm")

        def rw_lora_pe(pe, st, e):
            st.wait("lora", "rw.tanh")
            for j in range(4):
                st.do(mm(bank(j), A[0:64, 36, j * P:(j + 1) * P], A[0:64, 12, :], start=True, stop=True), f"rw.zmm{j}")
            for j in range(4):
                st.do(mm(bank(4 + j), A[64:128, 36, j * P:(j + 1) * P], A[64:128, 12, :], start=True, stop=True), f"rw.amm{j}")
            for j in range(4):
                st.wait(f"rw.w{j}", f"rw.sq{j}")
                st.do(mm(bank(j), ones64, T(22 + j), start=True, stop=True), f"rw.ksum{j}")
            for j in range(4):
                st.wait(f"rw.rk{j}")
                st.do(mm(bank(4 + j), ones64, T(34 + j), start=True, stop=True), f"rw.rksum{j}")

        def rw_keys(dve, st, e):
            st.wait("rw.w3", "reset1")
            st.do(v.tensor_scalar(W2(14, 4), W2(14, 4), -math.exp(-0.5), None, ALU.mult))
            st.settle()
            for j in range(4):
                st.do(v.tensor_tensor_scan(T(26 + j), T(35), T(14 + j), 0.0, ALU.mult, ALU.add))
            st.settle()
            for j in range(4):
                st.wait(f"rw.ksum{j}")
                st.do(v.tensor_scalar(T(22 + j), bank(j), 1e-24, None, ALU.max), "rw.kmax")
            st.wait("rw.a3", "rw.amm3")
            for j in range(4):
                st.do(v.tensor_scalar(T(34 + j), T(18 + j), vec("k_a", j), SM[:, OM + j:OM + j + 1], ALU.mult, ALU.add))
            st.settle()
            st.do(v.tensor_tensor(W2(4, 4), W2(4, 4), W2(34, 4), ALU.mult))
            st.settle()
            for j in range(4):
                st.do(v.scalar_tensor_tensor(out=T(34 + j), in0=T(j), scalar=vec("r_k", j), in1=T(4 + j), op0=ALU.mult, op1=ALU.mult), f"rw.rk{j}")
            st.wait("rw.knorm")
            st.do(v.reciprocal(W2(22, 4), W2(22, 4)))
            st.settle()
            st.do(v.tensor_tensor(W2(30, 4), W2(30, 4), W2(22, 4), ALU.mult))
            st.settle()
            st.do(v.tensor_tensor(W2(18, 4), W2(18, 4), W2(30, 4), ALU.mult))
            for j in range(4):
                st.wait(f"rw.rksum{j}")
                st.do(v.tensor_tensor(T(34 + j), T(8 + j), bank(4 + j), ALU.mult))
        Stage(tensor=rw_lora_pe, scalar=rw_lora_act, vector=rw_keys)

        ARS = (22, 24, 14, 16)
        AR = [W2(s, 2).rearrange("p (t w c) -> p t w c", t=TT, w=2) for s in ARS]
        t4 = lambda ap: ap.rearrange("p (t c) -> p t c", c=P)
        c64 = lambda ap: ap.rearrange("p (t c) -> p t c", c=64)

        def p1_act(act, st, e):
            for j in range(4):
                st.wait(f"p1.d{j}")
                st.do(a_.activation(SG[:, 0, :], T(26 + j), ACT.Exp))
                st.do(a_.activation(SG[:, 1, :], SG[:, 1, :], ACT.Exp))
                st.do(a_.activation(SG[:, 2, :], T(26 + j), ACT.Exp, scale=-1.0))
                st.do(a_.activation(SG[:, 3, :], SG[:, 3, :], ACT.Exp), f"p1.e{j}")

        def p1_dve(dve, st, e):
            for j in range(4):
                st.settle()
                st.do(v.tensor_tensor(SG[:, 1, :], T(26 + j), T(14 + j), ALU.subtract))
                st.do(v.tensor_tensor(c64(SG[:, 3, :]), c64(T(26 + j))[:, :, 63:64].to_broadcast([P, 8, 64]), c64(T(26 + j)), ALU.subtract), f"p1.d{j}")
                st.wait(f"p1.e{j}")
                st.settle()
                st.do(v.tensor_copy(SM[:, DCY + 8 * j:DCY + 8 * j + 8].rearrange("p (a b) -> p a b", b=1), c64(SG[:, 0, :])[:, :, 63:64]))
                st.do(v.scalar_tensor_tensor(out=AR[j][:, :, 0, :], in0=t4(T(30 + j)), scalar=-1.0, in1=t4(SG[:, 1, :]), op0=ALU.mult, op1=ALU.mult))
                st.do(v.tensor_tensor(AR[j][:, :, 1, :], t4(T(j)), t4(SG[:, 0, :]), ALU.mult))
                st.settle()
                st.do(v.tensor_tensor(T(j), T(18 + j), SG[:, 2, :], ALU.mult))
                st.do(v.tensor_tensor(T(30 + j), T(4 + j), SG[:, 2, :], ALU.mult))
                st.settle()
                st.do(v.tensor_tensor(T(18 + j), T(18 + j), SG[:, 3, :], ALU.mult))
                st.do(v.tensor_tensor(T(4 + j), T(4 + j), SG[:, 3, :], ALU.mult))
            st.do(v.memset(T(12), 0.0))
            st.wait("spill")
            st.do(v.memset(X[:, 4, 0:1], 0.0), "p1.done")
        Stage(scalar=p1_act, vector=p1_dve)

        TURN = [s + j for s in (8, 4, 18) for j in range(4)]

        def p1_turn_pe(pe, st, e):
            st.wait("p1.done")
            for n, k in enumerate(TURN):
                if n >= 4:
                    st.wait(f"p1.turned{n - 4}")
                for t in range(TT):
                    last = nc.tensor.transpose(PS[:, n % 4, t * P:(t + 1) * P], T(k)[:, t * P:(t + 1) * P], ident)
                st.do(last, f"p1.turn{n}")

        def p1_turn_act(act, st, e):
            for n, k in enumerate(TURN):
                st.wait(f"p1.turn{n}")
                st.do(a_.activation(T(k), bank(n % 4), ACT.Copy), f"p1.turned{n}")
        Stage(tensor=p1_turn_pe, scalar=p1_turn_act)

        RHS = X[:, 4:8, :].rearrange("p a b -> p (a b)").rearrange("p (h c) -> p h c", h=8)
        RB = X[:, 0:4, :].rearrange("p a b -> p (a b)").rearrange("p (h w c) -> p h w c", h=8, w=2)
        h4 = lambda ap: ap.rearrange("p (h c) -> p h c", h=4)
        two = lambda b, **k: PS[:, b:b + 2, :].rearrange("p a b -> p (a b)")
        G0, G1, G2, G3 = (SG[:, i, :] for i in range(4))
        AT = NR[:, 0, :]
        UT = NR[:, 1, :].rearrange("p (h c) -> p h c", h=8)
        ST = [T(12)[:, 0:256], T(12)[:, 256:512], SD[:, 0:256]]
        p4 = lambda ap: ap.rearrange("p (j c) -> p j c", j=4)
        m4 = lambda name: cst(name).rearrange("p (a c) -> p a c", a=1).to_broadcast([P, 4, P])

        def blk(t4_, h):
            return t4_[:, h * P:(h + 1) * P]

        def slot(h):
            return 4 * (h % 2) + h // 2

        def heads_of(g):
            return [4 * g, 4 * g + 2, 4 * g + 1, 4 * g + 3]

        def quad(ap, g):
            return ap.rearrange("p (w j) c -> p w j c", w=2)[:, :, 2 * g:2 * g + 2, :]

        q4 = lambda ap: ap.rearrange("p (w j c) -> p w j c", w=2, j=2)
        mq = lambda name: cst(name).rearrange("p (a b c) -> p a b c", a=1, b=1).to_broadcast([P, 2, 2, P])
        scores = PS[:, 0:7:6, 0:256].rearrange("p w (j c) -> p w j c", j=2)

        def solve_pe(st, t, g):
            i = f"r{t}.{g}"
            heads = heads_of(g)
            prev = f"r{t}.0" if g else (f"r{t - 1}.1" if t else None)
            if prev:
                st.wait(f"{prev}.at")
            if g == 0 and t:
                st.wait(f"y{t - 1}")
            st.wait("p1.turned11")
            for n, h in enumerate(heads):
                j, b = h // 2, 64 * (h % 2)
                c = slice(t * P, (t + 1) * P)
                mm(PS[:, 6 * (h % 2), (n % 2) * P:(n % 2 + 1) * P], AR[j][b:b + 64, t, 0, :], T(j)[b:b + 64, c], start=True, stop=True)
                mm(PS[:, 1 + n // 2, (n % 2) * 256:(n % 2 + 1) * 256], T(j)[b:b + 64, c], AR[j][b:b + 64, t, :, :].rearrange("p w c -> p (w c)"), start=True, stop=True)
                last = mm(PS[:, 3 + n // 2, (n % 2) * 256:(n % 2 + 1) * 256], T(30 + j)[b:b + 64, c], AR[j][b:b + 64, t, :, :].rearrange("p w c -> p (w c)"), start=True, stop=True)
            for q in range(2):
                last = nc.tensor.transpose(PS[:, 5, 256 + q * P:256 + (q + 1) * P], AR[2 * g + q][:, t, 0, :], ident)
            st.do(last, i + ".scores")
            st.wait(i + ".masked")
            for n, h in enumerate(heads):
                j, b = h // 2, 64 * (h % 2)
                last = mm(PS[:, 5, n * 64:(n + 1) * 64], blk(G2, n), T(8 + j)[:, t * P + b:t * P + b + 64], start=True, stop=True)
            st.do(last, i + ".w")

            def product(b, L, R, name, wait=None):
                if wait:
                    st.wait(i + wait)
                for n in range(4):
                    last = mm(PS[:, b, n * P:(n + 1) * P], L(n), R(n), start=True, stop=True)
                st.do(last, i + name)

            def apply(b, L, name, *waits):
                st.wait(*[i + w for w in waits])
                for n in range(4):
                    last = mm(PS[:, b + n // 2, (n % 2) * 256:(n % 2 + 1) * 256], blk(L, n), RHS[:, slot(heads[n]), :], start=True, stop=True)
                st.do(last, i + name)
            product(0, lambda n: blk(G1, n), lambda n: blk(G0, n), ".d2")
            product(1, lambda n: blk(G0, n), lambda n: blk(G1, n), ".d2t")
            apply(3, G1, ".a1", ".rhs")
            product(0, lambda n: blk(G3, n), lambda n: blk(G2, n), ".d4", ".d2t_")
            product(1, lambda n: blk(G2, n), lambda n: blk(G3, n), ".d4t")
            apply(6, G3, ".a2", ".r1")
            product(0, lambda n: blk(G0, n), lambda n: blk(G1, n), ".d8t", ".d4t_")
            apply(3, G1, ".a4", ".r2")
            apply(6, G2, ".a8", ".r4", ".d8t_")
            st.wait(i + ".r8")
            for n in range(4):
                last = nc.tensor.transpose(PS[:, 0, n * P:(n + 1) * P], RHS[:, slot(heads[n]), P:2 * P], ident)
            st.do(last, i + ".mt")
            product(1, lambda n: RHS[:, slot(heads[n]), P:2 * P], lambda n: blk(G0, n), ".m2t", ".mt_")
            st.wait(i + ".m2t_")
            for n in range(4):
                last = mm(PS[:, 3, n * P:(n + 1) * P], blk(G1, n), RHS[:, slot(heads[n]), 0:P], start=True, stop=True)
            st.do(last, i + ".b2")
            st.wait(i + ".q2")
            for n in range(4):
                last = mm(PS[:, 4, n * P:(n + 1) * P], blk(G0, n), RHS[:, slot(heads[n]), 0:P], start=True, stop=True)
            st.do(last, i + ".b1")
            st.wait(i + ".q1")
            for h in heads:
                o, q = 64 * (h % 2), h // 2 - 2 * g
                last = mm(PS[o:o + 64, 0, q * P:(q + 1) * P], RHS[:, slot(h), 0:64], ident, start=True, stop=True)
            st.do(last, i + ".turn")

        def solve_act(st, t, g):
            i = f"r{t}.{g}"
            R4 = quad(RHS, g)
            st.wait(i + ".masked", i + ".w")
            st.do(a_.activation(R4[:, :, :, 0:64], PS[:, 5, 256:512].rearrange("p (j w c) -> p w j c", j=2, w=2), ACT.Copy))
            st.do(a_.activation(R4[:, :, :, 64:P], q4(PS[:, 5, 0:256]), ACT.Copy), i + ".rhs")
            st.wait(i + ".d2")
            st.do(a_.activation(G2, bank(0), ACT.Copy))
            st.wait(i + ".d2t")
            st.do(a_.activation(G3, bank(1), ACT.Copy), i + ".d2t_")
            st.wait(i + ".d4t", i + ".a1")
            st.do(a_.activation(G0, bank(0), ACT.Copy))
            st.do(a_.activation(G1, bank(1), ACT.Copy), i + ".d4t_")
            st.wait(i + ".d8t", i + ".a2")
            st.do(a_.activation(G2, bank(0), ACT.Copy), i + ".d8t_")
            st.wait(i + ".mt", i + ".a8")
            st.do(a_.activation(G0, bank(0), ACT.Copy), i + ".mt_")
            st.wait(i + ".m2t")
            st.do(a_.activation(G1, bank(1), ACT.Copy), i + ".m2t_")
            st.wait(i + ".turn")
            if g == 0 and t:
                st.wait(f"y.mm{t - 1}")
            st.do(a_.activation(AT[:, 2 * g * P:(2 * g + 2) * P], PS[:, 0, 0:256], ACT.Copy), i + ".at")

        def solve_dve(st, t, g):
            i = f"r{t}.{g}"
            st.wait(i + ".scores")
            if g == 0 and t:
                st.wait(f"y.mm{t - 1}")
            R4 = quad(RHS, g)
            b12, b34 = h4(two(1)), h4(two(3))
            st.settle()
            st.do(v.tensor_tensor(h4(G2), b34[:, :, 0:P], m4("strictT"), ALU.mult))
            st.do(v.tensor_tensor(q4(G0), scores, mq("sub16"), ALU.mult))
            st.do(v.tensor_tensor(h4(G1), b12[:, :, 0:P], m4("sub16T"), ALU.mult))
            st.do(v.tensor_tensor(R4[:, :, :, P:2 * P], scores, mq("off16"), ALU.mult))
            st.do(v.tensor_tensor(quad(RB[:, :, 0, :], g), q4(two(1))[:, :, :, P:2 * P], mq("chunkT"), ALU.mult))
            st.do(v.tensor_tensor(quad(RB[:, :, 1, :], g), q4(two(3))[:, :, :, P:2 * P], mq("chunkT"), ALU.mult), i + ".masked")
            R = R4.rearrange("p w j c -> p w (j c)")
            st.wait(i + ".rhs")
            for a, b, r in ((".a1", 3, ".r1"), (".a2", 6, ".r2"), (".a4", 3, ".r4"), (".a8", 6, ".r8")):
                st.wait(i + a)
                st.settle()
                st.do(v.tensor_tensor(R, R, PS[:, b:b + 2, :], ALU.add), i + r)
            for a, b, r in ((".b2", 3, ".q2"), (".b1", 4, ".q1")):
                st.wait(i + a)
                st.settle()
                st.do(v.tensor_tensor(R4[:, :, :, 0:P], R4[:, :, :, 0:P], q4(bank(b)), ALU.add), i + r)

        def state_pe(st, t):
            for cc in range(2):
                n, r = 2 * t + cc, 64 * cc
                rows = slice(r, r + 64)
                st.wait(f"r{t}.1.at")
                if n:
                    st.wait(f"st{n - 1}")
                for h in range(8):
                    j, b = h // 2, 64 * (h % 2)
                    last = mm(PS[r:r + 64, 5 + h % 2, j * 64:(j + 1) * 64], AT[b:b + 64, j * P + r:j * P + r + 64],
                              ST[n % 3][b:b + 64, j * 64:(j + 1) * 64], start=True, stop=True)
                st.do(last, f"u.mm{n}")
                for h in range(8):
                    j, b = h // 2, 64 * (h % 2)
                    c = slice(t * P + b, t * P + b + 64)
                    o = PS[b:b + 64, 7, j * 64:(j + 1) * 64]
                    mm(o, T(4 + j)[rows, c], T(8 + j)[rows, c], start=True, stop=False)
                    if h == 0:
                        st.wait(f"u{n}")
                    last = mm(o, T(18 + j)[rows, c], UT[rows, slot(h), :], start=False, stop=True)
                st.do(last, f"s.mm{n}")
            for h in range(8):
                j, b = h // 2, 64 * (h % 2)
                o = PS[b:b + 64, 5, j * P:(j + 1) * P]
                mm(o, UT[:, slot(h), :], RB[:, slot(h), 0, :], start=True, stop=False)
                mm(o, T(8 + j)[:, t * P + b:t * P + b + 64], RB[:, slot(h), 1, :], start=False, stop=False)
                for cc in range(2):
                    last = mm(o[:, 64 * cc:64 * cc + 64], ST[(2 * t + cc) % 3][b:b + 64, j * 64:(j + 1) * 64],
                              AR[j][b:b + 64, t, 1, 64 * cc:64 * cc + 64], start=False, stop=(cc == 1))
            st.do(last, f"y.mm{t}")

        def state_dve(st, t):
            for cc in range(2):
                n, r = 2 * t + cc, 64 * cc
                rows = slice(r, r + 64)
                st.wait(f"u.mm{n}")
                st.settle()
                st.do(v.tensor_tensor(UT[rows].rearrange("p (w j) c -> p w j c", w=2), RHS[rows, :, 64:P].rearrange("p (w j) c -> p w j c", w=2),
                                      PS[rows, 5:7, 0:256].rearrange("p w (j c) -> p w j c", j=4), ALU.add), f"u{n}")
                if n == 0:
                    st.do(v.memset(SD[:], 0.0))
                st.settle()
                d = SM[:, DCY:DCY + 32].rearrange("p (j c) -> p j c", j=4)[:, :, n:n + 1].to_broadcast([P, 4, 64])
                if n >= 2:
                    st.wait(f"y.mm{(n - 2) // 2}")
                st.do(v.tensor_tensor(p4(ST[(n + 1) % 3]), p4(ST[n % 3]), d, ALU.mult))
                st.wait(f"s.mm{n}")
                st.settle()
                st.do(v.tensor_tensor(ST[(n + 1) % 3], ST[(n + 1) % 3], PS[:, 7, 0:256], ALU.add), f"st{n}")

        def rw_pe(pe, st, e):
            for t in range(TT):
                solve_pe(st, t, 0)
                solve_pe(st, t, 1)
                state_pe(st, t)

        def rw_act(act, st, e):
            for t in range(TT):
                solve_act(st, t, 0)
                solve_act(st, t, 1)
                st.wait(f"y.mm{t}")
                st.do(a_.activation(A[:, 26:30, t * P:(t + 1) * P], PS[:, 5, :].rearrange("p (j c) -> p j c", j=4), ACT.Copy), f"y{t}")

        def rw_dve(dve, st, e):
            for t in range(TT):
                solve_dve(st, t, 0)
                solve_dve(st, t, 1)
                state_dve(st, t)
        Stage(tensor=rw_pe, scalar=rw_act, vector=rw_dve)
        mark("gn.in", "scalar")
        dma("g2", T(22), io["lora"][:, S:2 * S], ready=["y.mm3"])

        def rw_gate_pe(pe, st, e):
            st.wait("g2", "y3")
            for j in range(4):
                st.do(mm(bank(j), T(22)[:, j * P:(j + 1) * P], T(13), start=True, stop=True), f"rw.g{j}")
        Stage(tensor=rw_gate_pe)

        def gn_apply(st, g, k, x, rstd):
            st.wait(f"rw.g{g}")
            st.do(v.scalar_tensor_tensor(out=x, in0=x, scalar=vec("lnx_g", g), in1=rstd, op0=ALU.mult, op1=ALU.mult))
            st.settle()
            st.do(v.scalar_tensor_tensor(out=x, in0=x, scalar=vec("lnx_b", g), in1=T(34 + g), op0=ALU.add, op1=ALU.add))
            st.settle()
            st.do(v.tensor_tensor(x, x, bank(g), ALU.mult), f"yb.{g}")
        colnorm("gn", [[T(26 + j)] for j in range(4)], 64, "epsx", True, gn_apply, lambda i: T(i), lambda i: T(18 + i), sums=ones64)
        split("yb", [T(18 + k) for k in range(4)], YH[:, 4:8, :], YL[:, 4:8, :], ready=lambda k: f"yb.{k}")
        class UpGates:

            def __init__(self):
                self.e0 = evac[0]
                evac[0] += 32
                PLAN.append(self)

            def tensor(self, pe, st):
                st.wait("yb.ready")
                for r in range(8):
                    u, b, y0 = U0["s.up"] + 3 * r, 4 * (r % 2), 0 if r < 4 else 4
                    pe.wait_ge(split_done, u + 1)
                    pe.wait_ge(banks_free, 4 + self.e0 + 4 * max(r - 1, 0))
                    for n in range(2):
                        for k in range(4):
                            c = slice((4 * n + k) * P, (4 * n + k + 1) * P)
                            last = unit_passes(bank(b + n), WH[:, u % SPLIT, c], WL[:, u % SPLIT, c],
                                               YH[:, y0 + k, :], YL[:, y0 + k, :], k == 0, k == 3)
                    last.then_inc(unit_done, 1)
                    for n in range(2):
                        u += 1
                        pe.wait_ge(split_done, u + 1)
                        for k in range(KT):
                            c = slice(k * P, (k + 1) * P)
                            last = unit_passes(bank(b + 2 + n), WH[:, u % SPLIT, c], WL[:, u % SPLIT, c],
                                               XH[:, k, :], XL[:, k, :], k == 0, k == KT - 1)
                        last.then_inc(unit_done, 1)

            def scalar(self, act, st):
                for r in range(8):
                    for n in range(2):
                        act.wait_ge(unit_done, U0["s.up"] + 3 * r + 2 + n)
                        act.wait_ge(banks_free, 4 + self.e0 + (4 * (r - 1) + 2 * (n + 1) if r else 0))
                        st.do(a_.activation(SG[:, n, :], bank(4 * (r % 2) + 2 + n), ACT.Sigmoid), f"up.gate{r}.{n}")

            def vector(self, dve, st):
                dve.wait_ge(banks_free, 4 + self.e0)
                for r in range(8):
                    for n in range(2):
                        st.wait(f"up.gate{r}.{n}")
                        m, up = T(24 + 2 * (r % 4) + n), bank(4 * (r % 2) + n)
                        if r < 4:
                            v.tensor_tensor(m, SG[:, n, :], up, ALU.mult).then_inc(banks_free, 2)
                        else:
                            st.do(v.tensor_tensor(SG[:, n, :], SG[:, n, :], up, ALU.mult))
                            st.settle()
                            v.tensor_tensor(m, m, SG[:, n, :], ALU.add).then_inc(banks_free, 2)
        UpGates()
        dma("unspill", X[:], io["spill"], ready=["yb.ready"])
        free_until("scalar", "vector")
        split("merged", [T(24 + k) for k in range(KT)], XH, XL)
        vs(lambda st: st.wait("unspill"))
        Linear("s.out", add=True, alpha=ALPHA, ready=["merged.ready"])
        layernorm("fns", "ln1_g", "ln1_b")
        ffn("s", ALPHA)
        layernorm("end2", "ln2_g", "ln2_b", split_it=False)

        mark("tn.in", "vector")
        rmsnorm("tn", "norm_g3", s0=24)
        mark("tn.done", "vector")
        dma("spill3", io["spill3"], X[:], ready=["tn.done"])

        def gif_pe(pe, st, e):
            st.wait("tn.ready")
            pe_tile(pe, U0["t.gif"], e, U0["t.gif"] % SPLIT, e % 4, XH, XL, S)
        IG, FL, GG, FX = T(32), T(33), T(34), T(37)

        def gif_act(act, st, e):
            act.wait_ge(unit_done, U0["t.gif"] + 1)
            b = e % 4
            st.wait("tn.done")
            st.do(a_.activation(IG[0:4, :], PS[0:4, b, :], ACT.Identity, bias=vec("ml_bi")[0:4, :]))
            st.do(a_.activation(FL[0:4, :], PS[32:36, b, :], ACT.Copy))
            st.do(a_.activation(FX[0:8, :], PS[64:72, b, :], ACT.Copy))
            st.settle()
            st.do(a_.activation(FL[0:4, :], FL[0:4, :], ACT.Identity, bias=vec("ml_bf")[0:4, :]), "gif.f")
            st.do(a_.activation(FX[0:8, :], FX[0:8, :], ACT.Identity, bias=vec("fox_bf")[0:8, :]), "gif.x")
            st.settle()
            for t, n, r in ((35, 4, FL), (36, 8, FX)):
                x = T(t)[0:n, :]
                st.do(a_.activation(x, r[0:n, :], ACT.Abs))
                st.settle()
                st.do(a_.activation(x, x, ACT.Exp, scale=-1.0))
                st.settle()
                st.do(a_.activation(x, x, ACT.Ln, bias=cst("one")[0:n, :]), f"gif.ln{n}")
            act.wait_ge(unit_done, U0["t.gif"] + 1)

        def gif_dve(dve, st, e):
            NRc = T(28)
            st.do(v.memset(NRc[0:8, :], 1.0))
            st.wait("gif.ln8")
            for t, n, r in ((35, 4, FL), (36, 8, FX)):
                st.do(v.scalar_tensor_tensor(out=T(t)[0:n, :], in0=r[0:n, :], scalar=0.0, in1=T(t)[0:n, :], op0=ALU.min, op1=ALU.subtract))
            st.settle()
            for t, n, r in ((35, 4, FL), (36, 8, FX)):
                st.do(v.tensor_tensor_scan(r[0:n, :], NRc[0:n, :], T(t)[0:n, :], 0.0, ALU.mult, ALU.add))
            st.settle()
            st.do(v.tensor_scalar(FX[0:8, :], FX[0:8, :], -1.0, None, ALU.mult), "fox.negf")
            st.do(v.tensor_tensor(IG[0:4, :], IG[0:4, :], FL[0:4, :], ALU.subtract))
            st.settle()
            st.do(v.tensor_tensor_scan(GG[0:4, :], IG[0:4, :], IG[0:4, :], 0.0, ALU.max, ALU.max))
            st.settle()
            st.do(v.tensor_tensor(FL[0:4, :], FL[0:4, :], GG[0:4, :], ALU.add))
            st.do(v.tensor_scalar(T(35)[0:4, :], GG[0:4, :], -1.0, None, ALU.mult))
            st.settle()
            v.tensor_copy(GG[0:4, :], T(35)[0:4, :]).then_inc(banks_free, 1)
            dve.wait_ge(banks_free, 4 + e + 1)
            names["ml.rows"] = (banks_free, 4 + e + 1)
        Stage(tensor=gif_pe, scalar=gif_act, vector=gif_dve)
        evac[0] += 1

        Linear("t.qk", dst=at(0))
        vs(lambda st: depthwise(st, lambda k: T(k), lambda k: T(16 + k), 4, "conv_w3", None, 16))
        mark("conv3", "vector")

        def qk_silu(act, st, e):
            st.wait("conv3")
            st.do(a_.activation(W2(16, 8), W2(16, 8), ACT.Silu))
            st.do(a_.activation(W2(24, 8), W2(24, 8), ACT.Silu), "ml.qk")
        Stage(scalar=qk_silu)
        TokenMajor("t.v", 2, lambda h, t: T(2 * t + h))
        Pairs("t.oz", 8, at(8), ACT.Sigmoid, func2=ACT.Silu)

        def ml_cols_pe(pe, st, e):
            pe.wait_ge(banks_free, 4 + e)
            st.wait("ml.rows", "ml.qk")
            for t in range(TT):
                last = nc.tensor.transpose(PS[:, 0, 4 * t:4 * t + 4], IG[0:4, t * P:(t + 1) * P], ident[0:4, 0:4])
            st.do(last, "ml.cols")

        def ml_cols_act(act, st, e):
            st.wait("ml.cols")
            st.do(a_.activation(SM[:, 48:64], PS[:, 0, 0:16], ACT.Copy), "ml.c")
        Stage(tensor=ml_cols_pe, scalar=ml_cols_act)

        EMT = T(36)

        def ml_pe(pe, st, e):
            st.wait("ml.c")

            def score(n):
                h, j = n // TT, n % TT
                c0 = j * P
                if n >= 2:
                    st.wait(f"ml.e{n - 2}", f"ml.p{n - 2}")
                o = PS[:, n % 2, c0:S]
                mm(o, bcast(ident[0:4, h:h + 1], P), GG[0:4, c0:S], start=True, stop=False)
                st.do(mm(PS[:, n % 2, c0:c0 + P], ident, cst("caddT"), start=False, stop=True), f"ml.d{n}")
                for d in range(2):
                    last = mm(PS[:, 2 + n % 2, c0:S], T(24 + 2 * h + d)[:, c0:c0 + P], T(16 + 2 * h + d)[:, c0:S],
                              start=(d == 0), stop=(d == 1))
                st.do(last, f"ml.s{n}")

            def gather(n):
                h, j = n // TT, n % TT
                c0 = j * P
                if j == 0:
                    if h:
                        st.wait(f"ml.h{h - 1}")
                    st.do(mm(PS[:, 7, :], bcast(ident[0:4, h:h + 1], P), FL[0:4, :], start=True, stop=True), f"ml.m{h}")
                st.wait(f"ml.p{n}")
                pt = SG[:, 2 + n % 2, c0:S]
                for d in range(2):
                    mm(PS[:, 4 + d, c0:S], W2(2 * j, 2)[:, h * 256 + d * P:h * 256 + (d + 1) * P], pt, start=(j == 0), stop=(j == TT - 1))
                st.do(mm(PS[:, 6, c0:S], ones, pt, start=(j == 0), stop=(j == TT - 1)), f"ml.n{n}")
            score(0)
            for n in range(16):
                if n < 15:
                    score(n + 1)
                gather(n)

        def ml_act(act, st, e):
            for n in range(16):
                h, j = n // TT, n % TT
                st.wait(f"ml.d{n}")
                if n >= 2:
                    st.wait(f"ml.p{n - 2}")
                st.do(a_.activation(SG[:, n % 2, j * P:S], PS[:, n % 2, j * P:S], ACT.Exp, bias=SM[:, 48 + 4 * j + h:49 + 4 * j + h]), f"ml.e{n}")
                if j == 3:
                    st.wait(f"ml.m{h}")
                    if h:
                        st.wait(f"ml.h{h - 1}")
                    st.do(a_.activation(EMT, bank(7), ACT.Exp, scale=-1.0), f"ml.em{h}")

        def ml_dve(dve, st, e):
            dve.wait_ge(banks_free, 4 + e)
            for n in range(16):
                h, j = n // TT, n % TT
                st.wait(f"ml.s{n}", f"ml.e{n}")
                if n >= 2:
                    st.wait(f"ml.n{n - 2}")
                st.do(v.scalar_tensor_tensor(out=SG[:, 2 + n % 2, j * P:S], in0=PS[:, 2 + n % 2, j * P:S], scalar=1.0 / 16,
                                             in1=SG[:, n % 2, j * P:S], op0=ALU.mult, op1=ALU.mult), f"ml.p{n}")
                if j == 3:
                    st.wait(f"ml.n{n}", f"ml.em{h}")
                    st.settle()
                    st.do(v.tensor_tensor(SD[:], bank(6), EMT, ALU.max))
                    st.settle()
                    st.do(v.scalar_tensor_tensor(out=SD[:], in0=bank(6), scalar=-1.0, in1=SD[:], op0=ALU.mult, op1=ALU.max))
                    st.settle()
                    st.do(v.reciprocal(SD[:], SD[:]))
                    st.settle()
                    for d in range(2):
                        st.do(v.tensor_tensor(T(16 + 2 * h + d), SD[:], bank(4 + d), ALU.mult), f"ml.h{h}")
        Stage(tensor=ml_pe, scalar=ml_act, vector=ml_dve)
        mark("mn.in", "vector")

        def ml_apply(st, g, k, x, rstd):
            st.do(v.scalar_tensor_tensor(out=x, in0=x, scalar=vec("ml_norm_g", 2 * g + k), in1=rstd, op0=ALU.mult, op1=ALU.mult))
            st.settle()
            st.do(v.tensor_tensor(x, x, T(8 + 2 * g + k), ALU.mult), f"yA.{2 * g + k}")
        colnorm("mn", [[T(16 + 2 * h), T(17 + 2 * h)] for h in range(4)], 256, "eps6", False, ml_apply, lambda i: T(24 + i), None, b0=0)
        split("yA", [T(16 + k) for k in range(KT)], YH, YL, ready=lambda k: f"yA.{k}")
        Pairs("t.br0", 8, at(24), ACT.Sigmoid, of=1, yh=(YH, YL), ready=["yA.ready"])

        Linear("t.fq", dst=at(0), scale=128 ** -0.5)
        Linear("t.fk", dst=at(8))
        TokenMajor("t.fv", 2, lambda h, t: T(16 + 2 * t + h))

        def fox_score(h, c, i, out):
            mm(out, T(h)[:, i * P:(i + 1) * P], T(8 + h)[:, 0:(i + 1) * P], start=True, stop=False)
            mm(out, bcast(ident[0:8, h:h + 1], P), FX[0:8, 0:(i + 1) * P], start=False, stop=False)
            return mm(out[:, i * P:(i + 1) * P], ident, cst("cadd"), start=False, stop=True)
        mark("fox.in", "vector")
        Stage(scalar=lambda act, st, e: st.wait("spill3"))
        Attention("fox", 8, lambda i: i + 1, fox_score, lambda h, j, s: W2(16 + 2 * j, 2)[:, h * P:(h + 1) * P],
                  lambda h: (0, P), lambda h, s: T(h), prob=lambda n: X[:, n, :], pt=32)
        Linear("t.fz", dst=at(8), func=ACT.Silu, pre=["fox.done"])

        def fox_gate(st):
            for k in range(KT):
                st.do(v.tensor_tensor(T(k), T(k), T(8 + k), ALU.mult), f"yB.{k}")
        vs(fox_gate)
        split("yB", [T(k) for k in range(KT)], YH, YL, ready=lambda k: f"yB.{k}")
        Pairs("t.br1", 8, at(24), ACT.Sigmoid, of=1, yh=(YH, YL), ready=["yB.ready"], acc=0)

        Linear("t.cu", dst=at(0))

        def pool_windows(st):
            for g in range(4):
                src = [T(2 * g), T(2 * g + 1)]
                for lv in range(g + 1):
                    sh = 1 << lv
                    dst = [T(8 + 2 * (lv % 2) + q + 4 * (g % 2)) for q in range(2)]
                    st.settle()
                    for q in range(2):
                        st.do(v.tensor_tensor(dst[q][:, sh:], src[q][:, sh:], src[q][:, :S - sh], ALU.add))
                        st.do(v.tensor_copy(dst[q][:, :sh], src[q][:, :sh]))
                    src = dst
                w = 2 << g
                st.settle()
                for q in range(2):
                    k = 2 * g + q
                    o = T(16 + k)
                    st.do(v.scalar_tensor_tensor(out=o[:, 16:], in0=src[q][:, 16:], scalar=1.0 / w, in1=T(k)[:, 16:],
                                                 op0=ALU.mult, op1=ALU.subtract))
                    st.do(v.tensor_tensor(o[:, :16], src[q][:, :16], cst("icnt", k=16 * k, n=16), ALU.mult))
                st.settle()
                for q in range(2):
                    k = 2 * g + q
                    st.do(v.tensor_tensor(T(16 + k)[:, :16], T(16 + k)[:, :16], T(k)[:, :16], ALU.subtract))
            st.do(v.memset(SM[:, 0:1], 0.0), "pool.d")
        vs(pool_windows)
        split("pd", [T(16 + k) for k in range(KT)], YH, YL, ready=lambda k: "pool.d")

        def pool_pe(pe, st, e):
            st.wait("pd.ready")
            pe.wait_ge(banks_free, 4 + e)
            for n in range(2):
                u = U0["t.pool"] + n
                pe.wait_ge(split_done, u + 1)
                for g in range(2):
                    for o in range(2):
                        for k in range(2):
                            c = slice((4 * g + 2 * o + k) * P, (4 * g + 2 * o + k + 1) * P)
                            q = 4 * n + 2 * g + k
                            last = unit_passes(bank(4 * n + 2 * g + o), WH[:, u % SPLIT, c], WL[:, u % SPLIT, c],
                                               YH[:, q, :], YL[:, q, :], k == 0, k == 1)
                last.then_inc(unit_done, 1)

        def pool_act(act, st, e):
            st.wait("pd.ready")
            act.wait_ge(unit_done, U0["t.pool"] + 2)
            for k in range(KT):
                a_.activation(T(8 + k), bank(k), ACT.Copy, scale=vec("pool_scale", k)).then_inc(banks_free, 1)
        Stage(tensor=pool_pe, scalar=pool_act)
        evac[0] += 8
        Linear("t.cz", dst=at(0), func=ACT.Silu, pre=["pd.ready"])

        def pool_gate(st):
            for k in range(KT):
                st.do(v.tensor_tensor(T(k), T(k), T(8 + k), ALU.mult), f"yC.{k}")
        vs(pool_gate)
        split("yC", [T(k) for k in range(KT)], YH, YL, ready=lambda k: f"yC.{k}")
        Pairs("t.br2", 8, at(24), ACT.Sigmoid, of=1, yh=(YH, YL), ready=["yC.ready"], acc=8)
        dma("unspill3", X[:], io["spill3"], ready=["fox.done"])
        free_until("scalar", "vector")
        split("mg3", [T(24 + k) for k in range(KT)], XH, XL)
        vs(lambda st: st.wait("unspill3"))
        Linear("t.out", add=True, ready=["mg3.ready"])
        colnorm("end3", [allx], D, "eps6", False, to_residual("final_g"), lambda i: T(24 + i), None)
        mark("end3.y", "vector")
        dma("store", io["outT"].rearrange("(k p) t -> p k t", p=P), X[:], ready=["end3.y"])
        Stage(scalar=lambda act, st, e: st.wait("store"))
        def walk(role, eng, sem_):
            st = Steps(eng, sem_, names, sems)
            for s in PLAN:
                if isinstance(s, Stage):
                    s.run(role, eng, st)
                elif role == "tensor":
                    s.tensor(eng, st)
                elif role == "scalar":
                    s.scalar(eng, st)
                elif role == "vector":
                    s.vector(eng, st)
            return st

        block = ctx.enter_context(nc.Block())

        @block.sync
        def _(sp):
            xin = io["xT"].rearrange("(k p) t -> p k t", p=P)
            sp.dma_start(CST[:], io["consts"]).then_inc(params, 16)
            sp.dma_start(VEC[:], io["vecs"]).then_inc(params, 16)
            sp.dma_start(X[:], xin).then_inc(params, 16)
            memv = A[:, 8:12, :].rearrange("p a (b c) -> p (a b) c", c=MEM)
            sp.dma_start(memv, io["memT"].rearrange("(k p) t -> p k t", p=P)).then_inc(params, 16)
            w = io["units"].rearrange("u p c -> p u c")
            for j in range(RAW):
                sp.dma_start(RW[:, j, :], w[:, j, :]).then_inc(raw_full[j], 16)
            with sp.Fori(1, NUNITS // RAW) as i:
                for j in range(RAW):
                    sp.wait_ge(split_done, i * RAW + (j - RAW + 1))
                    sp.dma_start(RW[:, j:j + 1, :], w[:, bass.ds(i * RAW + j, 1), :]).then_inc(raw_full[j], 16)
            for u in range(NUNITS // RAW * RAW, NUNITS):
                sp.wait_ge(split_done, u - RAW + 1)
                sp.dma_start(RW[:, u % RAW, :], w[:, u, :]).then_inc(raw_full[u % RAW], 16)

        @block.gpsimd
        def _(pool):
            def unit(u, fill, j, guard):
                pool.wait_ge(raw_full[j], fill)
                if guard:
                    pool.wait_ge(unit_done, u - SPLIT + 1)
                pool.sem_inc(slots_open, 1)
                nc.gpsimd.tensor_copy(WH[:, j % SPLIT, :], RW[:, j, :]).then_inc(split_hi, 1)
                pool.wait_ge(split_hi, u + 1)
                nc.gpsimd.tensor_tensor(WL[:, j % SPLIT, :], RW[:, j, :], WH[:, j % SPLIT, :].bitcast(F32),
                                        ALU.subtract).then_inc(split_done, 1)
                
            for j in range(RAW):
                unit(j, 16, j, j >= SPLIT)
            with pool.Fori(1, NUNITS // RAW) as i:
                for j in range(RAW):
                    unit(i * RAW + j, i * 16 + 16, j, True)
            for u in range(NUNITS // RAW * RAW, NUNITS):
                unit(u, 16 * (u // RAW + 1), u % RAW, True)

        @block.scalar
        def _(act):
            act.wait_ge(params, 64)
            walk("scalar", act, scalar_steps)

        @block.vector
        def _(dve):
            dve.sem_inc(banks_free, 4)
            dve.wait_ge(params, 64)
            walk("vector", dve, vector_steps)

        @block.tensor
        def _(pe):
            pe.wait_ge(params, 64)
            walk("tensor", pe, tensor_steps)


def blocks(w):
    k, n = w.shape
    return w.reshape(k // P, P, n // P, P).transpose(2, 1, 0, 3).reshape(n // P, P, k)


def rows2(w):
    return w.reshape(4, 2, P, -1, S).transpose(3, 0, 2, 1, 4).reshape(-1, P, D)


def alternate(a, b):
    return np.stack([a, b], 1).reshape(-1, P, D)


def weight_units(i):
    H = 512
    out = []
    ab = blocks(i["w_in_ab"][0])
    out += [alternate(ab[16:20], ab[20:24]), ab[0:4], ab[4:8], ab[8:12], ab[12:16], blocks(i["w_out_ab"][0])]

    def layer(l):
        kv = i["xa_wkv"][l]
        f = blocks(i["ffn_w_in"][l])
        return [blocks(kv[:, :D]), rows2(kv[:, D:]), blocks(i["xa_wq"][l]), blocks(i["xa_wo"][l]),
                alternate(f[:NH], f[NH:]), i["ffn_w_out"][l].reshape(NH, P, D)]
    out += layer(0)
    w = i["w_in_cd"][0]
    out += [blocks(w[:, :2 * H]), rows2(w[:, 2 * H:3 * H]), blocks(w[:, 3 * H:]), blocks(i["w_out_cd"][0])]
    out += layer(1)
    w = i["w_in_2"][0]
    gates = blocks(w[:, 3328:])
    ups = []
    for n, name in enumerate(("w_up_a_2", "w_up_b_2")):
        u = i[name][0].reshape(4, P, 4, 2, P).transpose(2, 1, 3, 0, 4).reshape(4, P, D)
        for r in range(4):
            ups += [u[r:r + 1], gates[8 * n + 2 * r:8 * n + 2 * r + 2]]
    out += [blocks(w[:, :2 * H]), rows2(w[:, 2 * H:3 * H]), blocks(w[:, 3 * H:3328]), *ups, blocks(i["w_out_2"][0]),
            alternate(blocks(i["ffn_w_gate_2"][0]), blocks(i["ffn_w_up_2"][0])), i["ffn_w_down_2"][0].reshape(NH, P, D)]
    w = i["w_in_3"][0]
    at, cut = 0, {}
    for name, n in (("aq", D), ("ak", D), ("av", D), ("ao", D), ("az", D), ("ai", 4), ("af", 4), ("bq", D), ("bk", D),
                    ("bv", D), ("bz", D), ("bf", 8), ("cu", D), ("cz", D), ("gates", 3 * D)):
        cut[name] = w[:, at:at + n]
        at += n
    gif = np.zeros((D, P), np.float32)
    gif[:, 0:4], gif[:, 32:36], gif[:, 64:72] = cut["ai"], cut["af"], cut["bf"]
    br = [alternate(blocks(i["w_branch_3"][0, n]), blocks(cut["gates"][:, n * D:(n + 1) * D])) for n in range(3)]
    pool = i["pool_w_3"][0].reshape(2, 2, 2, P, 2, P).transpose(0, 3, 1, 4, 2, 5).reshape(2, P, D)
    out += [blocks(gif), blocks(cut["aq"]), blocks(cut["ak"]), rows2(cut["av"]), alternate(blocks(cut["ao"]), blocks(cut["az"])),
            br[0], blocks(cut["bq"]), blocks(cut["bk"]), rows2(cut["bv"]), blocks(cut["bz"]), br[1],
            blocks(cut["cu"]), pool, blocks(cut["cz"]), br[2], blocks(i["w_out_3"][0])]
    return np.concatenate(out)


def vectors(i):
    def col(v):
        return v.reshape(-1, P).T

    def part(v):
        c = np.zeros((P, 1), np.float32)
        c[:v.size, 0] = v.ravel()
        return c
    parts = {
        "norm_mix0": col(i["norm_mix"][0]), "norm_mix1": col(i["norm_mix"][1]), "norm_xattn0": col(i["norm_xattn"][0]),
        "norm_xattn1": col(i["norm_xattn"][1]), "norm_ffn0": col(i["norm_ffn"][0]), "norm_ffn1": col(i["norm_ffn"][1]),
        "mem_norm": col(i["mem_norm"]), "final_norm": col(i["final_norm"]), "lb": col(i["hgrn_lower_bounds"]),
        "hgrn_out_norm": col(i["hgrn_out_norm"]),
        "conv_dw_w": i["conv_dw_w"][0].reshape(31, 4, P).transpose(2, 1, 0).reshape(P, 124), "conv_dw_b": col(i["conv_dw_b"]),
        "conv_ln_g": col(i["conv_ln_g"]), "conv_ln_b": col(i["conv_ln_b"]), "sgu_ln_g": col(i["sgu_ln_g"]), "sgu_ln_b": col(i["sgu_ln_b"]),
        "ln_in_g": col(i["ln_in_g_2"]), "ln_in_b": col(i["ln_in_b_2"]), "subln_g": col(i["diff_subln_g_2"]), "mu": col(i["rwkv_mu_2"]),
        "w0": col(i["rwkv_w0_2"]), "a0": col(i["rwkv_a0_2"]), "k_k": col(i["rwkv_k_k_2"]), "k_a": col(i["rwkv_k_a_2"]),
        "r_k": col(i["rwkv_r_k_2"]), "lnx_g": col(i["rwkv_lnx_g_2"]), "lnx_b": col(i["rwkv_lnx_b_2"]),
        "ln1_g": col(i["ln1_g_2"]), "ln1_b": col(i["ln1_b_2"]), "ln2_g": col(i["ln2_g_2"]), "ln2_b": col(i["ln2_b_2"]),
        "norm_g3": col(i["norm_g_3"]), "conv_w3": i["conv_w_3"][0].reshape(4, 16, P).transpose(2, 1, 0).reshape(P, 64),
        "ml_norm_g": col(i["ml_norm_g_3"]), "pool_scale": col(i["pool_scale_3"]), "final_g": col(i["final_g_3"]),
        "ml_bi": part(i["ml_bi_3"]), "ml_bf": part(i["ml_bf_3"]), "fox_bf": part(i["fox_bf_3"]),
    }
    return np.concatenate([parts[n] for n, _ in VECS], 1)


def laid_out(inputs):
    i = {k: np.asarray(a) for k, a in inputs.items()}
    lora = np.zeros((P, D), np.float32)
    lora[0:64, 0:S], lora[64:P, 0:S], lora[:, S:] = i["rwkv_w2_2"][0], i["rwkv_a2_2"][0], i["rwkv_g2_2"][0]
    lam = np.concatenate([i[f"diff_lam_{n}_2"][0] for n in ("q1", "k1", "q2", "k2")])
    return {
        "units": weight_units(i), "vecs": vectors(i), "consts": constants(), "reset": reset_mask(), "onehot": bucket_table(),
        "xT": i["x"][0].T, "memT": i["mem"][0].T, "rel": i["rel_bias_2"], "lora": lora,
        "lam": np.broadcast_to(lam, (P, 256)), "sguw": i["sgu_w"][0].transpose(2, 0, 1).reshape(P, S),
        "sgub": i["sgu_b"][0].reshape(1, S),
    }


def declare(nc, arrays):
    io = {n: nc.dram_tensor(f"in_{n}", a.shape, mybir.dt.from_np(a.dtype), kind="ExternalInput").ap() for n, a in arrays.items()}
    io["outT"] = nc.dram_tensor("out_T", (D, S), F32, kind="ExternalOutput").ap()
    for n in ("spill", "spill3"):
        io[n] = nc.dram_tensor(n, (P, KT, S), F32, kind="Internal").ap()
    return io


def kernel(**inputs):
    import concourse.bacc as _bacc
    from concourse.bass_utils import run_bass_kernel_spmd as _run

    arrays = {n: np.ascontiguousarray(a) for n, a in laid_out(inputs).items()}
    names = {}
    for counting in (True, False):
        nc = _bacc.Bacc("TRN2", target_bir_lowering=False, num_devices=1, dynamic_dma_scratch_size=1024)
        io = declare(nc, arrays)
        names["unknown"] = (nc.alloc_semaphore("unknown"), 1)
        if not counting:
            names.pop("unknown")
        program(nc, io, names)
    r = _run(nc, [{f"in_{n}": a for n, a in arrays.items()}], core_ids=[0])
    return np.ascontiguousarray(r.results[0]["out_T"].T)[None]
```

```python
import math
from contextlib import ExitStack

import numpy as np
import concourse.bass as bass
from concourse import mybir

F32 = mybir.dt.float32
F32R = mybir.dt.float32r
U32 = mybir.dt.uint32
ALU = mybir.AluOpType
ACT = mybir.ActivationFunctionType
AX = mybir.AxisListType

P = 128
S = 512
TT = S // P
D = 1024
KT = D // P
MEM = 256
HID = 2816
NH = HID // P
SPLIT = 2
RAW = 4
NEG = -1e30
EPS6, EPS5, EPSX = 1e-6, 1e-5, 64e-5
ALPHA = 2.0 ** 0.25
LAMBDA0 = 0.8 - 0.6 * math.exp(0.0)

VECS = [
    ("norm_mix0", 8), ("norm_mix1", 8), ("norm_xattn0", 8), ("norm_xattn1", 8), ("norm_ffn0", 8), ("norm_ffn1", 8),
    ("mem_norm", 8), ("final_norm", 8), ("lb", 12), ("hgrn_out_norm", 4), ("conv_dw_w", 124), ("conv_dw_b", 4),
    ("conv_ln_g", 4), ("conv_ln_b", 4), ("sgu_ln_g", 4), ("sgu_ln_b", 4),
    ("ln_in_g", 8), ("ln_in_b", 8), ("subln_g", 1), ("mu", 14), ("w0", 4), ("a0", 4), ("k_k", 4), ("k_a", 4),
    ("r_k", 4), ("lnx_g", 4), ("lnx_b", 4), ("ln1_g", 8), ("ln1_b", 8), ("ln2_g", 8), ("ln2_b", 8),
    ("norm_g3", 8), ("conv_w3", 64), ("ml_norm_g", 8), ("pool_scale", 8), ("final_g", 8),
    ("ml_bi", 1), ("ml_bf", 1), ("fox_bf", 1),
]
VCOL = {}
for _name, _n in VECS:
    VCOL[_name] = sum(n for _, n in VECS[:len(VCOL)])
NVEC = sum(n for _, n in VECS)

CONSTS = [("ident", 128), ("ones", 128), ("ones64", 128), ("cadd", 128), ("caddT", 128), ("chunkT", 128),
          ("causalT", 128), ("sub16", 128), ("off16", 128), ("sub16T", 128), ("strictT", 128),
          ("icnt", 128), ("flip", 128), ("caddR", 128),
          ("eps6", 1), ("eps5", 1), ("epsx", 1), ("one", 1)]
CCOL = {}
for _name, _n in CONSTS:
    CCOL[_name] = sum(n for _, n in CONSTS[:len(CCOL)])
NCONST = sum(n for _, n in CONSTS)


def constants():
    c = np.zeros((P, NCONST), np.float32)

    def put(name, a):
        c[:a.shape[0], CCOL[name]:CCOL[name] + a.shape[1]] = a

    p, f = np.arange(P)[:, None], np.arange(P)[None, :]
    chunk = p // 64 == f // 64
    block = p // 16 == f // 16
    put("ident", np.eye(P))
    put("ones", np.ones((P, P)))
    put("ones64", chunk * 1.0)
    put("cadd", np.where(f <= p, 0.0, NEG))
    put("flip", np.eye(P)[::-1])
    put("caddR", np.where(f <= P - 1 - p, 0.0, NEG))
    put("caddT", np.where(p <= f, 0.0, NEG))
    put("chunkT", (chunk & (p <= f)) * 1.0)
    put("causalT", (p <= f) * 1.0)
    put("sub16", (block & (f < p)) * 1.0)
    put("off16", (chunk & ~block & (f < p)) * 1.0)
    put("sub16T", (block & (p < f)) * 1.0)
    put("strictT", (chunk & (p < f)) * 1.0)
    cnt = np.zeros((8, 16))
    for g, w in enumerate((2, 4, 8, 16)):
        cnt[2 * g:2 * g + 2] = 1.0 / np.minimum(np.arange(16) + 1, w)
    put("icnt", np.repeat(cnt.reshape(1, 128), P, 0))
    for name, v in (("eps6", EPS6), ("eps5", EPS5), ("epsx", EPSX), ("one", 1.0)):
        put(name, np.full((P, 1), v))
    return c


def reset_mask():
    return np.repeat((np.arange(S) % 64 != 0)[None].astype(np.float32), P, 0)


def bucket_table():
    dist = np.maximum(255 - np.arange(383), 0)
    d = np.maximum(dist, 1).astype(np.float32)
    large = 16 + (np.log(d / np.float32(16)) / np.float32(math.log(8.0)) * np.float32(16)).astype(np.int32)
    bucket = np.where(dist < 16, dist, np.minimum(large, 31))
    hot = np.zeros((32, 384), np.float32)
    hot[bucket, np.arange(383)] = 1.0
    return hot


UNITS = [
    ("l0.glu", 8), ("l0.q", 4), ("l0.f", 4), ("l0.i", 4), ("l0.g", 4), ("x0.ka", 4), ("x0.va", 4), ("l0.out", 8),
    ("x0.k", 4), ("x0.v", 4), ("x0.q", 8), ("x0.o", 8), ("f0.up", 2 * NH), ("f0.down", NH),
    ("l1.qk", 8), ("l1.v", 4), ("l1.uz", 8), ("x1.va", 4), ("l1.out", 8),
    ("x1.k", 8), ("x1.v", 4), ("x1.q", 8), ("x1.o", 8), ("f1.up", 2 * NH), ("f1.down", NH),
    ("s.q", 4), ("s.k", 4), ("s.v", 4), ("s.rwkv", 14), ("s.up", 24), ("s.out", 8),
    ("fs.up", 2 * NH), ("fs.down", NH),
    ("t.gif", 1), ("t.qk", 16), ("t.v", 8), ("t.oz", 16), ("t.fq", 8),
    ("t.br0", 16), ("t.fk", 8), ("t.fv", 8), ("t.fz", 8), ("t.br1", 16),
    ("t.cu", 8), ("t.cz", 8), ("t.pool", 2), ("t.br2", 16), ("t.out", 8),
]
U0 = {}
for _name, _n in UNITS:
    U0[_name] = sum(n for _, n in UNITS[:len(U0)])
NUNITS = sum(n for _, n in UNITS)
NU = dict(UNITS)


class Steps:

    def __init__(self, eng, sem, names, sems):
        self.eng, self.sem, self.names, self.sems, self.n, self.seen = eng, sem, names, sems, 0, 0

    def do(self, ins, name=None):
        ins.then_inc(self.sem, 1)
        self.n = self.n + 1
        if name is not None:
            self.names[name] = (self.sem, self.n)

    def settle(self):
        if self.seen is not self.n:
            self.eng.wait_ge(self.sem, self.n)
            self.seen = self.n

    def wait(self, *names):
        for name in names:
            sem, n = self.names[name] if name in self.names else self.names["unknown"]
            self.eng.wait_ge(self.sems.get(sem.name, sem), n)


def program(nc, io, names):
    ctx = ExitStack()
    with ctx:
        def sb(name, shape, dt=F32):
            return ctx.enter_context(nc.sbuf_tensor(name, shape, dt))

        sems = {}

        def sem(name):
            sems[name] = ctx.enter_context(nc.semaphore(name))
            return sems[name]

        X = sb("X", [P, KT, S])
        XH, XL = sb("XH", [P, KT, S], F32R), sb("XL", [P, KT, S], F32R)
        YH, YL = sb("YH", [P, KT, S], F32R), sb("YL", [P, KT, S], F32R)
        RW = sb("RW", [P, RAW, D])
        WH, WL = sb("WH", [P, SPLIT, D], F32R), sb("WL", [P, SPLIT, D], F32R)
        A = sb("A", [P, 38, S])
        VEC = sb("VEC", [P, NVEC])
        CST = sb("CST", [P, NCONST])
        SD = sb("SD", [P, S])
        SM = sb("SM", [P, 160])
        PS = ctx.enter_context(nc.psum_tensor("PS", [P, 8, S], F32))
        TAB = nc.dram_tensor("bias_by_distance", [4, 384], F32, kind="Internal").ap()

        raw_full = [sem(f"raw_full{i}") for i in range(RAW)]
        split_hi, split_done = sem("split_hi"), sem("split_done")
        unit_done = sem("unit_done")
        banks_free = sem("banks_free")
        g2_loaded, rk_loaded = sem("g2_loaded"), sem("rk_loaded")
        params, mem_loaded = sem("params"), sem("mem_loaded")
        loads = [sem(f"load{i}") for i in range(24)]
        scalar_steps, vector_steps, tensor_steps = sem("scalar_steps"), sem("vector_steps"), sem("tensor_steps")

        MH = YH[:, 0:4, :].rearrange("p a (b c) -> p (a b) c", c=MEM)
        ML = YL[:, 0:4, :].rearrange("p a (b c) -> p (a b) c", c=MEM)

        def vec(name, k=0, n=1):
            return VEC[:, VCOL[name] + k:VCOL[name] + k + n]

        def cst(name, rows=P, k=0, n=None):
            n = dict(CONSTS)[name] if n is None else n
            return CST[0:rows, CCOL[name] + k:CCOL[name] + k + n]

        ident, ones, ones64 = cst("ident"), cst("ones"), cst("ones64")

        def T(i, n=None):
            return A[:, i, :] if n is None else A[:, i:i + n, :]

        def W2(i, n):
            return A[:, i:i + n, :].rearrange("p a b -> p (a b)")

        def bank(b, cols=S, rows=P, base=0):
            return PS[base:base + rows, b, 0:cols]

        mm = nc.tensor.matmul

        evac = [0]

        def unit_passes(out, hi, lo, xh, xl, first, last):
            mm(out, hi, xh, start=first, stop=False)
            mm(out, hi, xl, start=False, stop=False)
            return mm(out, lo, xh, start=False, stop=last)

        def pe_tile(pe, u, e, slot, b, xh, xl, cols):
            pe.wait_ge(split_done, u + 1)
            pe.wait_ge(banks_free, e + 1)
            for k in range(KT):
                last = unit_passes(bank(b, cols), WH[:, slot, k * P:(k + 1) * P], WL[:, slot, k * P:(k + 1) * P],
                                   xh[:, k, 0:cols], xl[:, k, 0:cols], k == 0, k == KT - 1)
            last.then_inc(unit_done, 1)

        def pe_start(pe, st, ready, u, e, xs, cols=S):
            pe.wait_ge(split_done, u + 2)
            pe.wait_ge(banks_free, e + 2)
            for k in range(KT):
                st.wait(f"{ready}.lo{k}")
                for j, (xh, xl) in enumerate(xs):
                    c = slice(k * P, (k + 1) * P)
                    last = unit_passes(bank((e + j) % 4, cols), WH[:, (u + j) % SPLIT, c], WL[:, (u + j) % SPLIT, c],
                                       xh[:, k, 0:cols], xl[:, k, 0:cols], k == 0, k == KT - 1)
                    if k == KT - 1:
                        last.then_inc(unit_done, 1)

        def pe_linear(pe, st, ready, u0, e0, xh, xl, cols, n):
            xh, xl = (XH, XL) if xh is None else (xh, xl)
            first = 0
            if ready is not None:
                pe_start(pe, st, ready, u0, e0, [(xh, xl), (xh, xl)], cols)
                for j in range(2, 4):
                    pe_tile(pe, u0 + j, e0 + j, (u0 + j) % SPLIT, (e0 + j) % 4, xh, xl, cols)
                first = 1
            if n // 4 > first:
                with pe.Fori(first, n // 4) as i:
                    for j in range(4):
                        pe_tile(pe, u0 + i * 4 + j, e0 + i * 4 + j, (u0 + j) % SPLIT, (e0 + j) % 4, xh, xl, cols)
            for j in range(n // 4 * 4, n):
                pe_tile(pe, u0 + j, e0 + j, (u0 + j) % SPLIT, (e0 + j) % 4, xh, xl, cols)

        def each_tile(eng, st, n, e0, u0, take, steps=0):
            def one(j, jj):
                eng.wait_ge(unit_done, u0 + j + 1)
                take(j, (e0 + jj) % 4).then_inc(banks_free, 1)
            eng.wait_ge(banks_free, 4 + e0)
            if n >= 4:
                base = st.n
                with eng.Fori(0, n // 4) as i:
                    for j in range(4):
                        st.n = base + (i * 4 + j) * steps
                        one(i * 4 + j, j)
                st.n = base + n // 4 * 4 * steps
            for j in range(n // 4 * 4, n):
                one(j, j)

        PLAN = []

        def stage(f, *args, **kw):
            PLAN.append((f, args, kw))

        class Linear:

            def __init__(self, name, dst=None, func=ACT.Copy, xh=None, xl=None, cols=S, n=None, ready=None, add=None,
                         scale=1.0, alpha=None, pre=(), squares=None, total=False, u_off=0):
                self.name, self.dst, self.func, self.cols = name, dst, func, cols
                self.xh, self.xl, self.ready, self.add, self.scale, self.alpha = xh, xl, ready, add, scale, alpha
                self.n = NU[name] if n is None else n
                self.pre, self.squares, self.total, self.u0 = pre, squares, total, U0[name] + u_off
                self.e0 = evac[0]
                evac[0] += self.n
                PLAN.append(self)

            def tensor(self, pe, st):
                pe_linear(pe, st, self.ready, self.u0, self.e0, self.xh, self.xl, self.cols, self.n)

            def scalar(self, act, st):
                if self.squares is not None:
                    for j in range(KT):
                        act.wait_ge(banks_free, 5 + self.e0 + j)
                        st.do(nc.scalar.activation(T(self.squares + j), X[:, j, :], ACT.Square), f"{self.name}.sq{j}")
                if self.add is not None:
                    return
                st.wait(*self.pre)
                st.settle()

                def take(j, b):
                    return nc.scalar.activation(self.dst(j), PS[:, b:b + 1, 0:self.cols], self.func, scale=self.scale)
                each_tile(act, st, self.n, self.e0, self.u0, take)

            def vector(self, dve, st):
                if self.add is None:
                    return
                st.settle()

                dve.wait_ge(banks_free, 4 + self.e0)
                for j in range(KT + 1):
                    if j < KT:
                        dve.wait_ge(unit_done, U0[self.name] + j + 1)
                        x, b = X[:, j, :], bank((self.e0 + j) % 4)
                        if self.alpha is None:
                            ins = nc.vector.tensor_tensor(x, x, b, ALU.add)
                        else:
                            ins = nc.vector.scalar_tensor_tensor(out=x, in0=x, scalar=self.alpha, in1=b, op0=ALU.mult, op1=ALU.add)
                        ins.then_inc(banks_free, 1)
                    if j >= 2 and (self.squares is not None or self.total):
                        term = lambda q: T(self.squares + q) if self.squares is not None else X[:, q, :]
                        if self.squares is not None:
                            st.wait(f"{self.name}.sq{j - 1}")
                        else:
                            dve.wait_ge(banks_free, 4 + self.e0 + j)
                        st.settle()
                        st.do(nc.vector.tensor_tensor(SD[:], term(0) if j == 2 else SD[:], term(j - 1), ALU.add), f"{self.name}.sum")

        class Pairs:

            def __init__(self, name, n, dst, func, of=0, yh=None, acc=None, ready=None, u_off=0, func2=None):
                self.name, self.n, self.dst, self.func, self.of, self.acc, self.ready = name, n, dst, func, of, acc, ready
                self.yh, self.u0, self.func2 = yh, U0[name] + u_off, func2
                self.e0 = evac[0]
                evac[0] += 2 * n
                PLAN.append(self)

            def tensor(self, pe, st):
                if self.ready is not None:
                    pe_start(pe, st, self.ready, self.u0, self.e0, [self.yh or (XH, XL), (XH, XL)])
                    for j in range(2, 4):
                        xh, xl = self.yh if (self.yh is not None and j % 2 == 0) else (XH, XL)
                        pe_tile(pe, self.u0 + j, self.e0 + j, (self.u0 + j) % SPLIT, (self.e0 + j) % 4, xh, xl, S)
                first = 0 if self.ready is None else 1
                if self.n // 2 == first:
                    return
                with pe.Fori(first, self.n // 2) as i:
                    for j in range(4):
                        xh, xl = self.yh if (self.yh is not None and j % 2 == 0) else (XH, XL)
                        pe_tile(pe, self.u0 + i * 4 + j, self.e0 + i * 4 + j, (self.u0 + j) % SPLIT, (self.e0 + j) % 4, xh, xl, S)

            def scalar(self, act, st):
                st.settle()
                base = st.n
                k = 1 if self.func2 is None else 2
                with act.Fori(0, self.n // 2) as i:
                    for j in range(2):
                        act.wait_ge(unit_done, self.u0 + i * 4 + 2 * j + 1 + self.of)
                        act.wait_ge(banks_free, self.e0 + 2 + i * 4 + 2 * j)
                        st.n = base + (i * 2 + j) * k
                        st.do(nc.scalar.activation(SG[:, j, :], bank((self.e0 + 2 * j + self.of) % 4), self.func))
                        if self.func2 is not None:
                            act.wait_ge(unit_done, self.u0 + i * 4 + 2 * j + 2 - self.of)
                            st.do(nc.scalar.activation(SG[:, 2 + j, :], bank((self.e0 + 2 * j + 1 - self.of) % 4), self.func2))
                st.n = base + self.n * k
                st.names[f"{self.name}.pairs{self.e0}"] = (scalar_steps, base)

            def vector(self, dve, st):
                st.settle()
                dve.wait_ge(banks_free, 4 + self.e0)
                k = 1 if self.func2 is None else 2
                base = st.names[f"{self.name}.pairs{self.e0}"][1]
                with dve.Fori(0, self.n // 2) as i:
                    for j in range(2):
                        dve.wait_ge(scalar_steps, base + (i * 2 + j + 1) * k)
                        dve.wait_ge(unit_done, self.u0 + i * 4 + 2 * j + 2)
                        other = PS[:, (self.e0 + 2 * j + 1 - self.of) % 4, :] if self.func2 is None else SG[:, 2 + j, :]
                        if self.acc is None:
                            nc.vector.tensor_tensor(self.dst(i * 2 + j), SG[:, j:j + 1, :] , other.rearrange("p (a b) -> p a b", a=1),
                                                    ALU.mult).then_inc(banks_free, 2)
                        else:
                            nc.vector.tensor_tensor(SG[:, j, :], SG[:, j, :], other, ALU.mult).then_inc(pair_products, 1)
                            dve.wait_ge(pair_products, self.acc + i * 2 + j + 1)
                            nc.vector.tensor_tensor(self.dst(i * 2 + j), self.dst(i * 2 + j), SG[:, j:j + 1, :],
                                                    ALU.add).then_inc(banks_free, 2)

        SG = sb("SG", [P, 4, S])
        pair_products = sem("pair_products")

        class TokenMajor:

            def __init__(self, name, halves, dst, xh=None, xl=None, tiles=TT, pre=(), h0=0, u_off=0):
                self.name, self.halves, self.dst, self.tiles, self.pre = name, halves, dst, tiles, pre
                self.xh, self.xl = (XH, XL) if xh is None else (xh, xl)
                self.e0, self.h0, self.u0 = evac[0], h0, U0[name] + 4 * h0 + u_off
                evac[0] += halves * tiles
                PLAN.append(self)

            def tensor(self, pe, st):
                for h in range(self.halves):
                    e = self.e0 + h * self.tiles
                    pe.wait_ge(banks_free, e + self.tiles)
                    for m in range(4):
                        u = self.u0 + 4 * h + m
                        pe.wait_ge(split_done, u + 1)
                        for kk in range(2):
                            k = 2 * m + kk
                            wh = WH[:, u % SPLIT, kk * S:(kk + 1) * S]
                            wl = WL[:, u % SPLIT, kk * S:(kk + 1) * S]
                            for t in range(self.tiles):
                                o = bank((e + t) % 4)
                                xh, xl = self.xh[:, k, t * P:(t + 1) * P], self.xl[:, k, t * P:(t + 1) * P]
                                mm(o, xh, wh, start=(k == 0), stop=False)
                                mm(o, xh, wl, start=False, stop=False)
                                last = mm(o, xl, wh, start=False, stop=(k == KT - 1))
                        last.then_inc(unit_done, 1)

            def scalar(self, act, st):
                st.wait(*self.pre)
                st.settle()
                act.wait_ge(banks_free, 4 + self.e0)
                for h in range(self.halves):
                    e = self.e0 + h * self.tiles
                    act.wait_ge(unit_done, self.u0 + 4 * h + 4)
                    for t in range(self.tiles):
                        nc.scalar.activation(self.dst(self.h0 + h, t), bank((e + t) % 4), ACT.Copy).then_inc(banks_free, 1)

            def vector(self, dve, st):
                pass

        class Down:

            def __init__(self, name, alpha=None):
                self.name, self.alpha, self.e0 = name, alpha, evac[0]
                evac[0] += KT
                PLAN.append(self)

            def hslot(self, k):
                return 4 + k % 4

            def tensor(self, pe, st):
                pe.wait_ge(banks_free, 4 + self.e0)
                u0 = U0[self.name]
                for k in range(NH):
                    pe.wait_ge(split_done, u0 + k + 1)
                    st.wait(f"{self.name}.lo{k}")
                    xh, xl = YH[:, self.hslot(k), :], YL[:, self.hslot(k), :]
                    for j in range(KT):
                        last = unit_passes(bank(j), WH[:, (u0 + k) % SPLIT, j * P:(j + 1) * P],
                                           WL[:, (u0 + k) % SPLIT, j * P:(j + 1) * P], xh, xl, k == 0, k == NH - 1)
                        if k == NH - 1 and j < KT - 1:
                            st.do(last, f"{self.name}.out{j}")
                    last.then_inc(unit_done, 1)

            def scalar(self, act, st):
                act.wait_ge(banks_free, 4 + self.e0)
                for k in range(NH):
                    if k >= 4:
                        act.wait_ge(unit_done, U0[self.name] + k - 3)
                        st.wait(f"{self.name}.lo{k - 4}")
                    st.do(nc.scalar.activation(YH[:, self.hslot(k), :], T(k), ACT.Copy), f"{self.name}.hi{k}")

            def vector(self, dve, st):
                dve.wait_ge(banks_free, 4 + self.e0)
                for k in range(NH):
                    st.wait(f"{self.name}.hi{k}")
                    st.do(nc.vector.tensor_tensor(YL[:, self.hslot(k), :], T(k), YH[:, self.hslot(k), :].bitcast(F32),
                                                  ALU.subtract), f"{self.name}.lo{k}")
                for j in range(KT):
                    if j < KT - 1:
                        st.wait(f"{self.name}.out{j}")
                    else:
                        dve.wait_ge(unit_done, U0[self.name] + NH)
                    if self.alpha is None:
                        nc.vector.tensor_tensor(X[:, j, :], X[:, j, :], bank(j), ALU.add).then_inc(banks_free, 1)
                    else:
                        nc.vector.scalar_tensor_tensor(out=X[:, j, :], in0=X[:, j, :], scalar=self.alpha, in1=bank(j),
                                                       op0=ALU.mult, op1=ALU.add).then_inc(banks_free, 1)

        class Stage:
            def __init__(self, **fns):
                self.fns = fns
                self.e = evac[0]
                PLAN.append(self)

            def run(self, role, eng, st):
                if role in self.fns:
                    st.settle()
                    self.fns[role](eng, st, self.e)

        def bcast(ap, n):
            return ap.to_broadcast([ap.shape[0], n])

        def colnorm(id, groups, n, eps, center, apply, sq, xc, sums=ones, cols=S, b0=4, summed=None, stream=False, arrive=None, squared=False):
            def src(g, k):
                i = sum(len(x) for x in groups[:g]) + k
                return xc(i) if center else groups[g][k]

            def tensor(pe, st, e):
                if not stream:
                    pe.wait_ge(banks_free, 4 + e)
                st.wait(*[id + ".in"] * (id + ".in" in names))
                if summed is not None:
                    st.wait(summed)
                    if center:
                        st.do(mm(bank(b0), sums, SD[:], start=True, stop=True), f"{id}.mean0")
                        squares(pe, st, 0)
                    else:
                        st.do(token_sums(0, SD[:], True, True), f"{id}.var0")
                    spread(st)
                    return
                for g, tiles in enumerate(groups):
                    if center:
                        if g >= 2:
                            st.wait(f"{id}.xc{sum(len(x) for x in groups[:g - 1]) - 1}")
                        for k, t in enumerate(tiles):
                            if stream:
                                pe.wait_ge(banks_free, e - KT + 5 + k)
                            if arrive is not None:
                                st.wait(arrive(k))
                            last = mm(bank(b0 + g % 2, cols), sums, t, start=(k == 0), stop=(k == len(tiles) - 1))
                        st.do(last, f"{id}.mean{g}")
                    if g >= 1 or not center:
                        squares(pe, st, g - 1 if center else g)
                if center:
                    squares(pe, st, len(groups) - 1)
                spread(st)

            heads = 1 if sums is ones else 2
            tiles_t = cols // P
            ncol = len(groups) * tiles_t * heads
            RS = SM[:, 104:104 + ncol]

            def token_sums(g, x, first, last):
                for t in range(tiles_t):
                    c = (g * tiles_t + t) * heads
                    ins = mm(PS[:, b0 + 2, c:c + heads], x[:, t * P:(t + 1) * P], sums[:, 0:P:P // heads],
                             start=(first and g == 0 and t == 0), stop=(last and g == len(groups) - 1 and t == tiles_t - 1))
                return ins

            def squares(pe, st, g):
                i0 = sum(len(x) for x in groups[:g])
                for k in range(len(groups[g])):
                    st.wait(f"{id}.sq{i0 + k}")
                    last = token_sums(g, sq(i0 + k), k == 0, k == len(groups[g]) - 1)
                st.do(last, f"{id}.var{g}")

            def spread(st):
                st.wait(f"{id}.inv")
                for g in range(len(groups)):
                    if g >= 2:
                        st.wait(f"{id}.rstd{g - 2}")
                    for t in range(tiles_t):
                        for q in range(heads):
                            c = (g * tiles_t + t) * heads + q
                            rows = P // heads
                            last = mm(PS[q * rows:(q + 1) * rows, 4 + g % 2, t * P:(t + 1) * P], bcast(RS[:, c:c + 1], rows), ident,
                                      start=True, stop=True)
                    st.do(last, f"{id}.rep{g}")

            def scalar(act, st, e):
                if not stream:
                    act.wait_ge(banks_free, 4 + e)
                st.wait(*[id + ".in"] * (id + ".in" in names))
                i = 0
                for g, tiles in enumerate(groups):
                    for k in range(len(tiles)):
                        if squared or (summed is not None and not center):
                            continue
                        if stream:
                            act.wait_ge(banks_free, e - KT + 5 + k)
                        if arrive is not None:
                            st.wait(arrive(k))
                        if center:
                            st.wait(f"{id}.xc{i}")
                        st.do(nc.scalar.activation(sq(i), src(g, k), ACT.Square), f"{id}.sq{i}")
                        i += 1
                st.wait(f"{id}.var{len(groups) - 1}")
                st.do(nc.scalar.activation(RS, PS[:, b0 + 2, 0:ncol], ACT.Sqrt, bias=cst(eps), scale=1.0 / n), f"{id}.std")

            def vector(dve, st, e):
                dve.wait_ge(banks_free, 4 + e)
                i = 0
                if center:
                    for g, tiles in enumerate(groups):
                        st.wait(f"{id}.mean{g}")
                        for k, t in enumerate(tiles):
                            st.do(nc.vector.scalar_tensor_tensor(out=xc(i), in0=bank(b0 + g % 2, cols), scalar=-1.0 / n,
                                                                 in1=t, op0=ALU.mult, op1=ALU.add), f"{id}.xc{i}")
                            i += 1
                st.wait(f"{id}.std")
                st.do(nc.vector.reciprocal(RS, RS), f"{id}.inv")
                for g, tiles in enumerate(groups):
                    st.wait(f"{id}.rep{g}")
                    for k in range(len(tiles)):
                        apply(st, g, k, src(g, k), bank(4 + g % 2, cols))
                    st.settle()
                    names[f"{id}.rstd{g}"] = (vector_steps, st.n)

            Stage(tensor=tensor, scalar=scalar, vector=vector)

        NR = sb("NR", [P, 2, S])

        def split(id, tiles, hi, lo, ready=None):
            def scalar(act, st, e):
                for k, t in enumerate(tiles):
                    if ready is not None:
                        st.wait(ready(k))
                    st.do(nc.scalar.activation(hi[:, k, :], t, ACT.Copy), f"{id}.hi{k}")

            def vector(dve, st, e):
                st.settle()
                for k, t in enumerate(tiles):
                    st.wait(f"{id}.hi{k}")
                    st.do(nc.vector.tensor_tensor(lo[:, k, :], t, hi[:, k, :].bitcast(F32), ALU.subtract), f"{id}.lo{k}")
                names[f"{id}.ready"] = (vector_steps, st.n)
            Stage(scalar=scalar, vector=vector)

        def split_hi_tiles(id, tiles, hi, ready, bias=None):
            def scalar(act, st, e):
                for k, t in enumerate(tiles):
                    st.wait(ready(k))
                    if bias is not None:
                        st.do(nc.scalar.activation(t, t, ACT.Identity, bias=vec(bias, k)), f"{id}.biased{k}")
                        st.settle()
                    st.do(nc.scalar.activation(hi[:, k, :], t, ACT.Copy), f"{id}.hi{k}")
            Stage(scalar=scalar)

        def split_lo_tile(st, id, k, t, hi, lo):
            st.wait(f"{id}.hi{k}")
            st.do(nc.vector.tensor_tensor(lo[:, k, :], t, hi[:, k, :].bitcast(F32), ALU.subtract), f"{id}.lo{k}")

        def rmsnorm(id, gain, src=None, hi=None, lo=None, cols=S, s0=0, summed=None, stream=False, arrive=None, squared=False):
            src = [X[:, k, :] for k in range(KT)] if src is None else src
            hi, lo = (XH, XL) if hi is None else (hi, lo)
            if cols == S:
                sq = lambda i: T(s0 + i)
            else:
                v = A[:, s0:s0 + 4, :].rearrange("p a (b c) -> p (a b) c", c=cols)
                sq = lambda i: v[:, i, :]

            def apply(st, g, k, x, rstd):
                st.do(nc.vector.scalar_tensor_tensor(out=sq(k), in0=x, scalar=vec(gain, k), in1=rstd,
                                                     op0=ALU.mult, op1=ALU.mult), f"{id}.y{k}")
                if k >= 1:
                    split_lo_tile(st, id, k - 1, sq(k - 1), hi, lo)
                if k == KT - 1:
                    split_lo_tile(st, id, k, sq(k), hi, lo)
            colnorm(id, [src], D, "eps6", False, apply, sq, None, cols=cols, summed=summed, stream=stream,
                    arrive=arrive, squared=squared, b0=-2 if stream else 4)
            split_hi_tiles(id, [sq(k) for k in range(KT)], hi, ready=lambda k: f"{id}.y{k}")

        def layernorm(id, gain, bias, split_it=True, summed=None, stream=False, arrive=None):
            def apply(st, g, k, x, rstd):
                st.do(nc.vector.scalar_tensor_tensor(out=X[:, k, :], in0=x, scalar=vec(gain, k), in1=rstd,
                                                     op0=ALU.mult, op1=ALU.mult), f"{id}.y{k}")
                if split_it and k >= 2:
                    split_lo_tile(st, id, k - 2, X[:, k - 2, :], XH, XL)
                if split_it and k == KT - 1:
                    split_lo_tile(st, id, k - 1, X[:, k - 1, :], XH, XL)
                    split_lo_tile(st, id, k, X[:, k, :], XH, XL)
            tiles = [X[:, k, :] for k in range(KT)]
            colnorm(id, [tiles], D, "eps5", True, apply, lambda i: T(i), lambda i: T(8 + i), summed=summed, stream=stream,
                    arrive=arrive, b0=0 if stream else 5)
            if split_it:
                split_hi_tiles(id, tiles, XH, ready=lambda k: f"{id}.y{k}", bias=bias)
            else:
                def scalar(act, st, e):
                    for k, t in enumerate(tiles):
                        st.wait(f"{id}.y{k}")
                        st.do(nc.scalar.activation(t, t, ACT.Identity, bias=vec(bias, k)), f"{id}.biased{k}")
                Stage(scalar=scalar)

        class Attention:

            def __init__(self, id, heads, keys, score, value, outd, dst, comps=1, scale=1.0, ptile=0, nkeys=4, lam=None, nsub=1, prob=None, pt=None):
                self.id, self.heads, self.keys, self.score, self.value, self.outd, self.dst = id, heads, keys, score, value, outd, dst
                self.comps, self.scale, self.nkeys, self.lam, self.nsub = comps, scale, nkeys, lam, nsub
                self.ptiles = (lambda n: A[:, ptile + n, :]) if prob is None else prob
                pt0 = ptile + 8 if pt is None else pt
                self.pts = [A[:, pt0:pt0 + 4, :], SG]
                self.e = evac[0]
                PLAN.append(self)

            def prob(self, n, i):
                return self.ptiles(4 * (n % (2 * self.comps)) + i)[:, 0:self.keys(i) * P]

            def tensor(self, pe, st):
                pe.wait_ge(banks_free, 4 + self.e)
                st.wait(*[self.id + ".in"] * (self.id + ".in" in names))
                n = self.heads * self.comps
                for m in range(n + 1):
                    if m < n:
                        for i in range(TT):
                            if m >= 1:
                                st.wait(f"{self.id}.exp{m - 1}.{i}")
                            last = self.score(m // self.comps, m % self.comps, i, bank(i, self.keys(i) * P))
                            st.do(last, f"{self.id}.sc{m}.{i}")
                    if m >= 1 and m % self.comps == 0:
                        h = m // self.comps - 1
                        for i in range(TT):
                            st.wait(f"{self.id}.prob{h}.{i}")
                            if i >= 2:
                                st.wait(f"{self.id}.pt{h}.{i - 2}")
                            elif h >= 1:
                                st.wait(f"{self.id}.pt{h - 1}.{i + 2}")
                            for j in range(self.keys(i)):
                                last = nc.tensor.transpose(PS[:, 4 + i % 2, j * P:(j + 1) * P],
                                                           self.ptiles(4 * (self.comps * (h % 2)) + i)[:, j * P:(j + 1) * P], ident)
                            st.do(last, f"{self.id}.tr{h}.{i}")
                        if h >= 1:
                            self.outputs(st, h - 1)
                self.outputs(st, self.heads - 1)

            def outputs(self, st, h):
                for i in range(TT):
                    st.wait(f"{self.id}.pt{h}.{i}")
                for s in range(self.nsub):
                    ob = 6 + (h * self.nsub + s) % 2
                    if h * self.nsub + s >= 2:
                        q = h * self.nsub + s - 2
                        st.wait(f"{self.id}.o{q // self.nsub}.{q % self.nsub}")
                    base, rows = self.outd(h)
                    for j in range(self.nkeys):
                        c0 = j * P if self.nkeys == TT and self.keys(0) == 1 else 0
                        last = mm(PS[base:base + rows, ob, c0:S], self.value(h, j, s), self.pts[h % 2][:, j, c0:S],
                                  start=(j == 0), stop=(j == self.nkeys - 1))
                    st.do(last, f"{self.id}.pv{h}.{s}")

            def scalar(self, act, st):
                st.settle()
                n = self.heads * self.comps
                for m in range(n + 1):
                    if m < n:
                        for i in range(TT):
                            st.wait(f"{self.id}.max{m}.{i}")
                            if m >= 2 * self.comps:
                                st.wait(f"{self.id}.tr{m // self.comps - 2}.{i}")
                            st.do(nc.scalar.activation(self.prob(m, i), bank(i, self.keys(i) * P), ACT.Exp,
                                                       bias=SM[:, (m % 2) * 4 + i:(m % 2) * 4 + i + 1], scale=self.scale,
                                                       accum_out=SM[:, 8 + (m % 2) * 4 + i:9 + (m % 2) * 4 + i]), f"{self.id}.exp{m}.{i}")
                    if m >= 1 and m % self.comps == 0:
                        h = m // self.comps - 1
                        for i in range(TT):
                            st.wait(f"{self.id}.tr{h}.{i}")
                            if h >= 2 and i == 0:
                                st.wait(f"{self.id}.pv{h - 2}.{self.nsub - 1}")
                            kk = self.keys(i)
                            st.do(nc.scalar.activation(self.pts[h % 2][:, 0:kk, i * P:(i + 1) * P],
                                                       PS[:, 4 + i % 2, 0:kk * P].rearrange("p (a b) -> p a b", b=P), ACT.Copy),
                                  f"{self.id}.pt{h}.{i}")

            def vector(self, dve, st):
                st.settle()
                n = self.heads * self.comps
                for m in range(n + 1):
                    if m < n:
                        for i in range(TT):
                            st.wait(f"{self.id}.sc{m}.{i}")
                            mx = SM[:, (m % 2) * 4 + i:(m % 2) * 4 + i + 1]
                            st.settle()
                            st.do(nc.vector.tensor_reduce(mx, bank(i, self.keys(i) * P), AX.X, ALU.max, negate=True))
                            if self.scale != 1.0:
                                st.settle()
                                st.do(nc.vector.tensor_scalar(mx, mx, self.scale, None, ALU.mult))
                            names[f"{self.id}.max{m}.{i}"] = (vector_steps, st.n)
                        for i in range(TT):
                            st.wait(f"{self.id}.exp{m}.{i}")
                            c, h = m % self.comps, m // self.comps
                            s = SM[:, 8 + (m % 2) * 4 + i:9 + (m % 2) * 4 + i]
                            r = SM[:, 16 + (m % 2) * 4 + i:17 + (m % 2) * 4 + i]
                            st.settle()
                            st.do(nc.vector.reciprocal(r, s))
                            st.settle()
                            if self.comps == 1:
                                st.do(nc.vector.tensor_scalar(self.prob(m, i), self.prob(m, i), r, None, ALU.mult), f"{self.id}.prob{h}.{i}")
                            elif c == 0:
                                st.do(nc.vector.tensor_scalar(self.prob(m, i), self.prob(m, i), r, None, ALU.mult))
                            else:
                                st.do(nc.vector.tensor_scalar(self.prob(m, i), self.prob(m, i), r, self.lam, ALU.mult, ALU.mult))
                                st.settle()
                                st.do(nc.vector.tensor_tensor(self.prob(m - 1, i), self.prob(m - 1, i), self.prob(m, i), ALU.subtract),
                                      f"{self.id}.prob{h}.{i}")
                    if m >= 1 and m % self.comps == 0:
                        h = m // self.comps - 1
                        if h >= 1:
                            self.take(st, h - 1)
                self.take(st, self.heads - 1)
                names[f"{self.id}.done"] = (vector_steps, st.n)

            def take(self, st, h):
                for s in range(self.nsub):
                    st.wait(f"{self.id}.pv{h}.{s}")
                    base, rows = self.outd(h)
                    ob = 6 + (h * self.nsub + s) % 2
                    st.do(nc.vector.tensor_copy(self.dst(h, s), PS[base:base + rows, ob, :]), f"{self.id}.o{h}.{s}")

        def at(i):
            return lambda j: A[:, bass.ds(i + j, 1), :]

        def mark(name, engine="vector"):
            def f(eng, st, e):
                names[name] = (st.sem, st.n)
            Stage(**{engine: f})

        def free_until(*roles):
            def f(eng, st, e):
                eng.wait_ge(banks_free, 4 + e)
            Stage(**{r: f for r in roles})

        nload = [0]

        def dma(id, dst, src, ready=(), settle=True):
            k = nload[0]
            nload[0] += 1

            def f(act, st, e):
                act.wait_ge(banks_free, 4 + e)
                st.wait(*ready)
                act.dma_start(dst, src).then_inc(loads[k], 16)
                names[id] = (loads[k], 16)
            Stage(scalar=f)

        def vs(f):
            Stage(vector=lambda dve, st, e: (dve.wait_ge(banks_free, 4 + e), f(st)))

        v, a_ = nc.vector, nc.scalar

        def xattn(l):
            KM = A[:, 20:24, :].rearrange("p a (b c) -> p (a b) c", c=MEM)
            rmsnorm(f"xn{l}", f"norm_xattn{l}", summed=("l0.out.sum", "l1.out.sum")[l])
            def early(act, st, e):
                act.wait_ge(banks_free, 4 + e)
                st.wait(f"x{l}.clear")
                if l == 0:
                    st.do(a_.activation(A[:, 20:22, :], SG[:, 0:2, :], ACT.Copy))
                for t in range(2):
                    st.do(a_.activation(T(24 + 2 * t), SG[:, 2 + t, :], ACT.Copy), f"x{l}.early")
            Stage(scalar=early)
            k0 = 4 if l == 0 else 0
            Linear(f"x{l}.k", dst=lambda j: KM[:, bass.ds(j + k0, 1), :], xh=MH, xl=ML, cols=MEM)
            TokenMajor(f"x{l}.v", 1, lambda h, t: T(24 + 2 * t + h), MH, ML, tiles=2, h0=1, u_off=-4)
            Linear(f"x{l}.q", dst=at(12), ready=f"xn{l}")

            def score(h, c, i, out):
                for d in range(2):
                    last = mm(out, T(12 + 2 * h + d)[:, i * P:(i + 1) * P], KM[:, 2 * h + d, :], start=(d == 0), stop=(d == 1))
                return last
            Attention(f"xa{l}", 4, lambda i: 2, score, lambda h, j, s: W2(24 + 2 * j, 2)[:, h * 256 + s * P:h * 256 + (s + 1) * P],
                      lambda h: (0, P), lambda h, s: T(28 + 2 * h + s), scale=1.0 / 16, nkeys=2, nsub=2)
            split(f"xo{l}", [T(28 + k) for k in range(KT)], XH, XL, ready=lambda k: f"xa{l}.o{k // 2}.{k % 2}")
            Linear(f"x{l}.o", add=True, ready=f"xo{l}", squares=0)

        def early_values(l):
            TokenMajor(f"x{l}.va", 1, lambda h, t: SG[:, 2 + t, :], MH, ML, tiles=2)

        def ffn(l, alpha=None):
            Pairs(f"f{l}.up", NH, at(0), ACT.Silu, ready=f"fn{l}")
            Down(f"f{l}.down", alpha)

        dma("reset0", T(36), io["reset"])
        memt = A[:, 28:32, :].rearrange("p a (b c) -> p (a b) c", c=MEM)
        rmsnorm("n0", "norm_mix0")
        LB = 24

        def lower_bounds(st):
            r = [vec("lb", 4 * i, 4) for i in range(3)]
            m = SM[:, LB + 12:LB + 16]
            st.do(v.tensor_tensor(m, r[0], r[1], ALU.max))
            st.settle()
            st.do(v.tensor_tensor(m, m, r[2], ALU.max))
            st.settle()
            for i in range(3):
                st.do(v.tensor_tensor(SM[:, LB + 4 * i:LB + 4 * i + 4], r[i], m, ALU.subtract), "lb.centred")
        vs(lower_bounds)

        def lb_exp(act, st, e):
            st.wait("lb.centred")
            st.do(a_.activation(SM[:, LB:LB + 12], SM[:, LB:LB + 12], ACT.Exp), "lb.exp")
        Stage(scalar=lb_exp)

        def lb_ratio(st):
            st.wait("lb.exp")
            m = SM[:, LB + 12:LB + 16]
            st.do(v.tensor_tensor(m, SM[:, LB:LB + 4], SM[:, LB + 4:LB + 8], ALU.add))
            st.settle()
            st.do(v.tensor_tensor(m, m, SM[:, LB + 8:LB + 12], ALU.add))
            st.settle()
            st.do(v.reciprocal(m, m))
            st.settle()
            st.do(v.tensor_tensor(SM[:, LB:LB + 4], SM[:, LB:LB + 4], m, ALU.mult))
            st.settle()
            st.do(v.tensor_scalar(SM[:, LB + 4:LB + 8], SM[:, LB:LB + 4], -1.0, 1.0, ALU.mult, ALU.add))
        vs(lb_ratio)

        def mem_squares(act, st, e):
            act.wait_ge(mem_loaded, 16)
            sq = A[:, 32:36, :].rearrange("p a (b c) -> p (a b) c", c=MEM)
            for k in range(KT):
                st.do(a_.activation(sq[:, k, :], memt[:, k, :], ACT.Square), f"mem.sq{k}")
        Stage(scalar=mem_squares)
        Pairs("l0.glu", 2, at(0), ACT.Sigmoid, of=1, ready="n0")
        rmsnorm("mem", "mem_norm", src=[memt[:, k, :] for k in range(KT)], hi=MH, lo=ML, cols=MEM, s0=32, squared=True)
        Pairs("l0.glu", 2, at(2), ACT.Sigmoid, of=1, u_off=4)

        def depthwise(st, src, dst, taps, w, b, n, k0=0, first=None, last=0):
            for k in range(n if first is None else 0):
                x, y = src(k), dst(k)
                st.do(v.tensor_scalar(y, x, vec(w, (k0 + k) * taps + taps - 1), vec(b, k) if b else 0.0, ALU.mult, ALU.add))
            for t in range(taps - 2 if first is None else first, last - 1, -1):
                sh = taps - 1 - t
                st.settle()
                for k in range(n):
                    x, y = src(k), dst(k)
                    st.do(v.scalar_tensor_tensor(out=y[:, sh:], in0=x[:, :S - sh], scalar=vec(w, (k0 + k) * taps + t),
                                                 in1=y[:, sh:], op0=ALU.mult, op1=ALU.add))

        def conv(st, first, last):
            depthwise(st, lambda k: T(k), lambda k: T(4 + k), 31, "conv_dw_w", "conv_dw_b", 4, first=first, last=last)
        HALF = 15
        vs(lambda st: conv(st, None, HALF))
        Linear("l0.q", dst=at(8), func=ACT.Silu)
        Linear("l0.f", dst=at(12), func=ACT.Sigmoid)
        def h_gates(st):
            st.settle()
            for h in range(4):
                st.do(v.tensor_scalar(T(12 + h), T(12 + h), SM[:, LB + 4 + h:LB + 5 + h], SM[:, LB + h:LB + h + 1], ALU.mult, ALU.add))
            st.settle()
            st.do(v.tensor_scalar(W2(32, 4), W2(12, 4), -1.0, 1.0, ALU.mult, ALU.add), "h.f")
        vs(h_gates)

        def h_ln(act, st, e):
            st.wait("h.f")
            st.do(a_.activation(W2(12, 4), W2(12, 4), ACT.Ln), "h.ln")
        Stage(scalar=h_ln)
        SGW = SG[:].rearrange("p a b -> p (a b)")
        SGc = SGW.rearrange("p (c t) -> p c t", t=64)
        chunks = lambda i, n: W2(i, n).rearrange("p (c t) -> p c t", t=64)

        def h_cum(st):
            st.wait("h.ln", "reset0")
            for h in range(4):
                st.do(v.tensor_tensor_scan(T(24 + h), T(36), T(12 + h), 0.0, ALU.mult, ALU.add), "h.cum")
            st.settle()
            last = chunks(24, 4)[:, :, 63:64].to_broadcast([P, 32, 64])
            st.do(v.tensor_tensor(SGc, last, chunks(24, 4), ALU.subtract), "h.kd")
            st.do(v.memset(W2(12, 4), 0.0))
        vs(h_cum)

        def h_exps(act, st, e):
            st.wait("h.cum")
            st.do(a_.activation(W2(28, 4), W2(24, 4), ACT.Exp), "h.e")
            st.wait("h.kd")
            st.do(a_.activation(SGW, SGW, ACT.Exp), "h.ekd")
            st.settle()
            st.do(a_.activation(W2(24, 4), W2(24, 4), ACT.Exp, scale=-1.0), "h.en")
        Stage(scalar=h_exps)
        DEC = 48

        def h_query(st):
            st.wait("h.e")
            st.do(v.tensor_copy(SM[:, DEC:DEC + 32].rearrange("p (a b) -> p a b", b=1), chunks(28, 4)[:, :, 63:64]))
            st.do(v.tensor_tensor(W2(8, 4), W2(8, 4), W2(28, 4), ALU.mult))
            conv(st, HALF - 1, 0)
        vs(h_query)
        Linear("l0.i", dst=at(16))
        Linear("l0.g", dst=at(20), func=ACT.Silu)

        def h_scaled(dve, st, e):
            st.wait("h.en")
            st.do(v.tensor_tensor(W2(0, 4), SGW, W2(32, 4), ALU.mult), "h.kd_done")
            st.settle()
            st.do(v.tensor_tensor(W2(32, 4), W2(32, 4), W2(24, 4), ALU.mult), "h.scaled")
        Stage(vector=h_scaled)

        SGK = SG[:, 0:2, :].rearrange("p a (b c) -> p (a b) c", c=MEM)
        Stage(tensor=lambda pe, st, e: st.wait("mem.lo7"))
        Linear("x0.ka", dst=lambda j: SGK[:, bass.ds(j, 1), :], xh=MH, xl=ML, cols=MEM, pre=["h.kd_done"])

        def h_turn_pe(pe, st, e):
            pe.wait_ge(banks_free, 4 + e)
            st.wait("h.scaled")
            for n in range(8):
                h, src = n // 2, (16, 0)[n % 2]
                if n >= 2:
                    st.wait(f"h.turned{n - 2}")
                for t in range(TT):
                    last = nc.tensor.transpose(PS[:, n % 2, t * P:(t + 1) * P], T(src + h)[:, t * P:(t + 1) * P], ident)
                st.do(last, f"h.turn{n}")

        def h_turn_act(act, st, e):
            for n in range(8):
                st.wait(f"h.turn{n}")
                st.do(a_.activation(T((28, 24)[n % 2] + n // 2), bank(n % 2), ACT.Copy), f"h.turned{n}")
        Stage(tensor=h_turn_pe, scalar=h_turn_act)

        def h_pe(pe, st, e):
            def inner(h):
                if h >= 2:
                    st.wait(f"h.att{h - 2}")
                elif h == 0:
                    st.wait("h.turned7")
                for t in range(TT):
                    c = slice(t * P, (t + 1) * P)
                    last = mm(PS[:, h % 2, c], T(32 + h)[:, c], T(8 + h)[:, c], start=True, stop=True)
                st.do(last, f"h.qk{h}")
                if h >= 2:
                    st.wait(f"h.state{h - 2}")
                for c in range(8):
                    b, t = 64 * (c % 2), c // 2
                    last = mm(PS[:, 2 + 2 * (h % 2) + c % 2, (c // 2) * P:(c // 2 + 1) * P], A[b:b + 64, 24 + h, t * P:(t + 1) * P],
                              A[b:b + 64, 28 + h, t * P:(t + 1) * P], start=True, stop=True)
                st.do(last, f"h.kv{h}")

            def outer(h):
                st.wait(f"h.att{h}", f"h.state{h}")
                if h >= 2:
                    st.wait(f"h.out{h - 2}")
                for t in range(TT):
                    c = slice(t * P, (t + 1) * P)
                    last = mm(PS[:, 6 + h % 2, c], T(28 + h)[:, c], T(12 + h)[:, c], start=True, stop=(t == 0 and False))
                    for q in range(2):
                        n = 2 * t + q
                        if n:
                            last = mm(PS[:, 6 + h % 2, n * 64:(n + 1) * 64], W2(2 * (h % 2), 2)[:, n * P:(n + 1) * P],
                                      T(8 + h)[:, n * 64:(n + 1) * 64], start=False, stop=(q == 1))
                st.do(last, f"h.o{h}")
            inner(0)
            for h in range(4):
                if h < 3:
                    inner(h + 1)
                outer(h)

        def h_vec(dve, st, e):
            for h in range(4):
                st.wait(f"h.qk{h}")
                for t in range(TT):
                    c = slice(t * P, (t + 1) * P)
                    st.do(v.copy_predicated(T(12 + h)[:, c], cst("chunkT").bitcast(U32), PS[:, h % 2, c]), f"h.att{h}")
                st.wait(f"h.kv{h}")
                if h >= 2:
                    st.wait(f"h.o{h - 2}")
                S2 = W2(2 * (h % 2), 2)
                kv = lambda c: PS[:, 2 + 2 * (h % 2) + c % 2, (c // 2) * P:(c // 2 + 1) * P]
                st.settle()
                st.do(v.tensor_copy(S2[:, P:2 * P], kv(0)))
                for c in range(1, 7):
                    st.settle()
                    st.do(v.scalar_tensor_tensor(out=S2[:, (c + 1) * P:(c + 2) * P], in0=S2[:, c * P:(c + 1) * P],
                                                 scalar=SM[:, DEC + 8 * h + c:DEC + 8 * h + c + 1], in1=kv(c),
                                                 op0=ALU.mult, op1=ALU.add))
                names[f"h.state{h}"] = (vector_steps, st.n)

        def h_act(act, st, e):
            for h in range(4):
                st.wait(f"h.o{h}")
                st.do(a_.activation(T(16 + h), bank(6 + h % 2), ACT.Copy), f"h.out{h}")
        Stage(tensor=h_pe, vector=h_vec, scalar=h_act)
        mark("ho.in", "scalar")

        def h_apply(st, g, k, x, rstd):
            st.do(v.scalar_tensor_tensor(out=x, in0=x, scalar=vec("hgrn_out_norm", g), in1=rstd, op0=ALU.mult, op1=ALU.mult))
            st.settle()
            st.do(v.tensor_tensor(x, x, T(20 + g), ALU.mult), f"y0.{g}")
        colnorm("ho", [[T(16 + h)] for h in range(4)], P, "eps6", False, h_apply, lambda i: T(24 + i), None)

        early_values(0)

        def c_apply(st, g, k, x, rstd):
            st.do(v.scalar_tensor_tensor(out=x, in0=x, scalar=vec("conv_ln_g", k), in1=rstd, op0=ALU.mult, op1=ALU.mult), f"cl.y{k}")
        colnorm("cl", [[T(4 + k) for k in range(4)]], 512, "eps6", True, c_apply, lambda i: T(24 + i), lambda i: T(8 + i), b0=0)

        def c_silu(act, st, e):
            for k in range(4):
                st.wait(f"cl.y{k}")
                st.do(a_.activation(T(8 + k), T(8 + k), ACT.Silu, bias=vec("conv_ln_b", k)), f"y0.{4 + k}")
        Stage(scalar=c_silu)
        split("y0", [T(16 + k) for k in range(4)] + [T(8 + k) for k in range(4)], XH, XL, ready=lambda k: f"y0.{k}")
        mark("x0.clear", "vector")
        Linear("l0.out", add=True, ready="y0", squares=0)
        xattn(0)
        rmsnorm("fn0", "norm_ffn0", summed="x0.o.sum")
        ffn(0)

        rmsnorm("n1", "norm_mix1", s0=24, stream=True)
        dma("sgu_w", T(36), io["sguw"])
        dma("sgu_b", T(37)[0:1, :], io["sgub"])
        Linear("l1.qk", dst=at(12), ready="n1", pre=["n1.lo7"])
        TokenMajor("l1.v", 1, lambda h, t: T(20 + t))
        Linear("l1.uz", dst=at(24), func=ACT.Gelu)

        def causal_score(q0, k0):
            def score(h, c, i, out):
                b = 64 * (h % 2)
                mm(out, A[b:b + 64, q0 + h // 2, i * P:(i + 1) * P], A[b:b + 64, k0 + h // 2, 0:(i + 1) * P], start=True, stop=False)
                return mm(out[:, i * P:(i + 1) * P], ident, cst("cadd"), start=False, stop=True)
            return score
        Attention("moba", 8, lambda i: i + 1, causal_score(12, 16), lambda h, j, s: T(20 + j)[:, h * 64:(h + 1) * 64],
                  lambda h: (64 * (h % 2), 64), lambda h, s: A[64 * (h % 2):64 * (h % 2) + 64, 32 + h // 2, :], scale=0.125)

        def z_apply(st, g, k, x, rstd):
            st.do(v.scalar_tensor_tensor(out=x, in0=x, scalar=vec("sgu_ln_g", g), in1=rstd, op0=ALU.mult, op1=ALU.mult))
            st.settle()
            st.do(v.tensor_scalar(x, x, vec("sgu_ln_b", g), None, ALU.add), f"z.{g}")
        colnorm("zn", [[T(28 + g)] for g in range(4)], P, "eps6", True, z_apply, lambda i: T(16 + i), lambda i: T(12 + i), b0=0)

        def sgu_mask(st):
            st.wait("sgu_w")
            for g in range(4):
                st.do(v.tensor_tensor(T(36)[:, g * P:(g + 1) * P], T(36)[:, g * P:(g + 1) * P], cst("causalT"), ALU.mult), "sgu.w")
        vs(sgu_mask)

        def sgu_pe(pe, st, e):
            for g in range(4):
                st.wait(f"z.{g}")
                if g >= 2:
                    st.wait(f"z.copied{g - 2}")
                for t in range(TT):
                    last = nc.tensor.transpose(PS[:, 6 + g % 2, t * P:(t + 1) * P], T(12 + g)[:, t * P:(t + 1) * P], ident)
                st.do(last, f"z.turned{g}")
            st.wait("sgu.w", "sgu_b")
            for g in range(4):
                st.wait(f"z.copied{g}")
                if g >= 2:
                    st.wait(f"z.mixed{g - 2}")
                for t in range(TT):
                    o = PS[:, 4 + g % 2, t * P:(t + 1) * P]
                    mm(o, T(16 + g)[:, t * P:(t + 1) * P], T(36)[:, g * P:(g + 1) * P], start=True, stop=False)
                    last = mm(o, ones[0:1, :], T(37)[0:1, g * P:(g + 1) * P], start=False, stop=True)
                st.do(last, f"z.mix{g}")

        def sgu_act(act, st, e):
            for g in range(4):
                st.wait(f"z.turned{g}")
                st.do(a_.activation(T(16 + g), bank(6 + g % 2), ACT.Copy), f"z.copied{g}")

        def sgu_dve(dve, st, e):
            for g in range(4):
                st.wait(f"z.mix{g}")
                st.do(v.tensor_tensor(T(24 + g), T(24 + g), bank(4 + g % 2), ALU.mult), f"z.mixed{g}")
        Stage(tensor=sgu_pe, scalar=sgu_act, vector=sgu_dve)
        early_values(1)
        split("y1", [T(32 + k) for k in range(4)] + [T(24 + k) for k in range(4)], XH, XL,
              ready=lambda k: "moba.done" if k < 4 else f"z.mixed{k - 4}")
        mark("x1.clear", "vector")
        Linear("l1.out", add=True, ready="y1", squares=0)
        xattn(1)
        rmsnorm("fn1", "norm_ffn1", summed="x1.o.sum")
        ffn(1)

        def to_residual(id, gain):
            def apply(st, g, k, x, rstd):
                st.do(v.scalar_tensor_tensor(out=X[:, k, :], in0=x, scalar=vec(gain, k), in1=rstd, op0=ALU.mult, op1=ALU.mult), f"{id}.x{k}")
            return apply
        allx = [X[:, k, :] for k in range(KT)]
        colnorm("end1", [allx], D, "eps6", False, to_residual("end1", "final_norm"), lambda i: T(24 + i), None, stream=True, b0=-2)

        layernorm("li", "ln_in_g", "ln_in_b", arrive=lambda k: f"end1.x{k}")
        dma("spill", io["spill"], X[:], ready=["li.lo7"])
        dma("onehot", T(30)[0:32, 0:384], io["onehot"], ready=["li.lo7"])
        dma("rel", T(31)[0:32, 0:4], io["rel"])
        dma("lamv", T(29)[:, 0:256], io["lam"])
        Linear("s.q", dst=at(12), ready="li", pre=["li.lo7"], scale=0.125)
        Linear("s.k", dst=at(16))
        TokenMajor("s.v", 1, lambda h, t: T(20 + t))

        def t5_pe(pe, st, e):
            st.wait("onehot", "rel")
            pe.wait_ge(banks_free, 4 + e)
            st.do(mm(PS[0:4, 0, 0:384], T(31)[0:32, 0:4], T(30)[0:32, 0:384], start=True, stop=True), "t5.g")

        def t5_act(act, st, e):
            st.wait("t5.g")
            st.do(a_.activation(T(28)[0:4, 0:384], PS[0:4, 0, 0:384], ACT.Copy), "t5.row")
        Stage(tensor=t5_pe, scalar=t5_act)
        dma("t5.out", TAB, T(28)[0:4, 0:384], ready=["t5.row"])
        BT = W2(36, 2).rearrange("p (h c) -> p h c", h=4)
        dma("t5.in", BT, bass.AP(tensor=TAB.tensor, offset=0, ap=[[1, P], [384, 4], [1, 256]]), ready=["t5.out"])

        def t5_mask(st):
            st.wait("t5.in")
            for h in range(4):
                st.do(v.tensor_tensor(BT[:, h, P:2 * P], BT[:, h, P:2 * P], cst("caddR"), ALU.add), "t5.masked")
        LAM = 40

        def lam_dots(st):
            st.wait("lamv")
            st.do(v.tensor_tensor(T(29)[:, 256:384].rearrange("p (a b) -> p a b", b=64), T(29)[:, 0:256].rearrange("p (a c b) -> p a c b", c=2, b=64)[:, :, 0, :],
                                  T(29)[:, 0:256].rearrange("p (a c b) -> p a c b", c=2, b=64)[:, :, 1, :], ALU.mult))
            st.settle()
            st.do(v.tensor_reduce(SM[:, LAM:LAM + 2], T(29)[:, 256:384].rearrange("p (a b) -> p a b", b=64), AX.X, ALU.add), "lam.dots")
        vs(lam_dots)

        def lam_exp(act, st, e):
            st.wait("lam.dots")
            st.do(a_.activation(SM[:, LAM:LAM + 2], SM[:, LAM:LAM + 2], ACT.Exp), "lam.exp")
        Stage(scalar=lam_exp)

        def lam_diff(st):
            st.wait("lam.exp")
            st.do(v.tensor_tensor(SM[:, LAM + 2:LAM + 3], SM[:, LAM:LAM + 1], SM[:, LAM + 1:LAM + 2], ALU.subtract))
            st.settle()
            st.do(v.tensor_scalar(SM[:, LAM + 2:LAM + 3], SM[:, LAM + 2:LAM + 3], LAMBDA0, None, ALU.add))
            st.do(v.tensor_scalar(SM[:, LAM + 3:LAM + 4], vec("subln_g"), 1.0 - LAMBDA0, None, ALU.mult))
            t5_mask(st)
        vs(lam_diff)
        mark("diff.in", "vector")

        def diff_score(h, c, i, out):
            b = 64 * c
            mm(out, A[b:b + 64, 12 + h, i * P:(i + 1) * P], A[b:b + 64, 16 + h, 0:(i + 1) * P], start=True, stop=False)
            if i >= 2:
                mm(out[:, 0:(i - 1) * P], bcast(ident[0:32, 31:32], P), bcast(T(31)[0:32, h:h + 1], (i - 1) * P), start=False, stop=False)
            if i == 0:
                return mm(out, cst("flip"), BT[:, h, P:2 * P], start=False, stop=True)
            return mm(out[:, (i - 1) * P:(i + 1) * P], cst("flip"), BT[:, h, :], start=False, stop=True)
        Stage(scalar=lambda act, st, e: st.wait("spill"))
        Attention("diff", 4, lambda i: i + 1, diff_score, lambda h, j, s: T(20 + j)[:, h * P:(h + 1) * P],
                  lambda h: (0, P), lambda h, s: T(32 + h), comps=2, prob=lambda n: A[:, n, :] if n < 8 else X[:, n - 8, :], pt=8, lam=SM[:, LAM + 2:LAM + 3])
        mark("dn.in", "vector")

        def d_apply(st, g, k, x, rstd):
            st.do(v.scalar_tensor_tensor(out=x, in0=x, scalar=SM[:, LAM + 3:LAM + 4], in1=rstd, op0=ALU.mult, op1=ALU.mult), f"ya.{g}")
        colnorm("dn", [[T(32 + h)] for h in range(4)], P, "eps5", False, d_apply, lambda i: T(24 + i), None)
        split("ya", [T(32 + k) for k in range(4)], YH, YL, ready=lambda k: f"ya.{k}")

        UP = []
        GATE_BANK = [6, 2, 6, 2, 4, 6, 4, 6]
        UP_BANK = [4, 0, 4, 0, 4, 0, 2, 4]
        gate_unit = lambda r: U0["s.up"] + (3 * r if r < 4 else 12 + 2 * (r - 4))
        up_unit = lambda r: U0["s.up"] + (3 * r + 2 if r < 4 else 20 + r - 4)

        def up_frees(r):
            return 4 + UP[0] + 4 * r

        def gates_pe(pe, st, r):
            for n in range(2):
                u = gate_unit(r) + n
                pe.wait_ge(split_done, u + 1)
                for k in range(KT):
                    c = slice(k * P, (k + 1) * P)
                    last = unit_passes(bank(GATE_BANK[r] + n), WH[:, u % SPLIT, c], WL[:, u % SPLIT, c],
                                       XH[:, k, :], XL[:, k, :], k == 0, k == KT - 1)
                last.then_inc(unit_done, 1)

        def ups_pe(pe, st, r):
            u, y0 = up_unit(r), 0 if r < 4 else 4
            pe.wait_ge(split_done, u + 1)
            for n in range(2):
                for k in range(4):
                    c = slice((4 * n + k) * P, (4 * n + k + 1) * P)
                    last = unit_passes(bank(UP_BANK[r] + n), WH[:, u % SPLIT, c], WL[:, u % SPLIT, c],
                                       YH[:, y0 + k, :], YL[:, y0 + k, :], k == 0, k == 3)
            last.then_inc(unit_done, 1)

        def round_pe(pe, st, r):
            gates_pe(pe, st, r)
            ups_pe(pe, st, r)

        def gates_act(act, st, r, gate):
            for n in range(2):
                act.wait_ge(unit_done, gate_unit(r) + 1 + n)
                st.do(a_.activation(gate(n), bank(GATE_BANK[r] + n), ACT.Sigmoid), f"up.gate{r}.{n}")

        def ups_dve(dve, st, r, gate, dst):
            dve.wait_ge(unit_done, up_unit(r) + 1)
            st.wait(f"up.gate{r}.1")
            for n in range(2):
                g, up = gate(n), bank(UP_BANK[r] + n)
                if r < 4:
                    v.tensor_tensor(dst(2 * r + n), g, up, ALU.mult).then_inc(banks_free, 2)
                else:
                    st.do(v.tensor_tensor(g, g, up, ALU.mult))
                    st.settle()
                    m = dst(2 * (r - 4) + n)
                    v.tensor_tensor(m, m, g, ALU.add).then_inc(banks_free, 2)
        mark("rw.clear", "vector")
        dma("lora", W2(36, 2), io["lora"], ready=["rw.clear"])
        dma("reset1", T(35), io["reset"], ready=["rw.clear"])
        Linear("s.rwkv", dst=at(0), pre=["rw.clear"])
        OM, DCY = 96, 64
        UP.append(evac[0])

        def upa_act(act, st, r):
            act.wait_ge(banks_free, up_frees(r))
            gates_act(act, st, r, lambda n: NR[:, n, :])

        def upa_dve(dve, st, r):
            ups_dve(dve, st, r, lambda n: NR[:, n, :], lambda q: X[:, q, :])

        def rw_shift(dve, st, e):
            dve.wait_ge(banks_free, 4 + e)
            st.do(v.tensor_tensor(A[:, 14:28, 1:S], A[:, 0:14, 0:S - 1], A[:, 0:14, 1:S], ALU.subtract))
            st.do(v.tensor_scalar(A[:, 14:28, 0:1], A[:, 0:14, 0:1], -1.0, None, ALU.mult))
            st.settle()
            for k in (12, 13, *range(12)):
                st.do(v.scalar_tensor_tensor(out=T(k), in0=T(14 + k), scalar=vec("mu", k), in1=T(k), op0=ALU.mult, op1=ALU.add), f"rw.p{k}")
                if k == 7:
                    st.wait("spill")
                    upa_dve(dve, st, 0)
            st.do(v.tensor_scalar(SM[:, OM:OM + 4], vec("k_a", 0, 4), -1.0, 1.0, ALU.mult, ALU.add))
            st.settle()
            for j in range(4):
                st.do(v.tensor_scalar(T(30 + j), T(4 + j), vec("k_k", j), None, ALU.mult), f"rw.kk{j}")
        Stage(vector=rw_shift)

        def rw_lora_act(act, st, e):
            st.wait("rw.p12")
            st.do(a_.activation(A[0:64, 12, :], A[0:64, 12, :], ACT.Tanh), "rw.tanh")
            st.wait("rw.p13")
            st.do(a_.activation(T(13), T(13), ACT.Sigmoid))
            upa_act(act, st, 0)
            st.wait("rw.p3")
            for j in range(4):
                st.wait(f"rw.zmm{j}")
                st.do(a_.activation(T(14 + j), bank(j), ACT.Sigmoid, bias=vec("w0", j)), f"rw.w{j}")
            st.wait("rw.p7")
            for j in range(4):
                st.wait(f"rw.amm{j}")
                st.do(a_.activation(T(18 + j), bank(4 + j), ACT.Sigmoid, bias=vec("a0", j)), f"rw.a{j}")
            st.wait("rw.kk3")
            for j in range(4):
                st.do(a_.activation(T(22 + j), T(30 + j), ACT.Square), f"rw.sq{j}")
            upa_act(act, st, 1)
            upa_act(act, st, 2)
            st.wait("rw.kmax")
            st.do(a_.activation(W2(22, 4), W2(22, 4), ACT.Sqrt), "rw.knorm")

        def rw_lora_pe(pe, st, e):
            round_pe(pe, st, 0)
            pe.wait_ge(banks_free, up_frees(0))
            st.wait("lora", "rw.tanh")
            for j in range(4):
                st.do(mm(bank(j), A[0:64, 36, j * P:(j + 1) * P], A[0:64, 12, :], start=True, stop=True), f"rw.zmm{j}")
            pe.wait_ge(banks_free, up_frees(1))
            for j in range(4):
                st.do(mm(bank(4 + j), A[64:128, 36, j * P:(j + 1) * P], A[64:128, 12, :], start=True, stop=True), f"rw.amm{j}")
            st.wait("rw.w3")
            round_pe(pe, st, 1)
            st.wait("rw.a3")
            round_pe(pe, st, 2)
            pe.wait_ge(banks_free, up_frees(2))
            for j in range(4):
                st.wait(f"rw.sq{j}")
                st.do(mm(bank(j), ones64, T(22 + j), start=True, stop=True), f"rw.ksum{j}")
            pe.wait_ge(banks_free, up_frees(3))
            for j in range(4):
                st.wait(f"rw.rk{j}")
                st.do(mm(bank(4 + j), ones64, T(34 + j), start=True, stop=True), f"rw.rksum{j}")
            st.wait("rw.kmax")
            round_pe(pe, st, 3)
            st.wait("rk.v")
            gates_pe(pe, st, 4)
            gates_pe(pe, st, 5)
            st.wait("up.gate4.1")
            gates_pe(pe, st, 6)

        def rw_keys(dve, st, e):
            st.wait("rw.w3", "reset1")
            st.do(v.tensor_scalar(W2(14, 4), W2(14, 4), -math.exp(-0.5), None, ALU.mult))
            st.settle()
            for j in range(4):
                st.do(v.tensor_tensor_scan(T(26 + j), T(35), T(14 + j), 0.0, ALU.mult, ALU.add))
            st.settle()
            upa_dve(dve, st, 1)
            st.wait("rw.a3", "rw.amm3")
            for j in range(4):
                st.do(v.tensor_scalar(T(34 + j), T(18 + j), vec("k_a", j), SM[:, OM + j:OM + j + 1], ALU.mult, ALU.add))
            st.settle()
            st.do(v.tensor_tensor(W2(4, 4), W2(4, 4), W2(34, 4), ALU.mult))
            st.settle()
            for j in range(4):
                st.do(v.scalar_tensor_tensor(out=T(34 + j), in0=T(j), scalar=vec("r_k", j), in1=T(4 + j), op0=ALU.mult, op1=ALU.mult), f"rw.rk{j}")
            upa_dve(dve, st, 2)
            for j in range(4):
                st.wait(f"rw.ksum{j}")
                st.do(v.tensor_scalar(T(22 + j), bank(j), 1e-24, None, ALU.max), "rw.kmax")
            for j in range(4):
                st.wait(f"rw.rksum{j}")
                st.do(v.tensor_tensor(T(34 + j), T(8 + j), bank(4 + j), ALU.mult), "rk.v")
            st.wait("rw.knorm")
            st.do(v.reciprocal(W2(22, 4), W2(22, 4)))
            st.settle()
            st.do(v.tensor_tensor(W2(30, 4), W2(30, 4), W2(22, 4), ALU.mult))
            st.settle()
            st.do(v.tensor_tensor(W2(18, 4), W2(18, 4), W2(30, 4), ALU.mult))
        Stage(tensor=rw_lora_pe, scalar=rw_lora_act, vector=rw_keys)
        evac[0] += 12
        dma("ma.out0", io["spill3"][:, 0:6, :], X[:, 0:6, :])
        dma("rk.out", io["spill_rk"], A[:, 34:38, :], ready=["rk.v"])

        ARS = (22, 24, 14, 16)
        AR = [W2(s, 2).rearrange("p (t w c) -> p t w c", t=TT, w=2) for s in ARS]
        t4 = lambda ap: ap.rearrange("p (t c) -> p t c", c=P)
        c64 = lambda ap: ap.rearrange("p (t c) -> p t c", c=64)

        EX = [SG, A[:, 34:38, :]]

        def p1_act(act, st, e):
            for j in range(4):
                E = EX[j % 2]
                st.wait(f"p1.d{j}")
                st.do(a_.activation(E[:, 0, :], T(26 + j), ACT.Exp))
                st.do(a_.activation(E[:, 3, :], T(26 + j), ACT.Exp, scale=-1.0))
                st.do(a_.activation(E[:, 1:3, :], E[:, 1:3, :], ACT.Exp), f"p1.e{j}")
                if j == 1:
                    st.wait("ma.out0")
                    gates_act(act, st, 4, lambda n: X[:, n, :])

        def p1_dve(dve, st, e):
            def exponents(j):
                E = EX[j % 2]
                if j == 1:
                    st.wait("rk.out")
                st.settle()
                st.do(v.tensor_tensor(E[:, 1, :], T(26 + j), T(14 + j), ALU.subtract))
                st.do(v.tensor_tensor(c64(E[:, 2, :]), c64(T(26 + j))[:, :, 63:64].to_broadcast([P, 8, 64]), c64(T(26 + j)), ALU.subtract), f"p1.d{j}")

            def scaled(j):
                E = EX[j % 2]
                st.wait(f"p1.e{j}")
                st.settle()
                st.do(v.tensor_copy(SM[:, DCY + 8 * j:DCY + 8 * j + 8].rearrange("p (a b) -> p a b", b=1), c64(E[:, 0, :])[:, :, 63:64]))
                st.do(v.scalar_tensor_tensor(out=AR[j][:, :, 0, :], in0=t4(T(30 + j)), scalar=-1.0, in1=t4(E[:, 1, :]), op0=ALU.mult, op1=ALU.mult))
                st.do(v.tensor_tensor(AR[j][:, :, 1, :], t4(T(j)), t4(E[:, 0, :]), ALU.mult))
                st.settle()
                st.do(v.tensor_tensor(T(j), T(18 + j), E[:, 3, :], ALU.mult))
                st.do(v.tensor_tensor(T(30 + j), T(4 + j), E[:, 3, :], ALU.mult))
                st.settle()
                st.do(v.tensor_tensor(T(18 + j), T(18 + j), E[:, 2, :], ALU.mult))
                st.do(v.tensor_tensor(T(4 + j), T(4 + j), E[:, 2, :], ALU.mult), f"p1.s{j}")
            exponents(0)
            for j in range(4):
                if j < 3:
                    exponents(j + 1)
                scaled(j)
            st.do(v.memset(T(12), 0.0), "p1.done")
            upa_dve(dve, st, 3)
        Stage(scalar=p1_act, vector=p1_dve)

        def late_gates(act, st, e):
            upa_act(act, st, 3)
            for r in (5, 6):
                gates_act(act, st, r, lambda n: X[:, 2 * (r - 4) + n, :])
        Stage(scalar=late_gates)
        evac[0] += 4

        TURN = [s + j for s in (8, 4, 18) for j in range(4)]

        def p1_turn_pe(pe, st, e):
            pe.wait_ge(banks_free, 4 + e)
            st.wait("p1.done")
            for n, k in enumerate(TURN):
                if n >= 4:
                    st.wait(f"p1.turned{n - 4}")
                for t in range(TT):
                    last = nc.tensor.transpose(PS[:, n % 4, t * P:(t + 1) * P], T(k)[:, t * P:(t + 1) * P], ident)
                st.do(last, f"p1.turn{n}")

        def p1_turn_act(act, st, e):
            for n, k in enumerate(TURN):
                st.wait(f"p1.turn{n}")
                st.do(a_.activation(T(k), bank(n % 4), ACT.Copy), f"p1.turned{n}")
        Stage(tensor=p1_turn_pe, scalar=p1_turn_act)
        dma("ma.out1", io["spill3"][:, 6:8, :], X[:, 6:8, :])
        dma("gb.out", io["spill_gates"], X[:, 0:6, :], ready=["up.gate6.1"])

        RHS = X[:, 4:8, :].rearrange("p a b -> p (a b)").rearrange("p (h c) -> p h c", h=8)
        RB = X[:, 0:4, :].rearrange("p a b -> p (a b)").rearrange("p (h w c) -> p h w c", h=8, w=2)
        h4 = lambda ap: ap.rearrange("p (h c) -> p h c", h=4)
        two = lambda b, **k: PS[:, b:b + 2, :].rearrange("p a b -> p (a b)")
        GS = [[SG[:, i, :] for i in range(4)], [T(34 + i) for i in range(4)]]
        AT = NR[:, 0, :]
        UT = NR[:, 1, :].rearrange("p (h c) -> p h c", h=8)
        ST = [T(12)[:, 0:256], T(12)[:, 256:512], SD[:, 0:256]]
        p4 = lambda ap: ap.rearrange("p (j c) -> p j c", j=4)
        m4 = lambda name: cst(name).rearrange("p (a c) -> p a c", a=1).to_broadcast([P, 4, P])

        def blk(t4_, h):
            return t4_[:, h * P:(h + 1) * P]

        def slot(h):
            return 4 * (h % 2) + h // 2

        def heads_of(g):
            return [4 * g, 4 * g + 2, 4 * g + 1, 4 * g + 3]

        def quad(ap, g):
            return ap.rearrange("p (w j) c -> p w j c", w=2)[:, :, 2 * g:2 * g + 2, :]

        q4 = lambda ap: ap.rearrange("p (w j c) -> p w j c", w=2, j=2)
        mq = lambda name: cst(name).rearrange("p (a b c) -> p a b c", a=1, b=1).to_broadcast([P, 2, 2, P])
        scores = PS[:, 0:7:6, 0:256].rearrange("p w (j c) -> p w j c", j=2)

        def scores_pe(st, t, g):
            i = f"r{t}.{g}"
            G2 = GS[g][2]
            heads = heads_of(g)
            if g:
                st.wait(f"r{t}.0.rhs")
            elif t:
                st.wait(f"y{t - 1}", f"st{2 * t - 1}")
            st.wait("p1.turned11")
            for n, h in enumerate(heads):
                j, b = h // 2, 64 * (h % 2)
                c = slice(t * P, (t + 1) * P)
                mm(PS[:, 6 * (h % 2), (n % 2) * P:(n % 2 + 1) * P], AR[j][b:b + 64, t, 0, :], T(j)[b:b + 64, c], start=True, stop=True)
                mm(PS[:, 1 + n // 2, (n % 2) * 256:(n % 2 + 1) * 256], T(j)[b:b + 64, c], AR[j][b:b + 64, t, :, :].rearrange("p w c -> p (w c)"), start=True, stop=True)
                last = mm(PS[:, 3 + n // 2, (n % 2) * 256:(n % 2 + 1) * 256], T(30 + j)[b:b + 64, c], AR[j][b:b + 64, t, :, :].rearrange("p w c -> p (w c)"), start=True, stop=True)
            for q in range(2):
                last = nc.tensor.transpose(PS[:, 5, 256 + q * P:256 + (q + 1) * P], AR[2 * g + q][:, t, 0, :], ident)
            st.do(last, i + ".scores")
            st.wait(i + ".masked")
            for n, h in enumerate(heads):
                j, b = h // 2, 64 * (h % 2)
                last = mm(PS[:, 5, n * 64:(n + 1) * 64], blk(G2, n), T(8 + j)[:, t * P + b:t * P + b + 64], start=True, stop=True)
            st.do(last, i + ".w")


        def scores_act(st, t, g):
            i = f"r{t}.{g}"
            R4 = quad(RHS, g)
            st.wait(i + ".masked", i + ".w")
            st.do(a_.activation(R4[:, :, :, 0:64], PS[:, 5, 256:512].rearrange("p (j w c) -> p w j c", j=2, w=2), ACT.Copy))
            st.do(a_.activation(R4[:, :, :, 64:P], q4(PS[:, 5, 0:256]), ACT.Copy), i + ".rhs")

        def scores_dve(st, t, g):
            i = f"r{t}.{g}"
            G0, G1, G2, G3 = GS[g]
            st.wait(i + ".scores")
            if g == 0 and t:
                st.wait(f"y.mm{t - 1}")
            if t == 0:
                st.wait("ma.out1", "gb.out", "rk.out")
            R4 = quad(RHS, g)
            b12, b34 = h4(two(1)), h4(two(3))
            st.settle()
            st.do(v.tensor_tensor(h4(G2), b34[:, :, 0:P], m4("strictT"), ALU.mult))
            st.do(v.tensor_tensor(q4(G0), scores, mq("sub16"), ALU.mult))
            st.do(v.tensor_tensor(h4(G1), b12[:, :, 0:P], m4("sub16T"), ALU.mult))
            st.do(v.tensor_tensor(R4[:, :, :, P:2 * P], scores, mq("off16"), ALU.mult))
            st.do(v.tensor_tensor(quad(RB[:, :, 0, :], g), q4(two(1))[:, :, :, P:2 * P], mq("chunkT"), ALU.mult))
            st.do(v.tensor_tensor(quad(RB[:, :, 1, :], g), q4(two(3))[:, :, :, P:2 * P], mq("chunkT"), ALU.mult), i + ".masked")

        STEPS = 9

        def solve_pe(st, t, g, step):
            i, B = f"r{t}.{g}", 4 * g
            heads = heads_of(g)
            G0, G1, G2, G3 = GS[g]
            rhs = lambda n, a, b: RHS[:, slot(heads[n]), a:b]

            def product(b, L, R, name):
                for n in range(4):
                    last = mm(PS[:, B + b, n * P:(n + 1) * P], L(n), R(n), start=True, stop=True)
                st.do(last, i + name)

            def apply(L, name):
                for n in range(4):
                    last = mm(PS[:, B + 2 + n // 2, (n % 2) * 256:(n % 2 + 1) * 256], blk(L, n), rhs(n, 0, 256), start=True, stop=True)
                st.do(last, i + name)
            if step == 0:
                product(0, lambda n: blk(G1, n), lambda n: blk(G0, n), ".d2")
                product(1, lambda n: blk(G0, n), lambda n: blk(G1, n), ".d2t")
                apply(G1, ".a1")
            elif step == 1:
                st.wait(i + ".d2t_")
                product(0, lambda n: blk(G3, n), lambda n: blk(G2, n), ".d4")
                product(1, lambda n: blk(G2, n), lambda n: blk(G3, n), ".d4t")
                st.wait(i + ".r1")
                apply(G3, ".a2")
            elif step == 2:
                st.wait(i + ".d4t_")
                product(0, lambda n: blk(G0, n), lambda n: blk(G1, n), ".d8t")
                st.wait(i + ".r2")
                apply(G1, ".a4")
            elif step == 3:
                st.wait(i + ".r4", i + ".d8t_")
                apply(G2, ".a8")
            elif step == 4:
                st.wait(i + ".r8")
                for n in range(4):
                    last = nc.tensor.transpose(PS[:, B, n * P:(n + 1) * P], rhs(n, P, 2 * P), ident)
                st.do(last, i + ".mt")
            elif step == 5:
                st.wait(i + ".mt_")
                product(1, lambda n: rhs(n, P, 2 * P), lambda n: blk(G0, n), ".m2t")
            elif step == 6:
                st.wait(i + ".m2t_")
                product(2, lambda n: blk(G1, n), lambda n: rhs(n, 0, P), ".b2")
            elif step == 7:
                st.wait(i + ".q2")
                product(3, lambda n: blk(G0, n), lambda n: rhs(n, 0, P), ".b1")
            else:
                st.wait(i + ".q1")
                for h in heads:
                    o, q = 64 * (h % 2), h // 2 - 2 * g
                    last = mm(PS[o:o + 64, B, q * P:(q + 1) * P], RHS[:, slot(h), 0:64], ident, start=True, stop=True)
                st.do(last, i + ".turn")

        def solve_act(st, t, g, step):
            i, B = f"r{t}.{g}", 4 * g
            G0, G1, G2, G3 = GS[g]
            if step == 0:
                st.wait(i + ".d2")
                st.do(a_.activation(G2, bank(B), ACT.Copy))
                st.wait(i + ".d2t")
                st.do(a_.activation(G3, bank(B + 1), ACT.Copy), i + ".d2t_")
            elif step == 1:
                st.wait(i + ".d4t", i + ".a1")
                st.do(a_.activation(G0, bank(B), ACT.Copy))
                st.do(a_.activation(G1, bank(B + 1), ACT.Copy), i + ".d4t_")
            elif step == 2:
                st.wait(i + ".d8t", i + ".a2")
                st.do(a_.activation(G2, bank(B), ACT.Copy), i + ".d8t_")
            elif step == 4:
                st.wait(i + ".mt", i + ".a8")
                st.do(a_.activation(G0, bank(B), ACT.Copy), i + ".mt_")
            elif step == 5:
                st.wait(i + ".m2t")
                st.do(a_.activation(G1, bank(B + 1), ACT.Copy), i + ".m2t_")
            elif step == 8:
                st.wait(i + ".turn")
                st.do(a_.activation(AT[:, 2 * g * P:(2 * g + 2) * P], PS[:, B, 0:256], ACT.Copy), i + ".at")

        def solve_dve(st, t, g, step):
            i, B = f"r{t}.{g}", 4 * g
            R4 = quad(RHS, g)
            if step < 4:
                name = (1, 2, 4, 8)[step]
                st.wait(f"{i}.a{name}", i + ".rhs")
                R = R4.rearrange("p w j c -> p w (j c)")
                st.do(v.tensor_tensor(R, R, PS[:, B + 2:B + 4, :], ALU.add), f"{i}.r{name}")
            elif step in (6, 7):
                a, b, r = ((".b2", 2, ".q2"), (".b1", 3, ".q1"))[step - 6]
                st.wait(i + a)
                st.settle()
                st.do(v.tensor_tensor(R4[:, :, :, 0:P], R4[:, :, :, 0:P], q4(bank(B + b)), ALU.add), i + r)

        def state_pe(st, t):
            for cc in range(2):
                n, r = 2 * t + cc, 64 * cc
                rows = slice(r, r + 64)
                st.wait(f"r{t}.1.at")
                if n:
                    st.wait(f"st{n - 1}")
                for h in range(8):
                    j, b = h // 2, 64 * (h % 2)
                    last = mm(PS[r:r + 64, 5 + h % 2, j * 64:(j + 1) * 64], AT[b:b + 64, j * P + r:j * P + r + 64],
                              ST[n % 3][b:b + 64, j * 64:(j + 1) * 64], start=True, stop=True)
                st.do(last, f"u.mm{n}")
                for h in range(8):
                    j, b = h // 2, 64 * (h % 2)
                    c = slice(t * P + b, t * P + b + 64)
                    o = PS[b:b + 64, 7, j * 64:(j + 1) * 64]
                    mm(o, T(4 + j)[rows, c], T(8 + j)[rows, c], start=True, stop=False)
                    if h == 0:
                        st.wait(f"u{n}")
                    last = mm(o, T(18 + j)[rows, c], UT[rows, slot(h), :], start=False, stop=True)
                st.do(last, f"s.mm{n}")
            for h in range(8):
                j, b = h // 2, 64 * (h % 2)
                o = PS[b:b + 64, 5, j * P:(j + 1) * P]
                mm(o, UT[:, slot(h), :], RB[:, slot(h), 0, :], start=True, stop=False)
                mm(o, T(8 + j)[:, t * P + b:t * P + b + 64], RB[:, slot(h), 1, :], start=False, stop=False)
                for cc in range(2):
                    last = mm(o[:, 64 * cc:64 * cc + 64], ST[(2 * t + cc) % 3][b:b + 64, j * 64:(j + 1) * 64],
                              AR[j][b:b + 64, t, 1, 64 * cc:64 * cc + 64], start=False, stop=(cc == 1))
            st.do(last, f"y.mm{t}")

        def state_dve(st, t):
            for cc in range(2):
                n, r = 2 * t + cc, 64 * cc
                rows = slice(r, r + 64)
                st.wait(f"u.mm{n}")
                st.settle()
                st.do(v.tensor_tensor(UT[rows].rearrange("p (w j) c -> p w j c", w=2), RHS[rows, :, 64:P].rearrange("p (w j) c -> p w j c", w=2),
                                      PS[rows, 5:7, 0:256].rearrange("p w (j c) -> p w j c", j=4), ALU.add), f"u{n}")
                if n == 0:
                    st.do(v.memset(SD[:], 0.0))
                st.settle()
                d = SM[:, DCY:DCY + 32].rearrange("p (j c) -> p j c", j=4)[:, :, n:n + 1].to_broadcast([P, 4, 64])
                if n >= 2:
                    st.wait(f"y.mm{(n - 2) // 2}")
                st.do(v.tensor_tensor(p4(ST[(n + 1) % 3]), p4(ST[n % 3]), d, ALU.mult))
                st.wait(f"s.mm{n}")
                st.settle()
                st.do(v.tensor_tensor(ST[(n + 1) % 3], ST[(n + 1) % 3], PS[:, 7, 0:256], ALU.add), f"st{n}")

        def rw_pe(pe, st, e):
            for t in range(TT):
                scores_pe(st, t, 0)
                scores_pe(st, t, 1)
                st.wait(f"r{t}.1.rhs")
                for step in range(STEPS):
                    for g in range(2):
                        solve_pe(st, t, g, step)
                state_pe(st, t)

        def rw_act(act, st, e):
            for t in range(TT):
                scores_act(st, t, 0)
                scores_act(st, t, 1)
                for step in range(STEPS):
                    for g in range(2):
                        solve_act(st, t, g, step)
                if t == TT - 1:
                    act.dma_start(SG[:, 3, :], io["lora"][:, S:2 * S]).then_inc(g2_loaded, 16)
                    act.dma_start(A[:, 34:38, :], io["spill_rk"]).then_inc(rk_loaded, 16)
                    names["g2"], names["rk.in"] = (g2_loaded, 16), (rk_loaded, 16)
                st.wait(f"y.mm{t}")
                st.do(a_.activation(A[:, 26:30, t * P:(t + 1) * P], PS[:, 5, :].rearrange("p (j c) -> p j c", j=4), ACT.Copy), f"y{t}")

        def rw_dve(dve, st, e):
            for t in range(TT):
                scores_dve(st, t, 0)
                scores_dve(st, t, 1)
                for step in range(STEPS):
                    for g in range(2):
                        solve_dve(st, t, g, step)
                state_dve(st, t)
        Stage(tensor=rw_pe, scalar=rw_act, vector=rw_dve)
        mark("gn.in", "scalar")
        dma("gb.in0", A[:, 14:18, :], io["spill_gates"][:, 0:4, :], ready=["y.mm3"])
        dma("gb.in1", A[:, 30:32, :], io["spill_gates"][:, 4:6, :], ready=["y.mm3"])
        dma("ma.in", A[:, 4:12, :], io["spill3"], ready=["y.mm3"])

        def rw_gate_pe(pe, st, e):
            st.wait("g2", "y3")
            for j in range(4):
                st.do(mm(bank(j), SG[:, 3, j * P:(j + 1) * P], T(13), start=True, stop=True), f"rw.g{j}")
        Stage(tensor=rw_gate_pe)

        def gn_apply(st, g, k, x, rstd):
            st.wait(f"rw.g{g}", "rk.in")
            st.do(v.scalar_tensor_tensor(out=x, in0=x, scalar=vec("lnx_g", g), in1=rstd, op0=ALU.mult, op1=ALU.mult))
            st.settle()
            st.do(v.scalar_tensor_tensor(out=x, in0=x, scalar=vec("lnx_b", g), in1=T(34 + g), op0=ALU.add, op1=ALU.add))
            st.settle()
            st.do(v.tensor_tensor(x, x, bank(g), ALU.mult), f"yb.{g}")
        colnorm("gn", [[T(26 + j)] for j in range(4)], 64, "epsx", True, gn_apply, lambda i: T(i), lambda i: T(18 + i), sums=ones64)
        split("yb", [T(18 + k) for k in range(4)], YH[:, 4:8, :], YL[:, 4:8, :], ready=lambda k: f"yb.{k}")
        GB = [(14, 15), (16, 17), (30, 31)]

        def upb_pe(pe, st, e):
            st.wait("gn.std")
            gates_pe(pe, st, 7)
            st.wait("yb.ready")
            for r in range(4, 8):
                if r == 7:
                    pe.wait_ge(banks_free, up_frees(5))
                ups_pe(pe, st, r)

        def upb_act(act, st, e):
            gates_act(act, st, 7, lambda n: SG[:, n, :])

        def upb_dve(dve, st, e):
            st.wait("ma.in", "gb.in0", "gb.in1")
            for r in range(4, 8):
                ups_dve(dve, st, r, (lambda n: SG[:, n, :]) if r == 7 else (lambda n: T(GB[r - 4][n])), lambda q: T(4 + q))
        Stage(tensor=upb_pe, scalar=upb_act, vector=upb_dve)
        evac[0] += 16
        dma("unspill", X[:], io["spill"], ready=["yb.ready"])
        free_until("scalar", "vector")
        split("merged", [T(4 + k) for k in range(KT)], XH, XL)
        vs(lambda st: st.wait("unspill"))
        Linear("s.out", add=True, alpha=ALPHA, ready="merged", total=True)
        layernorm("fns", "ln1_g", "ln1_b", summed="s.out.sum")
        ffn("s", ALPHA)
        layernorm("end2", "ln2_g", "ln2_b", split_it=False, stream=True)

        rmsnorm("tn", "norm_g3", s0=24, arrive=lambda k: f"end2.biased{k}")
        dma("spill3", io["spill3"], X[:], ready=["end2.biased7"])

        def gif_pe(pe, st, e):
            pe_start(pe, st, "tn", U0["t.gif"], e, [(XH, XL)])
        IG, FL, GG, FX = T(32), T(33), T(34), T(37)

        def gif_act(act, st, e):
            act.wait_ge(unit_done, U0["t.gif"] + 1)
            b = e % 4
            st.wait("tn.lo7")
            st.do(a_.activation(IG[0:4, :], PS[0:4, b, :], ACT.Identity, bias=vec("ml_bi")[0:4, :]))
            st.do(a_.activation(FL[0:4, :], PS[32:36, b, :], ACT.Copy))
            st.do(a_.activation(FX[0:8, :], PS[64:72, b, :], ACT.Copy))
            st.settle()
            st.do(a_.activation(FL[0:4, :], FL[0:4, :], ACT.Identity, bias=vec("ml_bf")[0:4, :]), "gif.f")
            st.do(a_.activation(FX[0:8, :], FX[0:8, :], ACT.Identity, bias=vec("fox_bf")[0:8, :]), "gif.x")
            st.settle()
            for t, n, r in ((35, 4, FL), (36, 8, FX)):
                x = T(t)[0:n, :]
                st.do(a_.activation(x, r[0:n, :], ACT.Abs))
                st.settle()
                st.do(a_.activation(x, x, ACT.Exp, scale=-1.0))
                st.settle()
                st.do(a_.activation(x, x, ACT.Ln, bias=cst("one")[0:n, :]), f"gif.ln{n}")
            act.wait_ge(unit_done, U0["t.gif"] + 1)

        def gif_dve(dve, st, e):
            NRc = T(28)
            st.do(v.memset(NRc[0:8, :], 1.0))
            st.wait("gif.ln8")
            for t, n, r in ((35, 4, FL), (36, 8, FX)):
                st.do(v.scalar_tensor_tensor(out=T(t)[0:n, :], in0=r[0:n, :], scalar=0.0, in1=T(t)[0:n, :], op0=ALU.min, op1=ALU.subtract))
            st.settle()
            for t, n, r in ((35, 4, FL), (36, 8, FX)):
                st.do(v.tensor_tensor_scan(r[0:n, :], NRc[0:n, :], T(t)[0:n, :], 0.0, ALU.mult, ALU.add))
            st.settle()
            st.do(v.tensor_scalar(FX[0:8, :], FX[0:8, :], -1.0, None, ALU.mult), "fox.negf")
            st.do(v.tensor_tensor(IG[0:4, :], IG[0:4, :], FL[0:4, :], ALU.subtract))
            st.settle()
            st.do(v.tensor_tensor_scan(GG[0:4, :], IG[0:4, :], IG[0:4, :], 0.0, ALU.max, ALU.max))
            st.settle()
            st.do(v.tensor_tensor(FL[0:4, :], FL[0:4, :], GG[0:4, :], ALU.add))
            st.do(v.tensor_scalar(T(35)[0:4, :], GG[0:4, :], -1.0, None, ALU.mult))
            st.settle()
            v.tensor_copy(GG[0:4, :], T(35)[0:4, :]).then_inc(banks_free, 1)
            dve.wait_ge(banks_free, 4 + e + 1)
            names["ml.rows"] = (banks_free, 4 + e + 1)
        Stage(tensor=gif_pe, scalar=gif_act, vector=gif_dve)
        evac[0] += 1

        Linear("t.qk", dst=at(0))

        def conv3(dve, st, e):
            for k in range(0, 16, 2):
                dve.wait_ge(banks_free, 4 + e - 16 + k + 2)
                depthwise(st, lambda q: T(k + q), lambda q: T(16 + k + q), 4, "conv_w3", None, 2, k)
        Stage(vector=conv3)
        mark("conv3", "vector")

        def qk_silu(act, st, e):
            st.wait("conv3")
            st.do(a_.activation(W2(16, 8), W2(16, 8), ACT.Silu))
            st.do(a_.activation(W2(24, 8), W2(24, 8), ACT.Silu), "ml.qk")
        Stage(scalar=qk_silu)
        TokenMajor("t.v", 2, lambda h, t: T(2 * t + h))
        Pairs("t.oz", 8, at(8), ACT.Sigmoid, func2=ACT.Silu)

        def ml_cols_pe(pe, st, e):
            pe.wait_ge(banks_free, 4 + e)
            st.wait("ml.rows", "ml.qk")
            for t in range(TT):
                last = nc.tensor.transpose(PS[:, 0, 4 * t:4 * t + 4], IG[0:4, t * P:(t + 1) * P], ident[0:4, 0:4])
            st.do(last, "ml.cols")

        def ml_cols_act(act, st, e):
            st.wait("ml.cols")
            st.do(a_.activation(SM[:, 48:64], PS[:, 0, 0:16], ACT.Copy), "ml.c")
        Stage(tensor=ml_cols_pe, scalar=ml_cols_act)

        EMT = T(36)

        def ml_pe(pe, st, e):
            st.wait("ml.c")

            def score(n):
                h, j = n // TT, n % TT
                c0 = j * P
                if n >= 2:
                    st.wait(f"ml.e{n - 2}", f"ml.p{n - 2}")
                o = PS[:, n % 2, c0:S]
                mm(o, bcast(ident[0:4, h:h + 1], P), GG[0:4, c0:S], start=True, stop=False)
                st.do(mm(PS[:, n % 2, c0:c0 + P], ident, cst("caddT"), start=False, stop=True), f"ml.d{n}")
                for d in range(2):
                    last = mm(PS[:, 2 + n % 2, c0:S], T(24 + 2 * h + d)[:, c0:c0 + P], T(16 + 2 * h + d)[:, c0:S],
                              start=(d == 0), stop=(d == 1))
                st.do(last, f"ml.s{n}")

            def gather(n):
                h, j = n // TT, n % TT
                c0 = j * P
                if j == 0:
                    if h:
                        st.wait(f"ml.h{h - 1}")
                    st.do(mm(PS[:, 7, :], bcast(ident[0:4, h:h + 1], P), FL[0:4, :], start=True, stop=True), f"ml.m{h}")
                st.wait(f"ml.p{n}")
                pt = SG[:, 2 + n % 2, c0:S]
                for d in range(2):
                    mm(PS[:, 4 + d, c0:S], W2(2 * j, 2)[:, h * 256 + d * P:h * 256 + (d + 1) * P], pt, start=(j == 0), stop=(j == TT - 1))
                st.do(mm(PS[:, 6, c0:S], ones, pt, start=(j == 0), stop=(j == TT - 1)), f"ml.n{n}")
            score(0)
            for n in range(16):
                if n < 15:
                    score(n + 1)
                gather(n)

        def ml_act(act, st, e):
            for n in range(16):
                h, j = n // TT, n % TT
                st.wait(f"ml.d{n}")
                if n >= 2:
                    st.wait(f"ml.p{n - 2}")
                st.do(a_.activation(SG[:, n % 2, j * P:S], PS[:, n % 2, j * P:S], ACT.Exp, bias=SM[:, 48 + 4 * j + h:49 + 4 * j + h]), f"ml.e{n}")
                if j == 3:
                    st.wait(f"ml.m{h}")
                    if h:
                        st.wait(f"ml.h{h - 1}")
                    st.do(a_.activation(EMT, bank(7), ACT.Exp, scale=-1.0), f"ml.em{h}")

        def ml_dve(dve, st, e):
            dve.wait_ge(banks_free, 4 + e)
            for n in range(16):
                h, j = n // TT, n % TT
                st.wait(f"ml.s{n}", f"ml.e{n}")
                if n >= 2:
                    st.wait(f"ml.n{n - 2}")
                st.do(v.scalar_tensor_tensor(out=SG[:, 2 + n % 2, j * P:S], in0=PS[:, 2 + n % 2, j * P:S], scalar=1.0 / 16,
                                             in1=SG[:, n % 2, j * P:S], op0=ALU.mult, op1=ALU.mult), f"ml.p{n}")
                if j == 3:
                    st.wait(f"ml.n{n}", f"ml.em{h}")
                    st.settle()
                    st.do(v.tensor_tensor(SD[:], bank(6), EMT, ALU.max))
                    st.settle()
                    st.do(v.scalar_tensor_tensor(out=SD[:], in0=bank(6), scalar=-1.0, in1=SD[:], op0=ALU.mult, op1=ALU.max))
                    st.settle()
                    st.do(v.reciprocal(SD[:], SD[:]))
                    st.settle()
                    for d in range(2):
                        st.do(v.tensor_tensor(T(16 + 2 * h + d), SD[:], bank(4 + d), ALU.mult), f"ml.h{h}")
        Stage(tensor=ml_pe, scalar=ml_act, vector=ml_dve)
        mark("mn.in", "vector")

        def ml_apply(st, g, k, x, rstd):
            st.do(v.scalar_tensor_tensor(out=x, in0=x, scalar=vec("ml_norm_g", 2 * g + k), in1=rstd, op0=ALU.mult, op1=ALU.mult))
            st.settle()
            st.do(v.tensor_tensor(x, x, T(8 + 2 * g + k), ALU.mult), f"yA.{2 * g + k}")
        colnorm("mn", [[T(16 + 2 * h), T(17 + 2 * h)] for h in range(4)], 256, "eps6", False, ml_apply, lambda i: T(24 + i), None)
        split("yA", [T(16 + k) for k in range(KT)], YH, YL, ready=lambda k: f"yA.{k}")
        Linear("t.fq", dst=at(0), scale=128 ** -0.5)
        Pairs("t.br0", 8, at(24), ACT.Sigmoid, of=1, yh=(YH, YL), ready="yA")

        Linear("t.fk", dst=at(8))
        TokenMajor("t.fv", 2, lambda h, t: T(16 + 2 * t + h))

        def fox_score(h, c, i, out):
            mm(out, T(h)[:, i * P:(i + 1) * P], T(8 + h)[:, 0:(i + 1) * P], start=True, stop=False)
            mm(out, bcast(ident[0:8, h:h + 1], P), FX[0:8, 0:(i + 1) * P], start=False, stop=False)
            return mm(out[:, i * P:(i + 1) * P], ident, cst("cadd"), start=False, stop=True)
        mark("fox.in", "vector")
        Stage(scalar=lambda act, st, e: st.wait("spill3"))
        Attention("fox", 8, lambda i: i + 1, fox_score, lambda h, j, s: W2(16 + 2 * j, 2)[:, h * P:(h + 1) * P],
                  lambda h: (0, P), lambda h, s: T(h), prob=lambda n: X[:, n, :], pt=32)
        Linear("t.fz", dst=at(8), func=ACT.Silu, pre=["fox.done"])

        def fox_gate(dve, st, e):
            for k in range(KT):
                dve.wait_ge(banks_free, 4 + e - KT + k + 1)
                st.do(v.tensor_tensor(T(k), T(k), T(8 + k), ALU.mult), f"yB.{k}")
        Stage(vector=fox_gate)
        split("yB", [T(k) for k in range(KT)], YH, YL, ready=lambda k: f"yB.{k}")
        Pairs("t.br1", 8, at(24), ACT.Sigmoid, of=1, yh=(YH, YL), ready="yB", acc=0)

        Linear("t.cu", dst=at(0))

        def pool_windows(st):
            for g in range(4):
                src = [T(2 * g), T(2 * g + 1)]
                for lv in range(g + 1):
                    sh = 1 << lv
                    dst = [T(8 + 2 * (lv % 2) + q + 4 * (g % 2)) for q in range(2)]
                    st.settle()
                    for q in range(2):
                        st.do(v.tensor_tensor(dst[q][:, sh:], src[q][:, sh:], src[q][:, :S - sh], ALU.add))
                        st.do(v.tensor_copy(dst[q][:, :sh], src[q][:, :sh]))
                    src = dst
                w = 2 << g
                st.settle()
                for q in range(2):
                    k = 2 * g + q
                    o = T(16 + k)
                    st.do(v.scalar_tensor_tensor(out=o[:, 16:], in0=src[q][:, 16:], scalar=1.0 / w, in1=T(k)[:, 16:],
                                                 op0=ALU.mult, op1=ALU.subtract))
                    st.do(v.tensor_tensor(o[:, :16], src[q][:, :16], cst("icnt", k=16 * k, n=16), ALU.mult))
                st.settle()
                for q in range(2):
                    k = 2 * g + q
                    st.do(v.tensor_tensor(T(16 + k)[:, :16], T(16 + k)[:, :16], T(k)[:, :16], ALU.subtract))
            st.do(v.memset(SM[:, 0:1], 0.0), "pool.d")
        Linear("t.cz", dst=lambda j: X[:, bass.ds(j, 1), :], func=ACT.Silu)
        Stage(vector=lambda dve, st, e: (dve.wait_ge(banks_free, 4 + e - KT), pool_windows(st)))
        split("pd", [T(16 + k) for k in range(KT)], YH, YL, ready=lambda k: "pool.d")

        def pool_pe(pe, st, e):
            st.wait("pd.ready")
            pe.wait_ge(banks_free, 4 + e)
            for n in range(2):
                u = U0["t.pool"] + n
                pe.wait_ge(split_done, u + 1)
                for g in range(2):
                    for o in range(2):
                        for k in range(2):
                            c = slice((4 * g + 2 * o + k) * P, (4 * g + 2 * o + k + 1) * P)
                            q = 4 * n + 2 * g + k
                            last = unit_passes(bank(4 * n + 2 * g + o), WH[:, u % SPLIT, c], WL[:, u % SPLIT, c],
                                               YH[:, q, :], YL[:, q, :], k == 0, k == 1)
                last.then_inc(unit_done, 1)

        def pool_act(act, st, e):
            st.wait("pd.ready")
            act.wait_ge(unit_done, U0["t.pool"] + 2)
            for k in range(KT):
                a_.activation(T(8 + k), bank(k), ACT.Copy, scale=vec("pool_scale", k)).then_inc(banks_free, 1)
        Stage(tensor=pool_pe, scalar=pool_act)
        evac[0] += 8

        def pool_gate(dve, st, e):
            for k in range(KT):
                dve.wait_ge(banks_free, 4 + e - KT + k + 1)
                st.do(v.tensor_tensor(T(k), X[:, k, :], T(8 + k), ALU.mult), f"yC.{k}")
        Stage(vector=pool_gate)
        split("yC", [T(k) for k in range(KT)], YH, YL, ready=lambda k: f"yC.{k}")
        dma("unspill3", X[:], io["spill3"], ready=["yC.7"])
        Pairs("t.br2", 8, at(24), ACT.Sigmoid, of=1, yh=(YH, YL), ready="yC", acc=8)
        free_until("scalar", "vector")
        split("mg3", [T(24 + k) for k in range(KT)], XH, XL)
        vs(lambda st: st.wait("unspill3"))
        Linear("t.out", add=True, ready="mg3", squares=24)
        colnorm("end3", [allx], D, "eps6", False, to_residual("end3", "final_g"), lambda i: T(24 + i), None, summed="t.out.sum")
        mark("end3.y", "vector")
        dma("store", io["outT"].rearrange("(k p) t -> p k t", p=P), X[:], ready=["end3.y"])
        Stage(scalar=lambda act, st, e: st.wait("store"))
        def walk(role, eng, sem_):
            st = Steps(eng, sem_, names, sems)
            for s in PLAN:
                if isinstance(s, Stage):
                    s.run(role, eng, st)
                elif role == "tensor":
                    s.tensor(eng, st)
                elif role == "scalar":
                    s.scalar(eng, st)
                elif role == "vector":
                    s.vector(eng, st)
            return st

        block = ctx.enter_context(nc.Block())

        @block.sync
        def _(sp):
            xin = io["xT"].rearrange("(k p) t -> p k t", p=P)
            sp.dma_start(X[:], xin).then_inc(params, 16)
            sp.dma_start(CST[:], io["consts"]).then_inc(params, 16)
            sp.dma_start(VEC[:], io["vecs"]).then_inc(params, 16)
            w = io["units"].rearrange("u p c -> p u c")
            for j in range(RAW):
                sp.dma_start(RW[:, j, :], w[:, j, :]).then_inc(raw_full[j], 16)
            memv = A[:, 28:32, :].rearrange("p a (b c) -> p (a b) c", c=MEM)
            sp.dma_start(memv, io["memT"].rearrange("(k p) t -> p k t", p=P)).then_inc(mem_loaded, 16)
            with sp.Fori(1, NUNITS // RAW) as i:
                for j in range(RAW):
                    sp.wait_ge(split_done, i * RAW + (j - RAW + 1))
                    sp.dma_start(RW[:, j:j + 1, :], w[:, bass.ds(i * RAW + j, 1), :]).then_inc(raw_full[j], 16)
            for u in range(NUNITS // RAW * RAW, NUNITS):
                sp.wait_ge(split_done, u - RAW + 1)
                sp.dma_start(RW[:, u % RAW, :], w[:, u, :]).then_inc(raw_full[u % RAW], 16)

        @block.gpsimd
        def _(pool):
            def unit(u, fill, j, guard):
                pool.wait_ge(raw_full[j], fill)
                if guard:
                    pool.wait_ge(unit_done, u - SPLIT + 1)
                nc.gpsimd.tensor_tensor(WH[:, j % SPLIT, :], RW[:, j, :], cst("one").to_broadcast([P, D]), ALU.mult).then_inc(split_hi, 1)
                pool.wait_ge(split_hi, u + 1)
                nc.gpsimd.tensor_tensor(WL[:, j % SPLIT, :], RW[:, j, :], WH[:, j % SPLIT, :].bitcast(F32),
                                        ALU.subtract).then_inc(split_done, 1)
                
            pool.wait_ge(params, 48)
            for j in range(RAW):
                unit(j, 16, j, j >= SPLIT)
            with pool.Fori(1, NUNITS // RAW) as i:
                for j in range(RAW):
                    unit(i * RAW + j, i * 16 + 16, j, True)
            for u in range(NUNITS // RAW * RAW, NUNITS):
                unit(u, 16 * (u // RAW + 1), u % RAW, True)

        @block.scalar
        def _(act):
            act.wait_ge(params, 48)
            walk("scalar", act, scalar_steps)

        @block.vector
        def _(dve):
            dve.sem_inc(banks_free, 4)
            dve.wait_ge(params, 48)
            walk("vector", dve, vector_steps)

        @block.tensor
        def _(pe):
            pe.wait_ge(params, 48)
            walk("tensor", pe, tensor_steps)


def blocks(w):
    k, n = w.shape
    return w.reshape(k // P, P, n // P, P).transpose(2, 1, 0, 3).reshape(n // P, P, k)


def rows2(w):
    return w.reshape(4, 2, P, -1, S).transpose(3, 0, 2, 1, 4).reshape(-1, P, D)


def alternate(a, b):
    return np.stack([a, b], 1).reshape(-1, P, D)


def weight_units(i):
    H = 512
    out = []
    ab = blocks(i["w_in_ab"][0])
    out += [alternate(ab[16:20], ab[20:24]), ab[0:4], ab[4:8], ab[8:12], ab[12:16]]

    def layer(l, k_early, w_out):
        k, v = blocks(i["xa_wkv"][l][:, :D]), rows2(i["xa_wkv"][l][:, D:])
        f = blocks(i["ffn_w_in"][l])
        return [k[:k_early], v[:4], blocks(w_out), k[k_early:], v[4:], blocks(i["xa_wq"][l]), blocks(i["xa_wo"][l]),
                alternate(f[:NH], f[NH:]), i["ffn_w_out"][l].reshape(NH, P, D)]
    out += layer(0, 4, i["w_out_ab"][0])
    w = i["w_in_cd"][0]
    out += [blocks(w[:, :2 * H]), rows2(w[:, 2 * H:3 * H]), blocks(w[:, 3 * H:])]
    out += layer(1, 0, i["w_out_cd"][0])
    w = i["w_in_2"][0]
    gates = blocks(w[:, 3328:])
    ups, late = [], []
    for n, name in enumerate(("w_up_a_2", "w_up_b_2")):
        u = i[name][0].reshape(4, P, 4, 2, P).transpose(2, 1, 3, 0, 4).reshape(4, P, D)
        for r in range(4):
            ups += [gates[8 * n + 2 * r:8 * n + 2 * r + 2]]
            (late if n else ups).append(u[r:r + 1])
    ups += late
    out += [blocks(w[:, :2 * H]), rows2(w[:, 2 * H:3 * H]), blocks(w[:, 3 * H:3328]), *ups, blocks(i["w_out_2"][0]),
            alternate(blocks(i["ffn_w_gate_2"][0]), blocks(i["ffn_w_up_2"][0])), i["ffn_w_down_2"][0].reshape(NH, P, D)]
    w = i["w_in_3"][0]
    at, cut = 0, {}
    for name, n in (("aq", D), ("ak", D), ("av", D), ("ao", D), ("az", D), ("ai", 4), ("af", 4), ("bq", D), ("bk", D),
                    ("bv", D), ("bz", D), ("bf", 8), ("cu", D), ("cz", D), ("gates", 3 * D)):
        cut[name] = w[:, at:at + n]
        at += n
    gif = np.zeros((D, P), np.float32)
    gif[:, 0:4], gif[:, 32:36], gif[:, 64:72] = cut["ai"], cut["af"], cut["bf"]
    br = [alternate(blocks(i["w_branch_3"][0, n]), blocks(cut["gates"][:, n * D:(n + 1) * D])) for n in range(3)]
    pool = i["pool_w_3"][0].reshape(2, 2, 2, P, 2, P).transpose(0, 3, 1, 4, 2, 5).reshape(2, P, D)
    out += [blocks(gif), blocks(cut["aq"]), blocks(cut["ak"]), rows2(cut["av"]), alternate(blocks(cut["ao"]), blocks(cut["az"])),
            blocks(cut["bq"]), br[0], blocks(cut["bk"]), rows2(cut["bv"]), blocks(cut["bz"]), br[1],
            blocks(cut["cu"]), blocks(cut["cz"]), pool, br[2], blocks(i["w_out_3"][0])]
    return np.concatenate(out)


def vectors(i):
    def col(v):
        return v.reshape(-1, P).T

    def part(v):
        c = np.zeros((P, 1), np.float32)
        c[:v.size, 0] = v.ravel()
        return c
    parts = {
        "norm_mix0": col(i["norm_mix"][0]), "norm_mix1": col(i["norm_mix"][1]), "norm_xattn0": col(i["norm_xattn"][0]),
        "norm_xattn1": col(i["norm_xattn"][1]), "norm_ffn0": col(i["norm_ffn"][0]), "norm_ffn1": col(i["norm_ffn"][1]),
        "mem_norm": col(i["mem_norm"]), "final_norm": col(i["final_norm"]), "lb": col(i["hgrn_lower_bounds"]),
        "hgrn_out_norm": col(i["hgrn_out_norm"]),
        "conv_dw_w": i["conv_dw_w"][0].reshape(31, 4, P).transpose(2, 1, 0).reshape(P, 124), "conv_dw_b": col(i["conv_dw_b"]),
        "conv_ln_g": col(i["conv_ln_g"]), "conv_ln_b": col(i["conv_ln_b"]), "sgu_ln_g": col(i["sgu_ln_g"]), "sgu_ln_b": col(i["sgu_ln_b"]),
        "ln_in_g": col(i["ln_in_g_2"]), "ln_in_b": col(i["ln_in_b_2"]), "subln_g": col(i["diff_subln_g_2"]), "mu": col(i["rwkv_mu_2"]),
        "w0": col(i["rwkv_w0_2"]), "a0": col(i["rwkv_a0_2"]), "k_k": col(i["rwkv_k_k_2"]), "k_a": col(i["rwkv_k_a_2"]),
        "r_k": col(i["rwkv_r_k_2"]), "lnx_g": col(i["rwkv_lnx_g_2"]), "lnx_b": col(i["rwkv_lnx_b_2"]),
        "ln1_g": col(i["ln1_g_2"]), "ln1_b": col(i["ln1_b_2"]), "ln2_g": col(i["ln2_g_2"]), "ln2_b": col(i["ln2_b_2"]),
        "norm_g3": col(i["norm_g_3"]), "conv_w3": i["conv_w_3"][0].reshape(4, 16, P).transpose(2, 1, 0).reshape(P, 64),
        "ml_norm_g": col(i["ml_norm_g_3"]), "pool_scale": col(i["pool_scale_3"]), "final_g": col(i["final_g_3"]),
        "ml_bi": part(i["ml_bi_3"]), "ml_bf": part(i["ml_bf_3"]), "fox_bf": part(i["fox_bf_3"]),
    }
    return np.concatenate([parts[n] for n, _ in VECS], 1)


def laid_out(inputs):
    i = {k: np.asarray(a) for k, a in inputs.items()}
    lora = np.zeros((P, D), np.float32)
    lora[0:64, 0:S], lora[64:P, 0:S], lora[:, S:] = i["rwkv_w2_2"][0], i["rwkv_a2_2"][0], i["rwkv_g2_2"][0]
    lam = np.concatenate([i[f"diff_lam_{n}_2"][0] for n in ("q1", "k1", "q2", "k2")])
    return {
        "units": weight_units(i), "vecs": vectors(i), "consts": constants(), "reset": reset_mask(), "onehot": bucket_table(),
        "xT": i["x"][0].T, "memT": i["mem"][0].T, "rel": i["rel_bias_2"], "lora": lora,
        "lam": np.broadcast_to(lam, (P, 256)), "sguw": i["sgu_w"][0].transpose(2, 0, 1).reshape(P, S),
        "sgub": i["sgu_b"][0].reshape(1, S),
    }


def declare(nc, arrays):
    io = {n: nc.dram_tensor(f"in_{n}", a.shape, mybir.dt.from_np(a.dtype), kind="ExternalInput").ap() for n, a in arrays.items()}
    io["outT"] = nc.dram_tensor("out_T", (D, S), F32, kind="ExternalOutput").ap()
    for n in ("spill", "spill3"):
        io[n] = nc.dram_tensor(n, (P, KT, S), F32, kind="Internal").ap()
    io["spill_gates"] = nc.dram_tensor("spill_gates", (P, 6, S), F32, kind="Internal").ap()
    io["spill_rk"] = nc.dram_tensor("spill_rk", (P, 4, S), F32, kind="Internal").ap()
    return io


def kernel(**inputs):
    import concourse.bacc as _bacc
    from concourse.bass_utils import run_bass_kernel_spmd as _run

    arrays = {n: np.ascontiguousarray(a) for n, a in laid_out(inputs).items()}
    names = {}
    for counting in (True, False):
        nc = _bacc.Bacc("TRN2", target_bir_lowering=False, num_devices=1, dynamic_dma_scratch_size=1024)
        io = declare(nc, arrays)
        names["unknown"] = (nc.alloc_semaphore("unknown"), 1)
        if not counting:
            names.pop("unknown")
        program(nc, io, names)
    r = _run(nc, [{f"in_{n}": a for n, a in arrays.items()}], core_ids=[0])
    return np.ascontiguousarray(r.results[0]["out_T"].T)[None]
```
